# Optimizing a Trainium2 kernel written in Bass

```python
import jax, jax.numpy as jnp
from jax import lax
import numpy as np

D_MODEL = 1024
BATCH = 1
SEQ = 256
DEPTH = 1
DEC_BATCH = 1
DEC_SEQ = 2048
PAST_LEN = 256

GRID_W = 64
CONV_DIM = 512
CONV_WIDTH = 31
N_HEADS = 8
QK_NOPE = 64
QK_ROPE = 32
V_DIM = 64
Q_LORA = 256
KV_LORA = 128
N_EXPERTS = 16
EXPERT_FF = 512
EC_FACTOR = 2
ROPE_BASE = 10000.0
Q_BLOCK = 128
EPS = 1e-6
IN_SIZES = (2 * CONV_DIM, Q_LORA, KV_LORA, QK_ROPE, 2 * D_MODEL)
IN_COLS = sum(IN_SIZES)
IN_SPLITS = tuple(int(s) for s in np.cumsum(IN_SIZES)[:-1])

kernel_name = 'hybrid_conformer_mla_ec_moe_diffusion_step'

def rmsnorm(x, g):
    xf = x.astype(jnp.float32)
    y = xf * lax.rsqrt(jnp.mean(xf * xf, axis=-1, keepdims=True) + EPS)
    return (y * g.astype(jnp.float32)).astype(x.dtype)

def layernorm(x, g, b):
    xf = x.astype(jnp.float32)
    mu = jnp.mean(xf, axis=-1, keepdims=True)
    var = jnp.mean(jnp.square(xf - mu), axis=-1, keepdims=True)
    y = (xf - mu) * lax.rsqrt(var + EPS)
    return (y * g.astype(jnp.float32) + b.astype(jnp.float32)).astype(x.dtype)

def grid_angles(n):
    rows = n // GRID_W
    r = jnp.repeat(jnp.arange(rows), GRID_W).astype(jnp.float32)
    col = jnp.tile(jnp.arange(GRID_W), rows).astype(jnp.float32)
    half = QK_ROPE // 2
    freqs = ROPE_BASE ** (-jnp.arange(0, half, 2, dtype=jnp.float32) / half)
    return r[:, None] * freqs, col[:, None] * freqs

def rotate(x, ang):
    x1, x2 = jnp.split(x.astype(jnp.float32), 2, axis=-1)
    cos, sin = jnp.cos(ang), jnp.sin(ang)
    return jnp.concatenate([x1 * cos - x2 * sin, x1 * sin + x2 * cos], axis=-1)

def rope_2d(x, ang_r, ang_c):
    half = QK_ROPE // 2
    out = jnp.concatenate([rotate(x[..., :half], ang_r), rotate(x[..., half:], ang_c)], axis=-1)
    return out.astype(x.dtype)

def conformer_conv(u, dw, dw_b, ln_g, ln_b, w_out):
    a, b = jnp.split(u, 2, axis=-1)
    v = a * jax.nn.sigmoid(b)
    pad = CONV_WIDTH // 2
    v = lax.conv_general_dilated(v, dw[:, None, :].astype(v.dtype), (1,), [(pad, pad)],
                                 dimension_numbers=('NWC', 'WIO', 'NWC'),
                                 feature_group_count=CONV_DIM) + dw_b
    v = jax.nn.silu(layernorm(v, ln_g, ln_b))
    return v @ w_out

def mla_attention(q, ckv, kpe, w_kvb, w_o):
    B, T = q.shape[0], q.shape[1]
    S = ckv.shape[1]
    kv = (ckv @ w_kvb).reshape(B, S, N_HEADS, QK_NOPE + V_DIM)
    k_nope, v = kv[..., :QK_NOPE], kv[..., QK_NOPE:]
    scale = (QK_NOPE + QK_ROPE) ** -0.5
    nb = T // Q_BLOCK
    qb = q.reshape(B, nb, Q_BLOCK, N_HEADS, QK_NOPE + QK_ROPE).transpose(1, 0, 2, 3, 4)

    def block(q_blk):
        s = (jnp.einsum('bqhd,bkhd->bhqk', q_blk[..., :QK_NOPE], k_nope)
             + jnp.einsum('bqhr,bkr->bhqk', q_blk[..., QK_NOPE:], kpe))
        p = jax.nn.softmax(s.astype(jnp.float32) * scale, axis=-1).astype(v.dtype)
        return jnp.einsum('bhqk,bkhd->bqhd', p, v)

    o = lax.map(block, qb)
    o = o.transpose(1, 0, 2, 3, 4).reshape(B, T, N_HEADS * V_DIM)
    return o @ w_o

def ec_moe(h, w_router, w_g, w_u, w_d):
    B, n, D = h.shape
    cap = EC_FACTOR * n // N_EXPERTS
    aff = jax.nn.softmax((h @ w_router).astype(jnp.float32), axis=-1)
    vals, idx = lax.top_k(aff.transpose(0, 2, 1), cap)
    xg = jax.vmap(lambda hb, ib: hb[ib])(h, idx)
    a = jnp.einsum('becd,edf->becf', xg, w_g)
    u = jnp.einsum('becd,edf->becf', xg, w_u)
    y = jnp.einsum('becf,efd->becd', jax.nn.silu(a) * u, w_d) * vals[..., None].astype(h.dtype)
    return jax.vmap(lambda ib, yb: jnp.zeros((n, D), yb.dtype).at[ib.reshape(-1)].add(yb.reshape(-1, D)))(idx, y)

def trunk_layer(x, mod_vec, p, ctx_ckv=None, ctx_kpe=None):
    B, n, _ = x.shape
    m = jnp.einsum('bd,de->be', jax.nn.silu(mod_vec), p['w_ada']) + p['b_ada']
    sh1, sc1, g1, sh2, sc2, g2 = jnp.split(m[:, None, :], 6, axis=-1)
    h = rmsnorm(x, p['norm1']) * (1 + sc1) + sh1
    proj = h @ p['w_in']
    conv_in, q_a, kv_a, k_rope, gate_lin = jnp.split(proj, IN_SPLITS, axis=-1)
    conv_out = conformer_conv(conv_in, p['conv_dw'], p['conv_dw_b'], p['conv_ln_g'], p['conv_ln_b'], p['w_conv_out'])
    q = (rmsnorm(q_a, p['q_norm']) @ p['w_qb']).reshape(B, n, N_HEADS, QK_NOPE + QK_ROPE)
    ckv = rmsnorm(kv_a, p['kv_norm'])
    if ctx_ckv is None:
        keys_ckv, keys_kpe = ckv, k_rope
    else:
        ang_r, ang_c = grid_angles(n)
        q = jnp.concatenate([q[..., :QK_NOPE], rope_2d(q[..., QK_NOPE:], ang_r[:, None], ang_c[:, None])], axis=-1)
        keys_ckv = jnp.concatenate([ctx_ckv, ckv], axis=1)
        keys_kpe = jnp.concatenate([ctx_kpe, rope_2d(k_rope, ang_r, ang_c)], axis=1)
    attn_out = mla_attention(q, keys_ckv, keys_kpe, p['w_kvb'], p['w_o_mla'])
    g_conv, g_attn = jnp.split(jax.nn.sigmoid(gate_lin), 2, axis=-1)
    x = x + g1 * ((g_conv * conv_out + g_attn * attn_out) @ p['w_out'])
    h2 = rmsnorm(x, p['norm2']) * (1 + sc2) + sh2
    x = x + g2 * ec_moe(h2, p['w_router'], p['w_e_gate'], p['w_e_up'], p['w_e_down'])
    return x, ckv, k_rope

def setup_inputs(seed: int = 0) -> dict:
    key = jax.random.key(seed)
    ks = jax.random.split(key, 32)
    f32 = jnp.float32

    def dense(k, shape, fan_in, scale=1.0):
        return jax.random.normal(k, shape, f32) * (fan_in ** -0.5) * scale

    def gain(k, shape):
        return 1.0 + 0.02 * jax.random.normal(k, shape, f32)

    def bias(k, shape):
        return 0.01 * jax.random.normal(k, shape, f32)

    return {
        'x_prompt': jax.random.normal(ks[0], (BATCH, SEQ, D_MODEL), f32),
        'x_sample': jax.random.normal(ks[1], (DEC_BATCH, DEC_SEQ, D_MODEL), f32),
        'cache_ckv': jax.random.normal(ks[2], (DEC_BATCH, DEPTH, PAST_LEN, KV_LORA), f32),
        'cache_kpe': jax.random.normal(ks[3], (DEC_BATCH, DEPTH, PAST_LEN, QK_ROPE), f32),
        'c': jax.random.normal(ks[4], (DEC_BATCH, D_MODEL), f32),
        'c_ctx': jax.random.normal(ks[5], (D_MODEL,), f32),
        'w_ada': dense(ks[6], (DEPTH, D_MODEL, 6 * D_MODEL), D_MODEL, 0.5),
        'b_ada': bias(ks[7], (DEPTH, 6 * D_MODEL)),
        'norm1': gain(ks[8], (DEPTH, D_MODEL)),
        'w_in': dense(ks[9], (DEPTH, D_MODEL, IN_COLS), D_MODEL),
        'conv_dw': dense(ks[10], (DEPTH, CONV_WIDTH, CONV_DIM), CONV_WIDTH),
        'conv_dw_b': bias(ks[11], (DEPTH, CONV_DIM)),
        'conv_ln_g': gain(ks[12], (DEPTH, CONV_DIM)),
        'conv_ln_b': bias(ks[13], (DEPTH, CONV_DIM)),
        'w_conv_out': dense(ks[14], (DEPTH, CONV_DIM, D_MODEL), CONV_DIM),
        'q_norm': gain(ks[15], (DEPTH, Q_LORA)),
        'w_qb': dense(ks[16], (DEPTH, Q_LORA, N_HEADS * (QK_NOPE + QK_ROPE)), Q_LORA),
        'kv_norm': gain(ks[17], (DEPTH, KV_LORA)),
        'w_kvb': dense(ks[18], (DEPTH, KV_LORA, N_HEADS * (QK_NOPE + V_DIM)), KV_LORA),
        'w_o_mla': dense(ks[19], (DEPTH, N_HEADS * V_DIM, D_MODEL), N_HEADS * V_DIM),
        'w_out': dense(ks[20], (DEPTH, D_MODEL, D_MODEL), D_MODEL),
        'norm2': gain(ks[21], (DEPTH, D_MODEL)),
        'w_router': dense(ks[22], (DEPTH, D_MODEL, N_EXPERTS), D_MODEL),
        'w_e_gate': dense(ks[23], (DEPTH, N_EXPERTS, D_MODEL, EXPERT_FF), D_MODEL),
        'w_e_up': dense(ks[24], (DEPTH, N_EXPERTS, D_MODEL, EXPERT_FF), D_MODEL),
        'w_e_down': dense(ks[25], (DEPTH, N_EXPERTS, EXPERT_FF, D_MODEL), EXPERT_FF),
        'final_norm': gain(ks[26], (D_MODEL,)),
    }

def reference(x_prompt, x_sample, cache_ckv, cache_kpe, c, c_ctx, w_ada, b_ada, norm1, w_in,
              conv_dw, conv_dw_b, conv_ln_g, conv_ln_b, w_conv_out, q_norm, w_qb, kv_norm, w_kvb,
              w_o_mla, w_out, norm2, w_router, w_e_gate, w_e_up, w_e_down, final_norm):
    xp, xs = x_prompt, x_sample
    new_ckv, new_kpe = [], []
    for l in range(DEPTH):
        p = {
            'w_ada': w_ada[l], 'b_ada': b_ada[l], 'norm1': norm1[l], 'w_in': w_in[l],
            'conv_dw': conv_dw[l], 'conv_dw_b': conv_dw_b[l], 'conv_ln_g': conv_ln_g[l],
            'conv_ln_b': conv_ln_b[l], 'w_conv_out': w_conv_out[l], 'q_norm': q_norm[l],
            'w_qb': w_qb[l], 'kv_norm': kv_norm[l], 'w_kvb': w_kvb[l], 'w_o_mla': w_o_mla[l],
            'w_out': w_out[l], 'norm2': norm2[l], 'w_router': w_router[l],
            'w_e_gate': w_e_gate[l], 'w_e_up': w_e_up[l], 'w_e_down': w_e_down[l],
        }
        xp, ckv_l, kpe_l = trunk_layer(xp, c_ctx[None, :], p)
        new_ckv.append(ckv_l)
        new_kpe.append(kpe_l)
        xs, _, _ = trunk_layer(xs, c, p, cache_ckv[:, l], cache_kpe[:, l])
    y_prompt = rmsnorm(xp, final_norm)
    y_sample = rmsnorm(xs, final_norm)
    new_cache_ckv = jnp.stack(new_ckv, axis=1)
    new_cache_kpe = jnp.stack(new_kpe, axis=1)
    return (y_prompt, y_sample, new_cache_ckv, new_cache_kpe)


_drawn_inputs = setup_inputs


def setup_inputs(seed=0):
    import zlib

    import numpy as np

    out = dict(_drawn_inputs(seed))
    spreads = {}
    factors = {'cache_ckv': 8.0,
     'cache_kpe': 8.0,
     'b_ada': 4.413,
     'norm1': 3.086,
     'conv_dw_b': 8.0,
     'conv_ln_g': 8.0,
     'conv_ln_b': 8.0,
     'q_norm': 8.0,
     'w_qb': 3.032,
     'kv_norm': 2.898,
     'norm2': 8.0,
     'final_norm': 2.796}
    for name, (base, spread) in spreads.items():
        noise = np.random.default_rng([zlib.crc32(name.encode()), seed]).standard_normal(out[name].shape)
        drawn = base * np.exp(spread * noise) if base else spread * noise
        out[name] = __import__('jax').numpy.asarray(drawn.astype(out[name].dtype))
    for name, factor in factors.items():
        out[name] = (out[name] * factor).astype(out[name].dtype)
    return out
```

```python
from contextlib import ExitStack

import numpy as np

import concourse.bass as bass
from concourse import mybir

F32 = mybir.dt.float32
F32R = mybir.dt.float32r
U32 = mybir.dt.uint32
ACT = mybir.ActivationFunctionType
ALU = mybir.AluOpType
AX = mybir.AxisListType

P = 128
D = 1024
KD = D // P
S = 2048
PR = 256
T = S + PR
PAST = 256
KEYS = PAST + T
BLK = 512
NB = S // BLK
BLOCKS = [(b * BLK, BLK) for b in range(NB)] + [(S, PR)]
CONV = 512
CT = CONV // P
TAPS = 31
PAD = TAPS // 2
H = 8
NOPE, ROPE, DV = 64, 32, 64
HQ = NOPE + ROPE
QL, KVL = 256, 128
E = 16
FF = 512
CAP = 2 * S // E
CAPP = 2 * PR // E
EPS = 1e-6
ADA = 6 * D
SM_SCALE = float(HQ) ** -0.5


def wait(eng, sem, value):
    if not isinstance(value, int) or value > 0:
        eng.wait_ge(sem, value)


def steps(eng, count, body):
    body(0)
    if count > 1:
        with eng.Fori(1, count) as i:
            body(i)


class Scope:

    def __init__(self, nc, ctx, tag):
        self.nc, self.ctx, self.tag, self.numbers = nc, ctx, tag, []
        ctx.callback(self.zero_sems)

    def sb(self, name, shape, dt=F32):
        return self.ctx.enter_context(self.nc.sbuf_tensor(f"{self.tag}_{name}", shape, dt))

    def ps(self, name, shape):
        return self.ctx.enter_context(self.nc.psum_tensor(f"{self.tag}_{name}", shape, F32))

    def sem(self, name):
        sem = self.ctx.enter_context(self.nc.semaphore(f"{self.tag}_{name}"))
        self.numbers.append(sem.num)
        return sem

    def sems(self, name, n):
        return [self.sem(f"{name}{k}") for k in range(n)]

    def zero_sems(self):
        runs = []
        for n in sorted(self.numbers):
            if runs and runs[-1][-1] == n - 1:
                runs[-1].append(n)
            else:
                runs.append([n])
        with self.nc.Block() as block:
            @block.gpsimd
            def _(pool):
                for run in runs:
                    pool.sem_clear(range(run[0], run[-1] + 1))


def ada_phase(nc, t):
    CH = 512
    NCH = ADA // CH
    U = 3
    with ExitStack() as ctx:
        p = Scope(nc, ctx, "ada")
        cond = p.sb("cond", [P, KD, 2])
        sig = p.sb("sig", [P, KD, 2])
        silu = p.sb("silu", [P, KD, 2])
        w = p.sb("w", [P, U, KD, CH])
        bias = p.sb("bias", [2, ADA])
        mod = p.sb("mod", [2, ADA])
        acc = p.ps("acc", [P, U, CH])
        cond_ld, bias_ld, mod_st = p.sem("cond_ld"), p.sem("bias_ld"), p.sem("mod_st")
        w_ld = p.sems("w_ld", U)
        sig_done, silu_done = p.sem("sig_done"), p.sem("silu_done")
        chunk_done, mod_done = p.sem("chunk_done"), p.sem("mod_done")
        with nc.Block() as block:
            @block.sync
            def _(sp):
                sp.dma_start(cond[:], t["cond"]).then_inc(cond_ld, 16)
                sp.dma_start(bias[:], t["b_ada"].partition_broadcast(2)).then_inc(bias_ld, 16)

                def load(i):
                    for u in range(U):
                        wait(sp, chunk_done, U * i + u - U + 1)
                        sp.dma_start(w[:, u], t["w_ada"][bass.ds(U * i + u, 1)].rearrange("o p k n -> (o p) k n")
                                     ).then_inc(w_ld[u], 16)
                steps(sp, NCH // U, load)
                sp.wait_ge(mod_done, NCH)
                sp.dma_start(t["mod"], mod[:]).then_inc(mod_st, 16)
                sp.wait_ge(mod_st, 16)

            @block.scalar
            def _(act):
                act.wait_ge(cond_ld, 16)
                act.activation(sig[:], cond[:], ACT.Sigmoid).then_inc(sig_done, 1)

            @block.tensor
            def _(pe):
                pe.wait_ge(silu_done, 1)

                def chunk(i):
                    for u in range(U):
                        pe.wait_ge(w_ld[u], 16 * i + 16)
                        wait(pe, mod_done, U * i + u - U + 1)
                        for k in range(KD):
                            mm = pe.matmul(acc[0:2, u, :], silu[:, k, :], w[:, u, k, :],
                                           start=(k == 0), stop=(k == KD - 1))
                        mm.then_inc(chunk_done, 1)
                steps(pe, NCH // U, chunk)

            @block.vector
            def _(dve):
                dve.wait_ge(sig_done, 1)
                dve.tensor_tensor(silu[:], cond[:], sig[:], ALU.mult).then_inc(silu_done, 1)
                dve.wait_ge(bias_ld, 16)

                def add(i):
                    for u in range(U):
                        dve.wait_ge(chunk_done, U * i + u + 1)
                        col = bass.ds((U * i + u) * CH, CH)
                        dve.tensor_tensor(mod[:, col], acc[0:2, u, :], bias[:, col], ALU.add
                                          ).then_inc(mod_done, 1)
                steps(dve, NCH // U, add)


def norm1_phase(nc, t, hT_hi, hT_lo, ident):
    with ExitStack() as ctx:
        p = Scope(nc, ctx, "n1")
        gain = p.sb("gain", [P, 2, D])
        shift = p.sb("shift", [P, 2, D])
        norm = p.sb("norm", [P, D])
        x = p.sb("x", [P, 2, D])
        h = p.sb("h", [P, 2, D])
        sumsq, meansq, root, rstd = (p.sb(n, [P, 2]) for n in ("sumsq", "meansq", "root", "rstd"))
        tp = p.ps("tp", [P, 2, D])
        rows_ld, ident_ld = p.sem("rows_ld"), p.sem("ident_ld")
        x_ld = p.sems("x_ld", 2)
        gain_done, sq_done, ms_done, root_done = (p.sem(n) for n in ("gain_done", "sq_done", "ms_done", "root_done"))
        rstd_done, scaled_done, h_done, tp_done = (p.sem(n) for n in ("rstd_done", "scaled_done", "h_done", "tp_done"))
        hi_done, lo_done = p.sem("hi_done"), p.sem("lo_done")
        PAIRS = T // P // 2

        def skewed(eng, front, back):
            front(0, 0)
            if back is None:
                with eng.Fori(1, PAIRS - 1) as i:
                    front(i, 0)
                front(PAIRS - 1, 1)
                return
            front(1, 0)
            back(0)
            with eng.Fori(2, PAIRS - 1) as i:
                front(i, 0)
                back(i - 1)
            front(PAIRS - 1, 1)
            back(PAIRS - 2)
            back(PAIRS - 1)

        with nc.Block() as block:
            @block.sync
            def _(sp):
                sp.dma_start(ident[:], t["ident"]).then_inc(ident_ld, 16)
                for s in range(2):
                    sp.dma_start(gain[:, s], t["mod"][s, D:2 * D].partition_broadcast(P)).then_inc(rows_ld, 16)
                    sp.dma_start(shift[:, s], t["mod"][s, 0:D].partition_broadcast(P)).then_inc(rows_ld, 16)
                sp.dma_start(norm[:], t["norm1"].partition_broadcast(P)).then_inc(rows_ld, 16)

                def load(i, s):
                    for u in range(2):
                        wait(sp, scaled_done, 2 * i + u - 1)
                        sp.dma_start(x[:, u], t["x"][bass.ds((2 * i + u) * P, P), :]).then_inc(x_ld[u], 16)
                skewed(sp, load, None)

            @block.scalar
            def _(act):
                def front(i, s):
                    for u in range(2):
                        act.wait_ge(x_ld[u], 16 * i + 16)
                        wait(act, tp_done, 2 * i + u - 1)
                        act.activation(h[:, u], x[:, u], ACT.Square, accum_out=sumsq[:, u:u + 1]
                                       ).then_inc(sq_done, 1)
                    for u in range(2):
                        act.wait_ge(ms_done, 2 * i + u + 1)
                        act.activation(root[:, u:u + 1], meansq[:, u:u + 1], ACT.Sqrt).then_inc(root_done, 1)

                def back(i):
                    for u in range(2):
                        act.wait_ge(tp_done, 2 * i + u + 1)
                        act.activation(hT_hi[:, :, bass.ds((2 * i + u) * P, P)],
                                       tp[:, u].rearrange("p (k n) -> p k n", k=KD), ACT.Copy).then_inc(hi_done, 1)
                skewed(act, front, back)

            @block.vector
            def _(dve):
                dve.wait_ge(rows_ld, 16 * 5)
                for s in range(2):
                    dve.scalar_tensor_tensor(out=gain[:, s], in0=gain[:, s], scalar=1.0, in1=norm[:],
                                             op0=ALU.add, op1=ALU.mult).then_inc(gain_done, 1)

                def front(i, s):
                    for u in range(2):
                        dve.wait_ge(sq_done, 2 * i + u + 1)
                        dve.tensor_scalar(meansq[:, u:u + 1], sumsq[:, u:u + 1], 1.0 / D, EPS, ALU.mult, ALU.add
                                          ).then_inc(ms_done, 1)
                    dve.wait_ge(gain_done, 2)
                    for u in range(2):
                        dve.wait_ge(root_done, 2 * i + u + 1)
                        dve.reciprocal(rstd[:, u:u + 1], root[:, u:u + 1]).then_inc(rstd_done, 1)
                        dve.wait_ge(rstd_done, 2 * i + u + 1)
                        dve.scalar_tensor_tensor(out=h[:, u], in0=x[:, u], scalar=rstd[:, u:u + 1],
                                                 in1=gain[:, s], op0=ALU.mult, op1=ALU.mult
                                                 ).then_inc(scaled_done, 1)

                def back(i):
                    for u in range(2):
                        dve.wait_ge(hi_done, 2 * i + u + 1)
                        cols = bass.ds((2 * i + u) * P, P)
                        dve.tensor_tensor(hT_lo[:, :, cols], tp[:, u].rearrange("p (k n) -> p k n", k=KD),
                                          hT_hi[:, :, cols].bitcast(F32), ALU.subtract).then_inc(lo_done, 1)
                skewed(dve, front, back)

            @block.gpsimd
            def _(pool):
                pool.wait_ge(rows_ld, 16 * 5)

                def front(i, s):
                    for u in range(2):
                        pool.wait_ge(scaled_done, 2 * i + u + 1)
                        pool.tensor_tensor(h[:, u], h[:, u], shift[:, s], ALU.add).then_inc(h_done, 1)
                skewed(pool, front, None)

            @block.tensor
            def _(pe):
                pe.wait_ge(ident_ld, 16)

                def front(i, s):
                    for u in range(2):
                        pe.wait_ge(h_done, 2 * i + u + 1)
                        wait(pe, lo_done, 2 * i + u - 1)
                        for k in range(KD):
                            mm = pe.transpose(tp[:, u, k * P:(k + 1) * P], h[:, u, k * P:(k + 1) * P], ident[:])
                        mm.then_inc(tp_done, 1)
                skewed(pe, front, None)


def in_proj_phase(nc, t, hT_hi, hT_lo):
    J = 7
    OTHER = J - 2
    VS = S + 2 * PAD
    with ExitStack() as ctx:
        p = Scope(nc, ctx, "ip")
        raw = p.sb("raw", [P, 2, KD, P])
        w_hi, w_lo = p.sb("w_hi", [P, 2, KD, P], F32R), p.sb("w_lo", [P, 2, KD, P], F32R)
        sig = p.sb("sig", [P, 2, BLK])
        stage = p.sb("stage", [P, len(BLOCKS), BLK])
        v = p.sb("v", [P, VS + PR + 2 * PAD])
        conv = p.sb("conv", [P, T])
        dw = p.sb("dw", [P, CT, TAPS + 1])
        pa = p.ps("pa", [P, 2, BLK])
        pb = p.ps("pb", [P, BLK])
        po = p.ps("po", [P, len(BLOCKS), BLK])
        raw_ld = p.sems("raw_ld", 2)
        dw_ld, conv_st = p.sem("dw_ld"), p.sem("conv_st")
        stage_st = p.sems("stage_st", len(BLOCKS))
        hi_done, lo_done = p.sem("hi_done"), p.sem("lo_done")
        a_done, b_done, o_done = p.sem("a_done"), p.sem("b_done"), p.sem("o_done")
        sig_done, v_done, out_done = p.sem("sig_done"), p.sem("v_done"), p.sem("out_done")
        pad_done, taps_s, taps_p = p.sem("pad_done"), p.sem("taps_s"), p.sem("taps_p")
        NBL = len(BLOCKS)

        def slot(j):
            return j % 2

        def slot_free(c, j):
            return J * c + j - {0: 0, 1: 2}.get(j, 1)

        def products_over(c, j):
            if j < 2:
                return o_done, NBL * (OTHER * c - j)
            if j < 4:
                return (a_done, b_done)[j - 2], NBL * (c + 1)
            return o_done, NBL * (OTHER * c + j - 3)

        def passes(pe, out, s, tok, n):
            ops = [(w_hi, hT_hi), (w_lo, hT_hi), (w_hi, hT_lo)]
            for k in range(KD):
                for q, (w, h) in enumerate(ops):
                    mm = pe.matmul(out, w[:, s, k, :], h[:, k, tok:tok + n],
                                   start=(k == 0 and q == 0), stop=(k == KD - 1 and q == 2))
            return mm

        with nc.Block() as block:
            @block.sync
            def _(sp):
                sp.dma_start(dw[:], t["conv_dw"]).then_inc(dw_ld, 16)

                def load(c):
                    for j in range(J):
                        n = J * c + j
                        wait(sp, lo_done, slot_free(c, j))
                        sp.dma_start(raw[:, slot(j)], t["w_in"][bass.ds(n, 1)].rearrange("o p k m -> (o p) k m")
                                     ).then_inc(raw_ld[slot(j)], 16)
                steps(sp, CT, load)

            def raw_count(c, j):
                return (4 * c + j // 2 + 1) if slot(j) == 0 else (3 * c + j // 2 + 1)

            @block.scalar
            def _(act):
                def split(c, j):
                    act.wait_ge(raw_ld[slot(j)], 16 * raw_count(c, j))
                    used, count = products_over(c, j)
                    wait(act, used, count)
                    act.activation(w_hi[:, slot(j)], raw[:, slot(j)], ACT.Copy).then_inc(hi_done, 1)

                def store(c, j, b):
                    tok, n = BLOCKS[b]
                    act.wait_ge(out_done, NBL * (OTHER * c + j - 2) + b + 1)
                    if j < J - 1:
                        dst = t["gates"][bass.ds((4 * c + j - 2) * P, P), tok:tok + n]
                    else:
                        dst = t["misc"][bass.ds(c * P, P), tok:tok + n]
                    act.dma_start(dst, stage[:, b, 0:n]).then_inc(stage_st[b], 16)

                def body(c):
                    split(c, 0)
                    split(c, 1)
                    for b, (tok, n) in enumerate(BLOCKS):
                        q = NBL * c + b
                        act.wait_ge(b_done, q + 1)
                        wait(act, v_done, q if b == 0 else q - 1)
                        act.activation(sig[:, b % 2, 0:n], pb[:, 0:n], ACT.Sigmoid).then_inc(sig_done, 1)
                    split(c, 2)
                    split(c, 3)
                    for j in range(2, J):
                        func = ACT.Sigmoid if j < J - 1 else ACT.Copy
                        for b, (tok, n) in enumerate(BLOCKS):
                            tile = OTHER * c + j - 2
                            act.wait_ge(o_done, NBL * tile + b + 1)
                            wait(act, stage_st[b], 16 * tile)
                            act.activation(stage[:, b, 0:n], po[:, b, 0:n], func).then_inc(out_done, 1)
                            if b:
                                store(c, j, b - 1)
                        store(c, j, NBL - 1)
                        if j + 2 < J:
                            split(c, j + 2)
                    act.wait_ge(taps_s, TAPS * c + TAPS)
                    act.wait_ge(taps_p, TAPS * c + TAPS)
                    act.dma_start(t["conv"][bass.ds(c * P, P), :], conv[:]).then_inc(conv_st, 16)

                steps(act, CT, body)
                for b in range(NBL):
                    act.wait_ge(stage_st[b], 16 * OTHER * CT)
                act.wait_ge(conv_st, 16 * CT)

            @block.gpsimd
            def _(pool):
                def split(c):
                    for j in range(J):
                        pool.wait_ge(hi_done, J * c + j + 1)
                        pool.tensor_tensor(w_lo[:, slot(j)], raw[:, slot(j)], w_hi[:, slot(j)].bitcast(F32),
                                           ALU.subtract).then_inc(lo_done, 1)
                steps(pool, CT, split)

            @block.tensor
            def _(pe):
                def body(c):
                    pe.wait_ge(lo_done, J * c + 2)
                    for b, (tok, n) in enumerate(BLOCKS):
                        q = NBL * c + b
                        wait(pe, v_done, q if b == 0 else q - 1)
                        mm = passes(pe, pa[:, b % 2, 0:n], 0, tok, n)
                        mm.then_inc(a_done, 1)
                        wait(pe, sig_done, q)
                        mm = passes(pe, pb[:, 0:n], 1, tok, n)
                        mm.then_inc(b_done, 1)
                    for j in range(2, J):
                        pe.wait_ge(lo_done, J * c + j + 1)
                        for b, (tok, n) in enumerate(BLOCKS):
                            tile = OTHER * c + j - 2
                            wait(pe, out_done, NBL * (tile - 1) + b + 1)
                            mm = passes(pe, po[:, b, 0:n], slot(j), tok, n)
                            mm.then_inc(o_done, 1)
                steps(pe, CT, body)

            @block.vector
            def _(dve):
                dve.memset(v[:], 0.0).then_inc(pad_done, 1)
                dve.wait_ge(pad_done, 1)
                dve.wait_ge(dw_ld, 16)
                segs = [(0, 0, S, taps_s), (VS, S, PR, taps_p)]

                def body(c):
                    for _, _, _, taps in segs:
                        wait(dve, taps, TAPS * c)
                    for b, (tok, n) in enumerate(BLOCKS):
                        q = NBL * c + b
                        at = PAD + tok if b < NB else VS + PAD
                        dve.wait_ge(a_done, q + 1)
                        dve.wait_ge(sig_done, q + 1)
                        dve.tensor_tensor(v[:, at:at + n], pa[:, b % 2, 0:n], sig[:, b % 2, 0:n], ALU.mult
                                          ).then_inc(v_done, 1)
                    dve.wait_ge(v_done, NBL * c + NBL)
                    wait(dve, conv_st, 16 * c)
                    def tap(w):
                        return dw[:, bass.ds(c, 1), w:w + 1].rearrange("p o w -> p (o w)")
                    for w in range(TAPS):
                        for at, tok, n, taps in segs:
                            out = conv[:, tok:tok + n]
                            if w == 0:
                                dve.tensor_scalar(out, v[:, at:at + n], tap(0), tap(TAPS), ALU.mult, ALU.add
                                                  ).then_inc(taps, 1)
                            else:
                                dve.wait_ge(taps, TAPS * c + w)
                                dve.scalar_tensor_tensor(out=out, in0=v[:, at + w:at + w + n], scalar=tap(w),
                                                         in1=out, op0=ALU.mult, op1=ALU.add).then_inc(taps, 1)
                steps(dve, CT, body)


def latents_phase(nc, t, V):
    KB = 5
    WH = 2 * HQ + P
    RO = slice(NOPE, HQ)
    NBL = len(BLOCKS)
    with ExitStack() as ctx:
        p = Scope(nc, ctx, "lt")
        qa = p.sb("qa", [P, 2, T])
        ckv = p.sb("ckv", [P, KEYS])
        kpe = p.sb("kpe", [HQ, KEYS])
        qn_hi, qn_lo = p.sb("qn_hi", [P, 2, T], F32R), p.sb("qn_lo", [P, 2, T], F32R)
        ckv_hi, ckv_lo = p.sb("ckv_hi", [P, KEYS], F32R), p.sb("ckv_lo", [P, KEYS], F32R)
        cos, sin = p.sb("cos", [HQ, S]), p.sb("sin", [HQ, S])
        wraw = p.sb("wraw", [P, H, WH])
        w_hi, w_lo = p.sb("w_hi", [P, 2, WH], F32R), p.sb("w_lo", [P, 2, WH], F32R)
        wv = p.sb("wv", [P, H * DV])
        wv_hi, wv_lo = p.sb("wv_hi", [P, H * DV], F32R), p.sb("wv_lo", [P, H * DV], F32R)
        stage_q = p.sb("stage_q", [P, NBL, BLK])
        stage_k = p.sb("stage_k", [P, KB, BLK])
        sq, root, rstd = stage_q[:, 0:3], stage_k[:, 0:2], stage_k[:, 2:4]
        turned = p.sb("turned", [HQ, 2, BLK])
        ones = p.sb("ones", [P, P])
        perm = p.sb("perm", [HQ, HQ])
        gain = p.sb("gain", [P, 3])
        eps = p.sb("eps", [P, 1])
        sums = p.ps("sums", [P, 2, BLK])
        pq = p.ps("pq", [P, 2, BLK])
        rot = p.ps("rot", [P, 2, BLK])
        pk = p.ps("pk", [P, 2, BLK])
        in_ld, w_ld, kpe_st = p.sem("in_ld"), p.sem("w_ld"), p.sem("kpe_st")
        const_done, sq_done, sums_done, root_done = (p.sem(n) for n in ("const_done", "sq_done", "sums_done", "root_done"))
        rstd_done, norm_done, hi_done, lo_done = (p.sem(n) for n in ("rstd_done", "norm_done", "hi_done", "lo_done"))
        v_mm, v_done, kr_mm, kr_rope = (p.sem(n) for n in ("v_mm", "v_done", "kr_mm", "kr_rope"))
        whi_done, wlo_done, q_mm, k_mm = (p.sem(n) for n in ("whi_done", "wlo_done", "q_mm", "k_mm"))
        q_done, k_done, rot_mm, rope_done = (p.sem(n) for n in ("q_done", "k_done", "rot_mm", "rope_done"))
        part_done = p.sem("part_done")
        q_st, k_st = p.sems("q_st", NBL), p.sems("k_st", KB)
        IN = 9

        with nc.Block() as block:
            @block.sync
            def _(sp):
                sp.dma_start(qa[:], t["misc"][0:2 * P, :].rearrange("(k p) n -> p k n", p=P)).then_inc(in_ld, 16)
                sp.dma_start(ckv[:, PAST:], t["misc"][2 * P:3 * P, :]).then_inc(in_ld, 16)
                sp.dma_start(gain[:], t["latent_norms"]).then_inc(in_ld, 16)
                sp.dma_start(ckv[:, 0:PAST], t["cache_ckv"]).then_inc(in_ld, 16)
                sp.dma_start(kpe[RO, 0:PAST], t["cache_kpe"]).then_inc(in_ld, 16)
                sp.dma_start(kpe[RO, PAST:], t["misc"][3 * P:3 * P + ROPE, :]).then_inc(in_ld, 16)
                sp.dma_start(cos[RO, :], t["cos"]).then_inc(in_ld, 16)
                sp.dma_start(sin[RO, :], t["sin"]).then_inc(in_ld, 16)
                sp.dma_start(perm[RO, :], t["perm"]).then_inc(in_ld, 16)
                sp.dma_start(wv[:], t["w_v"]).then_inc(w_ld, 16)
                sp.dma_start(wraw[:], t["w_head"]).then_inc(w_ld, 16)
                sp.dma_start(t["new_kpe"], t["misc"][3 * P:3 * P + ROPE, S:]).then_inc(kpe_st, 16)
                sp.wait_ge(norm_done, 3 * NBL)
                sp.dma_start(t["new_ckv"], ckv[:, PAST + S:]).then_inc(kpe_st, 16)
                sp.wait_ge(kr_rope, NB)
                sp.dma_start(t["kpe"], kpe[RO, :]).then_inc(kpe_st, 16)

                def store(h):
                    for b, (tok, n) in enumerate(BLOCKS):
                        sp.wait_ge(k_done, KB * h + b + 1)
                        sp.dma_start(t["k"][bass.ds(h, 1), :, b * BLK:(b + 1) * BLK].rearrange("o p n -> (o p) n"),
                                     stage_k[0:NOPE, b]).then_inc(k_st[b], 16)
                        if b < NB:
                            sp.wait_ge(rope_done, NB * h + b + 1)
                        else:
                            sp.wait_ge(q_done, NBL * h + b + 1)
                        sp.dma_start(t["q"][bass.ds(h, 1), :, tok:tok + n].rearrange("o p n -> (o p) n"),
                                     stage_q[0:HQ, b, 0:n]).then_inc(q_st[b], 16)
                steps(sp, H, store)
                for st in q_st + k_st:
                    sp.wait_ge(st, 16 * H)
                sp.wait_ge(kpe_st, 48)

            @block.scalar
            def _(act):
                act.wait_ge(const_done, 2)
                act.wait_ge(in_ld, 16 * IN)
                act.wait_ge(w_ld, 32)
                act.activation(wv_hi[:], wv[:], ACT.Copy).then_inc(hi_done, 1)

                def square(b):
                    tok, n = BLOCKS[b]
                    wait(act, sums_done, b)
                    act.activation(sq[:, 0:2, 0:n], qa[:, :, tok:tok + n], ACT.Square).then_inc(sq_done, 1)
                    act.activation(sq[:, 2, 0:n], ckv[:, PAST + tok:PAST + tok + n], ACT.Square).then_inc(sq_done, 1)

                square(0)
                for b, (tok, n) in enumerate(BLOCKS):
                    act.wait_ge(sums_done, b + 1)
                    wait(act, rstd_done, b)
                    act.activation(root[:, 0, 0:n], sums[:, 0, 0:n], ACT.Sqrt, scale=1.0 / QL, bias=eps[:]
                                   ).then_inc(root_done, 1)
                    act.activation(root[:, 1, 0:n], sums[:, 1, 0:n], ACT.Sqrt, scale=1.0 / KVL, bias=eps[:]
                                   ).then_inc(root_done, 1)
                    if b + 1 < NBL:
                        square(b + 1)
                    act.wait_ge(norm_done, 3 * b + 3)
                    act.activation(qn_hi[:, :, tok:tok + n], qa[:, :, tok:tok + n], ACT.Copy).then_inc(hi_done, 1)
                    at = 0 if b == 0 else PAST + tok
                    act.activation(ckv_hi[:, at:PAST + tok + n], ckv[:, at:PAST + tok + n], ACT.Copy
                                   ).then_inc(hi_done, 1)
                for k in range(KEYS // P):
                    act.wait_ge(v_mm, k + 1)
                    act.activation(V[:, :, k, :], pk[:, k % 2].rearrange("p (h d) -> p h d", h=H), ACT.Copy
                                   ).then_inc(v_done, 1)

                def heads(i):
                    for u in range(2):
                        h = 2 * i + u
                        wait(act, k_mm, KB * (h - 1))
                        act.activation(w_hi[:, u], wraw[:, bass.ds(h, 1)].rearrange("p o n -> p (o n)"), ACT.Copy
                                       ).then_inc(whi_done, 1)
                    for u in range(2):
                        h = 2 * i + u
                        for b, (tok, n) in enumerate(BLOCKS):
                            act.wait_ge(q_mm, NBL * h + b + 1)
                            wait(act, q_st[b], 16 * h)
                            act.activation(stage_q[0:HQ, b, 0:n], pq[0:HQ, b % 2, 0:n], ACT.Copy).then_inc(q_done, 1)
                            act.wait_ge(k_mm, KB * h + b + 1)
                            wait(act, k_st[b], 16 * h)
                            act.activation(stage_k[0:NOPE, b], pk[0:NOPE, b % 2], ACT.Copy).then_inc(k_done, 1)
                steps(act, H // 2, heads)

            @block.gpsimd
            def _(pool):
                pool.memset(ones[:], 1.0).then_inc(const_done, 1)
                pool.memset(eps[:], EPS).then_inc(const_done, 1)
                pool.wait_ge(hi_done, 1)
                pool.tensor_tensor(wv_lo[:], wv[:], wv_hi[:].bitcast(F32), ALU.subtract).then_inc(lo_done, 1)
                for b, (tok, n) in enumerate(BLOCKS):
                    pool.wait_ge(hi_done, 2 * b + 3)
                    pool.tensor_tensor(qn_lo[:, :, tok:tok + n], qa[:, :, tok:tok + n],
                                       qn_hi[:, :, tok:tok + n].bitcast(F32), ALU.subtract).then_inc(lo_done, 1)
                    at = 0 if b == 0 else PAST + tok
                    pool.tensor_tensor(ckv_lo[:, at:PAST + tok + n], ckv[:, at:PAST + tok + n],
                                       ckv_hi[:, at:PAST + tok + n].bitcast(F32), ALU.subtract).then_inc(lo_done, 1)

                def heads(i):
                    for u in range(2):
                        h = 2 * i + u
                        pool.wait_ge(whi_done, h + 1)
                        pool.tensor_tensor(w_lo[:, u], wraw[:, bass.ds(h, 1)].rearrange("p o n -> p (o n)"),
                                           w_hi[:, u].bitcast(F32), ALU.subtract).then_inc(wlo_done, 1)
                steps(pool, H // 2, heads)

            @block.tensor
            def _(pe):
                pe.wait_ge(const_done, 2)
                for b, (tok, n) in enumerate(BLOCKS):
                    pe.wait_ge(sq_done, 2 * b + 2)
                    wait(pe, root_done, 2 * b)
                    pe.matmul(sums[:, 0, 0:n], ones[:], sq[:, 0, 0:n], start=True, stop=False)
                    pe.matmul(sums[:, 0, 0:n], ones[:], sq[:, 1, 0:n], start=False, stop=True)
                    pe.matmul(sums[:, 1, 0:n], ones[:], sq[:, 2, 0:n], start=True, stop=True).then_inc(sums_done, 1)
                pe.wait_ge(in_ld, 16 * IN)
                for b in range(NB):
                    wait(pe, kr_rope, b - 1)
                    pe.matmul(rot[0:HQ, b % 2], perm[RO, :], kpe[RO, PAST + b * BLK:PAST + (b + 1) * BLK],
                              start=True, stop=True).then_inc(kr_mm, 1)
                pe.wait_ge(lo_done, 1 + 2 * NBL)
                for k in range(KEYS // P):
                    wait(pe, v_done, k - 1)
                    keys = slice(k * P, (k + 1) * P)
                    pe.matmul(pk[:, k % 2], ckv_hi[:, keys], wv_hi[:], start=True, stop=False)
                    pe.matmul(pk[:, k % 2], ckv_lo[:, keys], wv_hi[:], start=False, stop=False)
                    pe.matmul(pk[:, k % 2], ckv_hi[:, keys], wv_lo[:], start=False, stop=True).then_inc(v_mm, 1)
                pe.wait_ge(v_done, KEYS // P)
                pe.wait_ge(kr_rope, NB)

                def heads(i):
                    for u in range(2):
                        h = 2 * i + u
                        pe.wait_ge(wlo_done, h + 1)
                        for b, (tok, n) in enumerate(BLOCKS):
                            q = NBL * h + b
                            wait(pe, q_done, q if b == 0 else q - 1)
                            ops = [(w_hi, qn_hi), (w_lo, qn_hi), (w_hi, qn_lo)]
                            for k in range(2):
                                for o, (w, x) in enumerate(ops):
                                    mm = pe.matmul(pq[0:HQ, b % 2, 0:n], w[:, u, k * HQ:(k + 1) * HQ],
                                                   x[:, k, tok:tok + n], start=(k == 0 and o == 0),
                                                   stop=(k == 1 and o == 2))
                            mm.then_inc(q_mm, 1)
                            wait(pe, k_done, q if b == 0 else q - 1)
                            ops = [(w_hi, ckv_hi), (w_lo, ckv_hi), (w_hi, ckv_lo)]
                            for o, (w, x) in enumerate(ops):
                                mm = pe.matmul(pk[:, b % 2], w[:, u, 2 * HQ:], x[:, b * BLK:(b + 1) * BLK],
                                               start=(o == 0), stop=(o == 2))
                            mm.then_inc(k_mm, 1)
                            if b < NB:
                                pe.wait_ge(q_done, q + 1)
                                wait(pe, rope_done, NB * h + b - 1)
                                pe.matmul(rot[0:HQ, b % 2], perm[RO, :], stage_q[RO, b], start=True, stop=True
                                          ).then_inc(rot_mm, 1)
                steps(pe, H // 2, heads)

            @block.vector
            def _(dve):
                dve.wait_ge(in_ld, 16 * IN)
                for b, (tok, n) in enumerate(BLOCKS):
                    dve.wait_ge(root_done, 2 * b + 2)
                    wait(dve, norm_done, 3 * b)
                    dve.reciprocal(rstd[:, :, 0:n], root[:, :, 0:n]).then_inc(rstd_done, 1)
                    dve.wait_ge(rstd_done, b + 1)
                    for k in range(2):
                        x = qa[:, k, tok:tok + n]
                        dve.scalar_tensor_tensor(out=x, in0=x, scalar=gain[:, k:k + 1], in1=rstd[:, 0, 0:n],
                                                 op0=ALU.mult, op1=ALU.mult).then_inc(norm_done, 1)
                    x = ckv[:, PAST + tok:PAST + tok + n]
                    dve.scalar_tensor_tensor(out=x, in0=x, scalar=gain[:, 2:3], in1=rstd[:, 1, 0:n],
                                             op0=ALU.mult, op1=ALU.mult).then_inc(norm_done, 1)

                def rope(x, r, blk, parts, done):
                    wait(dve, part_done, parts)
                    dve.tensor_tensor(turned[RO, 0], x, cos[RO, blk], ALU.mult).then_inc(part_done, 1)
                    dve.tensor_tensor(turned[RO, 1], r, sin[RO, blk], ALU.mult).then_inc(part_done, 1)
                    dve.wait_ge(part_done, parts + 2)
                    dve.tensor_tensor(x, turned[RO, 0], turned[RO, 1], ALU.add).then_inc(done, 1)

                for b in range(NB):
                    dve.wait_ge(kr_mm, b + 1)
                    wait(dve, kr_rope, b)
                    rope(kpe[RO, PAST + b * BLK:PAST + (b + 1) * BLK], rot[RO, b % 2],
                         slice(b * BLK, (b + 1) * BLK), 2 * b, kr_rope)
                dve.wait_ge(kr_rope, NB)

                def heads(h):
                    for b in range(NB):
                        dve.wait_ge(rot_mm, NB * h + b + 1)
                        wait(dve, rope_done, NB * h + b)
                        rope(stage_q[RO, b], rot[RO, b % 2], slice(b * BLK, (b + 1) * BLK),
                             2 * (NB * h + b) + 2 * NB, rope_done)
                steps(dve, H, heads)


def attention_phase(nc, t, V, ident):
    NS = 9
    STEPS = [(b, c) for b in range(NB) for c in range(NS)] + [(NB, 0)]
    G = len(STEPS)
    BH = NB + 1
    PIECES = 5
    AT_STEP = {2: 0, 5: 1, 8: 2, 11: 3, 13: 4}
    FIRST_MAX = 2 * NS + 1
    KC, QC = KEYS // 2, T // 2
    PAIRS = H // 2
    LAG = 2
    with ExitStack() as ctx:
        p = Scope(nc, ctx, "at")
        q_hi = [p.sb(f"q_hi{u}", [HQ + 1, T], F32R) for u in range(2)]
        q_lo = [p.sb(f"q_lo{u}", [HQ, T], F32R) for u in range(2)]
        k_hi = [p.sb(f"k_hi{u}", [HQ + 1, KEYS], F32R) for u in range(2)]
        k_lo = [p.sb(f"k_lo{u}", [HQ, KEYS], F32R) for u in range(2)]
        v_hi = [p.sb(f"v_hi{u}", [P, KEYS // P, P], F32R) for u in range(2)]
        v_lo = [p.sb(f"v_lo{u}", [P, KEYS // P, P], F32R) for u in range(2)]
        raw = p.sb("raw", [HQ, KC])
        w = p.sb("w", [P, 2, 2, BLK])
        w_hi, w_lo = p.sb("w_hi", [P, LAG + 1, 2, BLK], F32R), p.sb("w_lo", [P, LAG + 1, 2, BLK], F32R)
        o = p.sb("o", [DV + 1, 2, BLK])
        mpart = p.sb("mpart", [P, 4, NS])
        mfin = p.sb("mfin", [P, 4])
        sc = p.ps("sc", [P, 4, BLK])
        mx = p.ps("mx", [P, 4, 256])
        acc = p.ps("acc", [P, 2, BLK])
        raw_ld, kpe_ld, o_st = p.sem("raw_ld"), p.sem("kpe_ld"), p.sem("o_st")
        hi_piece, lo_piece, kpe_hi, kpe_lo = (p.sem(n) for n in ("hi_piece", "lo_piece", "kpe_hi", "kpe_lo"))
        s_mm, exp_done, hi_done, lo_done, pv_mm = (p.sem(n) for n in ("s_mm", "exp_done", "hi_done", "lo_done", "pv_mm"))
        m_mm, red_done, mfin_done, tr_done, row_done = (p.sem(n) for n in ("m_mm", "red_done", "mfin_done", "tr_done", "row_done"))
        o_done, o_free, const_done = (p.sem(n) for n in ("o_done", "o_free", "const_done"))
        SLOTS = 2

        def max_of(u, b, last):
            if b < 2:
                return u, b + 2
            if last and u == 1:
                return None
            return 1 - u, (b - 2 if b < NB else NB)

        def blocks_in(last):
            out, before = [], (0, NB)
            for u in range(2):
                for b in range(BH):
                    out.append((u, b, before))
                    before = max_of(u, b, last)
            return out

        def needs_row(h, b):
            return {0: 5 * h + 1, 1: 5 * h + 2, 2: 5 * h + 4, 3: 5 * h + 5, 4: 5 * h + 3}[b]

        def piece_load(sp, h, r):
            wait(sp, lo_piece, PIECES * h + r if r else PIECES * h - 1)
            if r < 2:
                sp.dma_start(raw[0:NOPE, :], t["k"][bass.ds(h, 1), :, r * KC:(r + 1) * KC].rearrange("o p n -> (o p) n")
                             ).then_inc(raw_ld, 16)
            else:
                sp.dma_start(raw[0:HQ, 0:QC], t["q"][bass.ds(h, 1), :, (r - 2) * QC:(r - 1) * QC].rearrange("o p n -> (o p) n")
                             ).then_inc(raw_ld, 16)

        def piece_aps(u, r, rows, h):
            if r < 2:
                c = slice(r * KC, (r + 1) * KC)
                return raw[rows, :], k_hi[u][rows, c], k_lo[u][rows, c]
            if r < 4:
                c = slice((r - 2) * QC, (r - 1) * QC)
                return raw[0:HQ, 0:QC], q_hi[u][0:HQ, c], q_lo[u][0:HQ, c]
            return (V[:, bass.ds(h, 1)].rearrange("p o k d -> p (o k) d"),
                    v_hi[u][:, :, 0:DV], v_lo[u][:, :, 0:DV])

        def max_products(pe, buf, b, c, count):
            pe.wait_ge(lo_piece, count)
            tok, n = BLOCKS[b]
            k0 = c * 256 if b < NB else PAST + S
            for q in range(n // P):
                mm = pe.matmul(mx[:, q, :], q_hi[buf][0:HQ, tok + q * P:tok + (q + 1) * P],
                               k_hi[buf][0:HQ, k0:k0 + 256], start=True, stop=True)
            return mm

        def turn_max(pe, b):
            for q in range(BLOCKS[b][1] // P):
                mm = pe.transpose(mx[0:1, q, 0:P], mfin[:, q:q + 1], ident[:])
            return mm

        with nc.Block() as block:
            @block.sync
            def _(sp):
                sp.sem_inc(o_free, SLOTS)
                for r in range(4):
                    piece_load(sp, 0, r)
                    if r < 2:
                        wait(sp, kpe_lo, r)
                        sp.dma_start(raw[NOPE:HQ, :], t["kpe"][:, r * KC:(r + 1) * KC]).then_inc(kpe_ld, 16)

                def pair(i, last):
                    for u in range(2):
                        h = 2 * i + u
                        if not (last and u == 1):
                            for r in range(4):
                                piece_load(sp, h + 1, r)
                        for b, (tok, n) in enumerate(BLOCKS):
                            j = BH * h + b
                            sp.wait_ge(o_done, SLOTS + j + 1)
                            slot = (BH * u + b) % 2
                            sp.dma_start(t["o"][bass.ds(h * DV, DV), tok:tok + n], o[0:DV, slot, 0:n]).then_inc(o_st, 16)
                            sp.dma_start(t["sums"][bass.ds(h, 1), tok:tok + n], o[DV:DV + 1, slot, 0:n]).then_inc(o_st, 16)
                            sp.wait_ge(o_st, 32 * j + 32)
                            sp.sem_inc(o_free, 1)
                with sp.Fori(0, PAIRS - 1) as i:
                    pair(i, False)
                pair(PAIRS - 1, True)

            @block.scalar
            def _(act):
                act.sem_inc(exp_done, SLOTS)

                def split(u, h, r, rows=slice(0, NOPE)):
                    if r < 4:
                        act.wait_ge(raw_ld, 16 * (4 * h + r + 1))
                    src, hi, _ = piece_aps(u, r, rows, h)
                    act.activation(hi, src, ACT.Copy).then_inc(hi_piece, 1)
                act.wait_ge(const_done, 6)
                for r in range(PIECES):
                    if r < 2:
                        act.wait_ge(kpe_ld, 16 * r + 16)
                        c = slice(r * KC, (r + 1) * KC)
                        act.activation(k_hi[1][NOPE:HQ, c], raw[NOPE:HQ, :], ACT.Copy).then_inc(kpe_hi, 1)
                    split(0, 0, r, slice(0, HQ))

                def pair(i, last):
                    for u in range(2):
                        h = 2 * i + u
                        for l, (b, c) in enumerate(STEPS):
                            g, slot, n = G * h + l, (G * u + l) % 2, BLOCKS[b][1]
                            act.wait_ge(s_mm, g + 1)
                            act.wait_ge(lo_done, g + 1)
                            act.activation(w[:, slot, :, 0:n], sc[:, 2 * slot:2 * slot + 2, 0:n], ACT.Exp, scale=SM_SCALE
                                           ).then_inc(exp_done, 1)
                            act.wait_ge(exp_done, SLOTS + g + 1)
                            gu = G * u + l
                            act.wait_ge(pv_mm, SLOTS + (g - LAG if gu > LAG else 2 * G * i))
                            act.activation(w_hi[:, gu % (LAG + 1), :, 0:n], w[:, slot, :, 0:n], ACT.Copy).then_inc(hi_done, 1)
                            if l in AT_STEP and not (last and u == 1):
                                split(1 - u, h + 1, AT_STEP[l])
                with act.Fori(0, PAIRS - 1) as i:
                    pair(i, False)
                pair(PAIRS - 1, True)

            @block.gpsimd
            def _(pool):
                def split(u, h, r, rows=slice(0, NOPE)):
                    pool.wait_ge(hi_piece, PIECES * h + r + 1)
                    src, hi, lo = piece_aps(u, r, rows, h)
                    pool.tensor_tensor(lo, src, hi.bitcast(F32), ALU.subtract).then_inc(lo_piece, 1)
                pool.wait_ge(const_done, 6)
                for r in range(PIECES):
                    if r < 2:
                        pool.wait_ge(kpe_hi, r + 1)
                        wait(pool, lo_piece, r)
                        c = slice(r * KC, (r + 1) * KC)
                        pool.tensor_tensor(k_lo[1][NOPE:HQ, c], raw[NOPE:HQ, :], k_hi[1][NOPE:HQ, c].bitcast(F32),
                                           ALU.subtract).then_inc(kpe_lo, 1)
                        pool.wait_ge(kpe_lo, r + 1)
                    split(0, 0, r, slice(0, HQ))

                def pair(i, last):
                    for u in range(2):
                        if not (last and u == 1):
                            for r in range(PIECES):
                                split(1 - u, 2 * i + u + 1, r)
                with pool.Fori(0, PAIRS - 1) as i:
                    pair(i, False)
                pair(PAIRS - 1, True)

            @block.tensor
            def _(pe):
                pe.sem_inc(pv_mm, SLOTS)
                pe.wait_ge(const_done, 6)
                m = 0
                for x, b in enumerate((0, 1, NB)):
                    for c in range(NS if b < NB else 1):
                        wait(pe, red_done, m)
                        if c == 0 and x:
                            pe.wait_ge(mfin_done, x)
                            turn_max(pe, (0, 1, NB)[x - 1]).then_inc(tr_done, 1)
                            pe.wait_ge(row_done, x)
                        max_products(pe, 0, b, c, 4).then_inc(m_mm, 1)
                        m += 1

                def pair(i, last):
                    before = blocks_in(last)

                    def value_product(h, l, gu):
                        b, c = STEPS[l]
                        g, slot, n, u = G * h + l, gu % (LAG + 1), BLOCKS[b][1], gu // G
                        k0 = 2 * c if b < NB else (PAST + S) // P
                        if c == 0:
                            pe.wait_ge(o_done, BH * h + b + 1)
                        pe.wait_ge(lo_done, SLOTS + g + 1)
                        bank = acc[:, (BH * u + b) % 2, 0:n]
                        end = b == NB or c == NS - 1
                        for k in range(2):
                            pe.matmul(bank, v_hi[u][:, k0 + k, :], w_hi[:, slot, k, 0:n],
                                      start=(c == 0 and k == 0), stop=False)
                            pe.matmul(bank, v_lo[u][:, k0 + k, :], w_hi[:, slot, k, 0:n], start=False, stop=False)
                            mm = pe.matmul(bank, v_hi[u][:, k0 + k, :], w_lo[:, slot, k, 0:n],
                                           start=False, stop=(end and k == 1))
                        mm.then_inc(pv_mm, 1)

                    for u in range(2):
                        h = 2 * i + u
                        pe.wait_ge(lo_piece, PIECES * h + PIECES)
                        for l, (b, c) in enumerate(STEPS):
                            g, gu = G * h + l, G * u + l
                            slot = gu % 2
                            tok, n = BLOCKS[b]
                            k0 = 2 * c if b < NB else (PAST + S) // P
                            x = 3 + BH * h + b
                            tail = before[BH * u + b][2]
                            if c == 0 and tail is not None:
                                pe.wait_ge(mfin_done, x)
                                turn_max(pe, tail[1]).then_inc(tr_done, 1)
                            if c == 0:
                                pe.wait_ge(row_done, needs_row(h, b))
                            pe.wait_ge(exp_done, g + 1)
                            for k in range(2):
                                keys = slice((k0 + k) * P, (k0 + k + 1) * P)
                                bank = sc[:, 2 * slot + k, 0:n]
                                pe.matmul(bank, k_hi[u][:, keys], q_hi[u][:, tok:tok + n], start=True, stop=False)
                                pe.matmul(bank, k_lo[u][:, keys], q_hi[u][0:HQ, tok:tok + n], start=False, stop=False)
                                mm = pe.matmul(bank, k_hi[u][0:HQ, keys], q_lo[u][:, tok:tok + n], start=False, stop=True)
                            mm.then_inc(s_mm, 1)
                            ahead = max_of(u, b, last)
                            if ahead is not None:
                                if c == 0:
                                    pe.wait_ge(row_done, x)
                                pe.wait_ge(red_done, FIRST_MAX + g)
                                owner = h + 1 if ahead[0] != u else h
                                max_products(pe, ahead[0], ahead[1], c, PIECES * owner + 4).then_inc(m_mm, 1)
                            if gu >= LAG:
                                value_product(h if l >= LAG else h - 1, (gu - LAG) % G, gu - LAG)
                    for l in range(G - LAG, G):
                        value_product(h, l, G + l)
                with pe.Fori(0, PAIRS - 1) as i:
                    pair(i, False)
                pair(PAIRS - 1, True)

            @block.vector
            def _(dve):
                dve.sem_inc(lo_done, SLOTS)
                dve.sem_inc(o_done, SLOTS)
                for u in range(2):
                    dve.memset(k_hi[u][HQ:HQ + 1, :].bitcast(F32), 1.0).then_inc(const_done, 1)
                    dve.memset(v_hi[u][:, :, DV:].bitcast(F32), 1.0).then_inc(const_done, 1)
                    dve.memset(v_lo[u][:, :, DV:].bitcast(F32), 0.0).then_inc(const_done, 1)

                def reduce_max(b, c, m):
                    q = BLOCKS[b][1] // P
                    dve.wait_ge(m_mm, m + 1)
                    dve.tensor_reduce(mpart[:, 0:q, c], mx[:, 0:q, :], AX.X, ALU.max).then_inc(red_done, 1)
                    if b == NB or c == NS - 1:
                        dve.wait_ge(red_done, m + 1)
                        dve.tensor_reduce(mfin[:, 0:q], mpart[:, 0:q, 0:c + 1], AX.X, ALU.max).then_inc(mfin_done, 1)

                def write_row(buf, b, x):
                    tok, n = BLOCKS[b]
                    dve.wait_ge(tr_done, x + 1)
                    dve.tensor_scalar(q_hi[buf][HQ:HQ + 1, tok:tok + n].rearrange("p (q n) -> p q n", n=P),
                                      mx[0:1, 0:n // P, 0:P], -1.0, None, ALU.mult).then_inc(row_done, 1)

                m = 0
                for x, b in enumerate((0, 1, NB)):
                    for c in range(NS if b < NB else 1):
                        if c == 0 and x:
                            write_row(0, (0, 1, NB)[x - 1], x - 1)
                        reduce_max(b, c, m)
                        m += 1

                def pair(i, last):
                    before = blocks_in(last)

                    def take_out(h, u, b):
                        j, slot, n = BH * h + b, (BH * u + b) % 2, BLOCKS[b][1]
                        dve.wait_ge(pv_mm, SLOTS + G * h + (NS * b + NS if b < NB else G))
                        dve.wait_ge(o_free, j + 1)
                        dve.tensor_copy(o[:, slot, 0:n], acc[0:DV + 1, slot, 0:n]).then_inc(o_done, 1)

                    for u in range(2):
                        h = 2 * i + u
                        for l, (b, c) in enumerate(STEPS):
                            g, slot, n = G * h + l, (G * u + l) % 2, BLOCKS[b][1]
                            tail = before[BH * u + b][2]
                            if c == 0 and tail is not None:
                                write_row(*tail, 2 + BH * h + b)
                            ahead = max_of(u, b, last)
                            if ahead is not None:
                                reduce_max(ahead[1], c, FIRST_MAX + g)
                            dve.wait_ge(hi_done, g + 1)
                            s3 = (G * u + l) % (LAG + 1)
                            dve.tensor_tensor(w_lo[:, s3, :, 0:n], w[:, slot, :, 0:n], w_hi[:, s3, :, 0:n].bitcast(F32),
                                              ALU.subtract).then_inc(lo_done, 1)
                            if c == LAG - 1 and b:
                                take_out(h, u, b - 1)
                            elif c == LAG - 1 and u:
                                take_out(h - 1, 0, NB - 1)
                                take_out(h - 1, 0, NB)
                    take_out(h, 1, NB - 1)
                    take_out(h, 1, NB)
                with dve.Fori(0, PAIRS - 1) as i:
                    pair(i, False)
                pair(PAIRS - 1, True)


def mix_phase(nc, t):
    M = D // P
    NBL = len(BLOCKS)
    with ExitStack() as ctx:
        p = Scope(nc, ctx, "mx")
        wraw = p.sb("wraw", [P, CT, D])
        wc_hi, wc_lo = p.sb("wc_hi", [P, CT, D], F32R), p.sb("wc_lo", [P, CT, D], F32R)
        wo_hi, wo_lo = p.sb("wo_hi", [P, CT, D], F32R), p.sb("wo_lo", [P, CT, D], F32R)
        c = p.sb("c", [P, CT, BLK])
        sq = p.sb("sq", [P, CT, BLK])
        o = p.sb("o", [P, CT, BLK])
        c_hi, c_lo = p.sb("c_hi", [P, 2, CT, BLK], F32R), p.sb("c_lo", [P, 2, CT, BLK], F32R)
        o_hi, o_lo = p.sb("o_hi", [P, 2, CT, BLK], F32R), p.sb("o_lo", [P, 2, CT, BLK], F32R)
        gates = p.sb("gates", [P, 2, 2, BLK])
        mixed = p.sb("mixed", [P, 2, BLK])
        root, rstd = p.sb("root", [P, BLK]), p.sb("rstd", [P, BLK])
        mean_w = p.sb("mean_w", [P, P])
        inv = p.sb("inv", [P, CT, BLK])
        sums = p.sb("sums", [P, 2, H * T // P])
        sums_ld, inv_done, inv_st, inv_ld, o_scaled = (p.sem(n) for n in ("sums_ld", "inv_done", "inv_st", "inv_ld", "o_scaled"))
        norm = p.sb("norm", [P, 2, CT])
        eps = p.sb("eps", [P, 1])
        mean, var = p.ps("mean", [P, BLK]), p.ps("var", [P, BLK])
        pc, po = p.ps("pc", [P, 2, BLK]), p.ps("po", [P, 2, BLK])
        w_ld, in_ld, norm_ld = p.sems("w_ld", CT), p.sem("in_ld"), p.sem("norm_ld")
        g_ld, mix_st = p.sems("g_ld", 2), p.sems("mix_st", 2)
        const_done, w_hi_done, w_lo_done = p.sem("const_done"), p.sem("w_hi_done"), p.sems("w_lo_done", 2)
        mean_mm, cent_done, sq_done, var_mm = (p.sem(n) for n in ("mean_mm", "cent_done", "sq_done", "var_mm"))
        root_done, rstd_done, y_done, silu_done = (p.sem(n) for n in ("root_done", "rstd_done", "y_done", "silu_done"))
        hi_done, lo_done, mm_done, gated, mix_done = (p.sem(n) for n in ("hi_done", "lo_done", "mm_done", "gated", "mix_done"))

        def split_w_lo(eng, j):
            hi, lo = (wc_hi, wc_lo) if j >= CT else (wo_hi, wo_lo)
            eng.wait_ge(w_hi_done, j + 1)
            eng.tensor_tensor(lo[:, j % CT], wraw[:, j % CT], hi[:, j % CT].bitcast(F32), ALU.subtract
                              ).then_inc(w_lo_done[j % 2], 1)

        with nc.Block() as block:
            @block.sync
            def _(sp):
                def load(b):
                    tok, n = BLOCKS[b]
                    wait(sp, hi_done, 2 * b)
                    wait(sp, lo_done, 2 * b)
                    sp.dma_start(c[:, :, 0:n], t["conv"][:, tok:tok + n].rearrange("(k p) n -> p k n", p=P)
                                 ).then_inc(in_ld, 16)
                    sp.dma_start(o[:, :, 0:n], t["o"][:, tok:tok + n].rearrange("(k p) n -> p k n", p=P)
                                 ).then_inc(in_ld, 16)
                    if b == 0:
                        sp.wait_ge(inv_done, 1)
                        sp.dma_start(flat(t["inverse"]), sums[:, 1]).then_inc(inv_st, 16)
                        sp.wait_ge(inv_st, 16)
                    for h in range(H):
                        sp.dma_start(inv[h % 2 * DV:h % 2 * DV + DV, h // 2, 0:n],
                                     t["inverse"][h, tok:tok + n].partition_broadcast(DV)).then_inc(inv_ld, 16)
                def flat(rows):
                    return rows.rearrange("h (g n) -> (h g) n", n=H * T // P)
                sp.dma_start(norm[:], t["conv_norm"]).then_inc(norm_ld, 16)
                sp.dma_start(sums[:, 0], flat(t["sums"])).then_inc(sums_ld, 16)

                def load_w(j):
                    if j >= CT:
                        sp.wait_ge(w_lo_done[j % 2], (j - CT) // 2 + 1)
                    sp.dma_start(wraw[:, j % CT], t["w_conv_out" if j >= CT else "w_o"][:, j % CT]).then_inc(w_ld[j % CT], 16)
                for j in range(CT):
                    load_w(j)
                load(0)
                for j in range(CT, 2 * CT):
                    load_w(j)
                for b, (tok, n) in enumerate(BLOCKS):
                    if b + 1 < NBL:
                        load(b + 1)
                    for m in range(M):
                        j = M * b + m
                        wait(sp, mix_done, j - 1)
                        for g in range(2):
                            sp.dma_start(gates[:, m % 2, g, 0:n], t["gates"][g * D + m * P:g * D + (m + 1) * P, tok:tok + n]
                                         ).then_inc(g_ld[m % 2], 16)

            @block.gpsimd
            def _(pool):
                pool.memset(mean_w[:], 1.0 / CONV).then_inc(const_done, 1)
                pool.memset(eps[:], EPS).then_inc(const_done, 1)
                for j in (0, 2):
                    split_w_lo(pool, j)
                for b, (tok, n) in enumerate(BLOCKS):
                    pool.wait_ge(in_ld, 32 * b + 32)
                    pool.wait_ge(inv_ld, 16 * H * (b + 1))
                    pool.tensor_tensor(o[:, :, 0:n], o[:, :, 0:n], inv[:, :, 0:n], ALU.mult).then_inc(o_scaled, 1)
                    for q, (src, hi, lo) in enumerate(((o, o_hi, o_lo), (c, c_hi, c_lo))):
                        if b == 0 and q == 1:
                            for j in (CT, CT + 2):
                                split_w_lo(pool, j)
                        pool.wait_ge(hi_done, 2 * b + q + 1)
                        pool.tensor_tensor(lo[:, b % 2, :, 0:n], src[:, :, 0:n], hi[:, b % 2, :, 0:n].bitcast(F32),
                                           ALU.subtract).then_inc(lo_done, 1)

            @block.scalar
            def _(act):
                act.wait_ge(const_done, 2)
                act.wait_ge(norm_ld, 16)

                def store(j):
                    b, m = divmod(j, M)
                    tok, n = BLOCKS[b]
                    act.wait_ge(mix_done, j + 1)
                    act.dma_start(t["mixed"][m * P:(m + 1) * P, tok:tok + n], mixed[:, m % 2, 0:n]
                                  ).then_inc(mix_st[m % 2], 16)

                def prepare(b):
                    tok, n = BLOCKS[b]
                    act.wait_ge(in_ld, 32 * b + 32)
                    wait(act, mm_done, M * (b - 1))
                    act.wait_ge(cent_done, CT * b + CT)
                    act.activation(sq[:, :, 0:n], c[:, :, 0:n], ACT.Square).then_inc(sq_done, 1)
                    act.wait_ge(o_scaled, b + 1)
                    act.activation(o_hi[:, b % 2, :, 0:n], o[:, :, 0:n], ACT.Copy).then_inc(hi_done, 1)
                    yield
                    act.wait_ge(var_mm, b + 1)
                    wait(act, rstd_done, b)
                    act.activation(root[:, 0:n], var[:, 0:n], ACT.Sqrt, bias=eps[:]).then_inc(root_done, 1)
                    act.wait_ge(y_done, CT * b + CT)
                    for k in range(CT):
                        act.activation(c[:, k, 0:n], c[:, k, 0:n], ACT.Silu, bias=norm[:, 1, k:k + 1]
                                       ).then_inc(silu_done, 1)
                    act.wait_ge(silu_done, CT * b + CT)
                    act.activation(c_hi[:, b % 2, :, 0:n], c[:, :, 0:n], ACT.Copy).then_inc(hi_done, 1)

                def split_w_hi(j):
                    act.wait_ge(w_ld[j % CT], 16 * (j // CT) + 16)
                    act.activation((wc_hi if j >= CT else wo_hi)[:, j % CT], wraw[:, j % CT], ACT.Copy).then_inc(w_hi_done, 1)
                for j in range(CT):
                    split_w_hi(j)
                for _ in prepare(0):
                    for j in range(CT, 2 * CT):
                        split_w_hi(j)
                for b in range(NBL):
                    ahead = prepare(b + 1) if b + 1 < NBL else iter(())
                    for m in range(M):
                        store(M * b + m)
                        if m in (2, 4):
                            next(ahead, None)
                for u in range(2):
                    act.wait_ge(mix_st[u], 16 * NBL * M // 2)

            @block.vector
            def _(dve):
                dve.wait_ge(sums_ld, 16)
                dve.reciprocal(sums[:, 1], sums[:, 0]).then_inc(inv_done, 1)
                dve.wait_ge(norm_ld, 16)

                def prepare(b):
                    tok, n = BLOCKS[b]
                    dve.wait_ge(mean_mm, b + 1)
                    for k in range(CT):
                        dve.tensor_tensor(c[:, k, 0:n], c[:, k, 0:n], mean[:, 0:n], ALU.subtract).then_inc(cent_done, 1)
                    yield
                    dve.wait_ge(root_done, b + 1)
                    wait(dve, y_done, CT * b)
                    dve.reciprocal(rstd[:, 0:n], root[:, 0:n]).then_inc(rstd_done, 1)
                    dve.wait_ge(rstd_done, b + 1)
                    for k in range(CT):
                        dve.scalar_tensor_tensor(out=c[:, k, 0:n], in0=c[:, k, 0:n], scalar=norm[:, 0, k:k + 1],
                                                 in1=rstd[:, 0:n], op0=ALU.mult, op1=ALU.mult).then_inc(y_done, 1)

                for j in (1, 3):
                    split_w_lo(dve, j)
                for _ in prepare(0):
                    for j in (CT + 1, CT + 3):
                        split_w_lo(dve, j)
                for b, (tok, n) in enumerate(BLOCKS):
                    ahead = prepare(b + 1) if b + 1 < NBL else iter(())
                    for m in range(M):
                        j = M * b + m
                        u = m % 2
                        dve.wait_ge(g_ld[u], 32 * (j // 2 + 1))
                        dve.wait_ge(mm_done, j + 1)
                        for g, bank in enumerate((pc, po)):
                            dve.tensor_tensor(gates[:, u, g, 0:n], bank[:, u, 0:n], gates[:, u, g, 0:n], ALU.mult
                                              ).then_inc(gated, 1)
                        wait(dve, mix_st[u], 16 * (j // 2))
                        dve.wait_ge(gated, 2 * j + 2)
                        dve.tensor_tensor(mixed[:, u, 0:n], gates[:, u, 0, 0:n], gates[:, u, 1, 0:n], ALU.add
                                          ).then_inc(mix_done, 1)
                        if m in (2, 4):
                            next(ahead, None)

            @block.tensor
            def _(pe):
                pe.wait_ge(const_done, 2)

                def average(b, out, src, done):
                    n = BLOCKS[b][1]
                    for k in range(CT):
                        mm = pe.matmul(out[:, 0:n], mean_w[:], src[:, k, 0:n], start=(k == 0), stop=(k == CT - 1))
                    mm.then_inc(done, 1)

                pe.wait_ge(in_ld, 32)
                average(0, mean, c, mean_mm)
                pe.wait_ge(sq_done, 1)
                average(0, var, sq, var_mm)
                pe.wait_ge(w_lo_done[0], CT)
                pe.wait_ge(w_lo_done[1], CT)
                for b, (tok, n) in enumerate(BLOCKS):
                    pe.wait_ge(lo_done, 2 * b + 2)
                    for m in range(M):
                        j, u = M * b + m, m % 2
                        wait(pe, mix_done, j - 1)
                        cols = slice(m * P, (m + 1) * P)
                        for bank, w, x in ((pc, (wc_hi, wc_lo), (c_hi, c_lo)), (po, (wo_hi, wo_lo), (o_hi, o_lo))):
                            for k in range(CT):
                                for q, (a, e) in enumerate(((0, 0), (1, 0), (0, 1))):
                                    mm = pe.matmul(bank[:, u, 0:n], w[a][:, k, cols], x[e][:, b % 2, k, 0:n],
                                                   start=(k == 0 and q == 0), stop=(k == CT - 1 and q == 2))
                        mm.then_inc(mm_done, 1)
                        if b + 1 < NBL and m == 1:
                            pe.wait_ge(in_ld, 32 * b + 64)
                            pe.wait_ge(cent_done, CT * b + CT)
                            average(b + 1, mean, c, mean_mm)
                        if b + 1 < NBL and m == 4:
                            pe.wait_ge(sq_done, b + 2)
                            pe.wait_ge(root_done, b + 1)
                            average(b + 1, var, sq, var_mm)


def out_phase(nc, t, affT, ident):
    PAIRS = T // P // 2
    with ExitStack() as ctx:
        p = Scope(nc, ctx, "op")
        wraw = p.sb("wraw", [P, 2, D])
        w_hi, w_lo = p.sb("w_hi", [P, KD, D], F32R), p.sb("w_lo", [P, KD, D], F32R)
        gate, gain, shift = p.sb("gate", [P, 2, D]), p.sb("gain", [P, 2, D]), p.sb("shift", [P, 2, D])
        norm = p.sb("norm", [P, D])
        m_raw = p.sb("m_raw", [P, 2, KD, 2 * P])
        m_hi, m_lo = p.sb("m_hi", [P, 2, KD, 2 * P], F32R), p.sb("m_lo", [P, 2, KD, 2 * P], F32R)
        x, h = p.sb("x", [P, 2, D]), p.sb("h", [P, 2, D])
        y = p.sb("y", [P, 2, D])
        hT = p.sb("hT", [P, 2, KD, P])
        w_r = p.sb("w_r", [P, KD, E])
        sumsq, meansq, root, rstd = (p.sb(n, [P, 2]) for n in ("sumsq", "meansq", "root", "rstd"))
        top, esum, einv = (p.sb(n, [P, 2]) for n in ("top", "esum", "einv"))
        ex, aff = p.sb("ex", [P, 2, E]), p.sb("aff", [P, 2, E])
        po = p.ps("po", [P, 2, D])
        tp = p.ps("tp", [P, D])
        lg = p.ps("lg", [P, 2, E])
        at = p.ps("at", [E, 2, P])
        w_ld, wr_ld = p.sems("w_ld", 2), p.sem("wr_ld")
        rows_ld, m_ld = p.sem("rows_ld"), p.sems("m_ld", 2)
        x_ld, x2_st, h_st = p.sems("x_ld", 2), p.sems("x2_st", 2), p.sems("h_st", 2)
        w_hi_done, w_lo_done = p.sem("w_hi_done"), p.sems("w_lo_done", 2)
        m_hi_done, m_lo_done = p.sem("m_hi_done"), p.sem("m_lo_done")
        gain_done, mm_done, gated, x2_done = (p.sem(n) for n in ("gain_done", "mm_done", "gated", "x2_done"))
        sq_done, ms_done, root_done, rstd_done = (p.sem(n) for n in ("sq_done", "ms_done", "root_done", "rstd_done"))
        scaled, h_done, tp_done, hT_done = (p.sem(n) for n in ("scaled", "h_done", "tp_done", "hT_done"))
        lg_done, top_done, ex_done, einv_done = (p.sem(n) for n in ("lg_done", "top_done", "ex_done", "einv_done"))
        aff_done, at_done, affT_done = (p.sem(n) for n in ("aff_done", "at_done", "affT_done"))

        def pipeline(eng, step):
            step(0, 0, 0, True, False, False)
            step(0, 1, 0, True, True, False)
            with eng.Fori(1, (PAIRS - 1) // 2) as c:
                step(c, 0, 0, True, True, True)
                step(c, 1, 0, True, True, True)
            step(PAIRS // 2, 0, 1, True, True, True)
            step(PAIRS // 2, 1, 1, False, True, True)
            step(PAIRS // 2 + 1, 0, 1, False, False, True)

        with nc.Block() as block:
            @block.sync
            def _(sp):
                def load_m(i, slot):
                    wait(sp, m_lo_done, i - 1)
                    sp.dma_start(m_raw[:, slot], t["mixed"][:, bass.ds(i * 2 * P, 2 * P)].rearrange("(k p) n -> p k n", p=P)
                                 ).then_inc(m_ld[slot], 16)

                def load_x(i, u):
                    sp.dma_start(x[:, u], t["x"][bass.ds((2 * i + u) * P, P), :]).then_inc(x_ld[u], 16)

                for k in range(KD):
                    if k > 1:
                        sp.wait_ge(w_lo_done[k % 2], k // 2)
                    sp.dma_start(wraw[:, k % 2], t["w_out"][k * P:(k + 1) * P, :]).then_inc(w_ld[k % 2], 16)
                    if k == 1:
                        load_m(0, 0)
                    if k == 2:
                        sp.dma_start(gate[:, 0], t["mod"][0, 2 * D:3 * D].partition_broadcast(P)).then_inc(rows_ld, 16)
                        sp.dma_start(gate[:, 1], t["mod"][1, 2 * D:3 * D].partition_broadcast(P)).then_inc(rows_ld, 16)
                load_x(0, 0)
                load_x(0, 1)
                for s in range(2):
                    for dst, at_col in ((shift, 3), (gain, 4)):
                        sp.dma_start(dst[:, s], t["mod"][s, at_col * D:(at_col + 1) * D].partition_broadcast(P)
                                     ).then_inc(rows_ld, 16)
                sp.dma_start(norm[:], t["norm2"].partition_broadcast(P)).then_inc(rows_ld, 16)
                sp.dma_start(w_r[:], t["w_router"]).then_inc(wr_ld, 16)

                def step(c, slot, s, cur, prev, old):
                    i = 2 * c + slot
                    if not cur:
                        return
                    if s == 0:
                        load_m(i + 1, 1 - slot)
                    for u in range(2):
                        j = 2 * i + u
                        sp.wait_ge(x2_done, j + 1)
                        sp.dma_start(t["x2"][bass.ds(j * P, P), :], y[:, u]).then_inc(x2_st[u], 16)
                        if s == 0:
                            load_x(i + 1, u)
                    for u in range(2):
                        j = 2 * i + u
                        sp.wait_ge(h_done, j + 1)
                        sp.dma_start(t["h2"][bass.ds(j * P, P), :], h[:, u]).then_inc(h_st[u], 16)
                pipeline(sp, step)
                for u in range(2):
                    sp.wait_ge(x2_st[u], 16 * PAIRS)
                    sp.wait_ge(h_st[u], 16 * PAIRS)

            @block.scalar
            def _(act):
                def split_m(i, slot, half):
                    act.wait_ge(m_ld[slot], 16 * half + 16)
                    wait(act, mm_done, 2 * i - 2)
                    act.activation(m_hi[:, slot], m_raw[:, slot], ACT.Copy).then_inc(m_hi_done, 1)

                for k in range(KD):
                    act.wait_ge(w_ld[k % 2], 16 * (k // 2 + 1))
                    act.activation(w_hi[:, k], wraw[:, k % 2], ACT.Copy).then_inc(w_hi_done, 1)
                    if k == 1:
                        split_m(0, 0, 0)

                def step(c, slot, s, cur, prev, old):
                    i = 2 * c + slot
                    if cur and s == 0:
                        split_m(i + 1, 1 - slot, c + slot)
                    for u in range(2):
                        if prev:
                            j = 2 * (i - 1) + u
                            act.wait_ge(tp_done, j + 1)
                            wait(act, lg_done, i - 1)
                            act.activation(hT[:, u], tp[:].rearrange("p (k n) -> p k n", k=KD), ACT.Copy).then_inc(hT_done, 1)
                        if cur:
                            j = 2 * i + u
                            act.wait_ge(x2_done, j + 1)
                            wait(act, tp_done, j - 1)
                            wait(act, h_st[u], 16 * i)
                            act.activation(h[:, u], y[:, u], ACT.Square, accum_out=sumsq[:, u:u + 1]).then_inc(sq_done, 1)
                            act.wait_ge(ms_done, j + 1)
                            act.activation(root[:, u:u + 1], meansq[:, u:u + 1], ACT.Sqrt).then_inc(root_done, 1)
                        if old and u == 0:
                            act.wait_ge(top_done, i - 1)
                            for v in range(2):
                                act.activation(ex[:, v], lg[:, v], ACT.Exp, bias=top[:, v:v + 1], accum_out=esum[:, v:v + 1]
                                               ).then_inc(ex_done, 1)
                    if old:
                        act.wait_ge(at_done, i - 1)
                        act.activation(affT[:, bass.ds((i - 2) * 2 * P, 2 * P)], at[:].rearrange("e u n -> e (u n)"), ACT.Copy
                                       ).then_inc(affT_done, 1)
                pipeline(act, step)

            @block.gpsimd
            def _(pool):
                def split_m(i, slot):
                    pool.wait_ge(m_hi_done, i + 1)
                    pool.tensor_tensor(m_lo[:, slot], m_raw[:, slot], m_hi[:, slot].bitcast(F32), ALU.subtract
                                       ).then_inc(m_lo_done, 1)

                for k in range(0, KD, 2):
                    pool.wait_ge(w_hi_done, k + 1)
                    pool.tensor_tensor(w_lo[:, k], wraw[:, 0], w_hi[:, k].bitcast(F32), ALU.subtract
                                       ).then_inc(w_lo_done[0], 1)
                    if k == 0:
                        split_m(0, 0)
                pool.wait_ge(rows_ld, 16 * 7)

                def step(c, slot, s, cur, prev, old):
                    i = 2 * c + slot
                    if cur:
                        if s == 0:
                            split_m(i + 1, 1 - slot)
                        for u in range(2):
                            pool.wait_ge(scaled, 2 * i + u + 1)
                            pool.tensor_tensor(h[:, u], h[:, u], shift[:, s], ALU.add).then_inc(h_done, 1)
                pipeline(pool, step)

            @block.vector
            def _(dve):
                for k in range(1, KD, 2):
                    dve.wait_ge(w_hi_done, k + 1)
                    dve.tensor_tensor(w_lo[:, k], wraw[:, 1], w_hi[:, k].bitcast(F32), ALU.subtract
                                      ).then_inc(w_lo_done[1], 1)
                dve.wait_ge(rows_ld, 16 * 7)
                for s in range(2):
                    dve.scalar_tensor_tensor(out=gain[:, s], in0=gain[:, s], scalar=1.0, in1=norm[:],
                                             op0=ALU.add, op1=ALU.mult).then_inc(gain_done, 1)
                dve.wait_ge(gain_done, 2)

                def step(c, slot, s, cur, prev, old):
                    i = 2 * c + slot
                    for u in range(2):
                        j = 2 * i + u
                        if cur:
                            dve.wait_ge(mm_done, j + 1)
                            wait(dve, x2_st[u], 16 * i)
                            dve.tensor_tensor(y[:, u], po[:, u], gate[:, s], ALU.mult).then_inc(gated, 1)
                            dve.wait_ge(gated, j + 1)
                            dve.wait_ge(x_ld[u], 16 * i + 16)
                            dve.tensor_tensor(y[:, u], y[:, u], x[:, u], ALU.add).then_inc(x2_done, 1)
                        if old and u == 0:
                            dve.wait_ge(lg_done, i - 1)
                            dve.tensor_reduce(top[:], lg[:], AX.X, ALU.max, negate=True).then_inc(top_done, 1)
                        if cur:
                            dve.wait_ge(sq_done, j + 1)
                            dve.tensor_scalar(meansq[:, u:u + 1], sumsq[:, u:u + 1], 1.0 / D, EPS, ALU.mult, ALU.add
                                              ).then_inc(ms_done, 1)
                            dve.wait_ge(root_done, j + 1)
                            dve.reciprocal(rstd[:, u:u + 1], root[:, u:u + 1]).then_inc(rstd_done, 1)
                            dve.wait_ge(rstd_done, j + 1)
                            dve.scalar_tensor_tensor(out=h[:, u], in0=y[:, u], scalar=rstd[:, u:u + 1], in1=gain[:, s],
                                                     op0=ALU.mult, op1=ALU.mult).then_inc(scaled, 1)
                        if old and u == 0:
                            dve.wait_ge(ex_done, 2 * i - 2)
                            wait(dve, aff_done, 2 * i - 4)
                            dve.reciprocal(einv[:], esum[:]).then_inc(einv_done, 1)
                            dve.wait_ge(einv_done, i - 1)
                            wait(dve, at_done, i - 2)
                            for v in range(2):
                                dve.tensor_scalar(aff[:, v], ex[:, v], einv[:, v:v + 1], None, ALU.mult).then_inc(aff_done, 1)
                pipeline(dve, step)

            @block.tensor
            def _(pe):
                def step(c, slot, s, cur, prev, old):
                    i = 2 * c + slot
                    for u in range(2):
                        j = 2 * i + u
                        if cur:
                            wait(pe, gated, j - 1)
                            pe.wait_ge(m_lo_done, i + 1)
                            for k in range(KD):
                                if isinstance(i, int) and i == 0 and u == 0:
                                    pe.wait_ge(w_lo_done[k % 2], k // 2 + 1)
                                for m, w in ((m_hi, w_hi), (m_hi, w_lo), (m_lo, w_hi)):
                                    for n in range(2):
                                        mm = pe.matmul(po[:, u, n * BLK:(n + 1) * BLK], m[:, slot, k, u * P:(u + 1) * P],
                                                       w[:, k, n * BLK:(n + 1) * BLK],
                                                       start=(k == 0 and m is m_hi and w is w_hi),
                                                       stop=(k == KD - 1 and m is m_lo))
                            mm.then_inc(mm_done, 1)
                        if old and u == 0:
                            if not isinstance(i, int) or i > 2:
                                pe.wait_ge(ex_done, 2 * i - 4)
                            pe.wait_ge(hT_done, 2 * i - 2)
                            for v in range(2):
                                for k in range(KD):
                                    mm = pe.matmul(lg[:, v], hT[:, v, k], w_r[:, k], start=(k == 0), stop=(k == KD - 1),
                                                   skip_group_check=True)
                            mm.then_inc(lg_done, 1)
                        if prev:
                            jp = 2 * (i - 1) + u
                            pe.wait_ge(h_done, jp + 1)
                            wait(pe, hT_done, jp)
                            for k in range(KD):
                                mm = pe.transpose(tp[:, k * P:(k + 1) * P], h[:, u, k * P:(k + 1) * P], ident[:])
                            mm.then_inc(tp_done, 1)
                    if old:
                        pe.wait_ge(aff_done, 2 * i - 2)
                        wait(pe, affT_done, i - 2)
                        for v in range(2):
                            mm = pe.transpose(at[:, v], aff[:, v], ident[:])
                        mm.then_inc(at_done, 1)
                pe.wait_ge(wr_ld, 16)
                pipeline(pe, step)


def topk_phase(nc, t, affT, idx, val, ident):
    with ExitStack() as ctx:
        p = Scope(nc, ctx, "tk")
        top = p.sb("top", [E, CAP + CAPP])
        at = p.sb("at", [E, CAP + CAPP], U32)
        atf = p.sb("atf", [E, CAP + CAPP])
        tp = p.ps("tp", [P, 2, 3, E])
        max_done, at_done, cut_done = p.sem("max_done"), p.sem("at_done"), p.sem("cut_done")
        atf_done, tp_done, out_done = p.sem("atf_done"), p.sem("tp_done"), p.sem("out_done")
        ROUNDS = (CAP + CAPP) // 8
        SLICES = ((0, P), (P, P), (CAP, CAPP))
        with nc.Block() as block:
            @block.vector
            def _(dve):
                dve.memset(idx[:].bitcast(F32), 0.0).then_inc(out_done, 1)
                dve.memset(val[:], 0.0).then_inc(out_done, 1)
                for r in range(ROUNDS):
                    slot = slice(8 * r, 8 * r + 8)
                    aff = affT[:, 0:S] if r < CAP // 8 else affT[:, S:T]
                    wait(dve, cut_done, r)
                    dve.max(top[:, slot], aff).then_inc(max_done, 1)
                    dve.wait_ge(max_done, r + 1)
                    dve.max_index(at[:, slot], top[:, slot], aff).then_inc(at_done, 1)
                    dve.wait_ge(at_done, r + 1)
                    dve.match_replace(aff, top[:, slot], aff, -1.0).then_inc(cut_done, 1)
                dve.tensor_copy(atf[:, 0:CAP], at[:, 0:CAP]).then_inc(atf_done, 1)
                dve.tensor_scalar(atf[:, CAP:], at[:, CAP:], 1.0, float(S), ALU.mult, ALU.add).then_inc(atf_done, 1)
                dve.wait_ge(tp_done, 1)
                dve.wait_ge(out_done, 2)
                for src, dst in ((0, val), (1, idx)):
                    for i, (_, n) in enumerate(SLICES):
                        dve.tensor_copy(dst[0:n, :, i], tp[0:n, src, i]).then_inc(out_done, 1)

            @block.tensor
            def _(pe):
                pe.wait_ge(atf_done, 2)
                for src, rows in enumerate((top, atf)):
                    for i, (at0, n) in enumerate(SLICES):
                        mm = pe.transpose(tp[0:n, src, i], rows[:, at0:at0 + n], ident[0:E, 0:E])
                mm.then_inc(tp_done, 1)


def moe_phase(nc, t, idx, val, ident):
    TOK = CAP + CAPP
    TOKP = 3 * P
    M = FF // P
    SL = ((0, P), (P, P), (CAP, CAPP))
    with ExitStack() as ctx:
        p = Scope(nc, ctx, "moe")
        raw_gu, raw_d = p.sb("raw_gu", [P, 2, 2, KD, P]), p.sb("raw_d", [P, 2, D])
        gu_hi, gu_lo = p.sb("gu_hi", [P, 2, 2, KD, P], F32R), p.sb("gu_lo", [P, 2, 2, KD, P], F32R)
        d_hi, d_lo = p.sb("d_hi", [P, 2, D], F32R), p.sb("d_lo", [P, 2, D], F32R)
        xg = p.sb("xg", [P, 3, D])
        x_hi, x_lo = p.sb("x_hi", [P, 2, KD, TOK], F32R), p.sb("x_lo", [P, 2, KD, TOK], F32R)
        act_g, hid = p.sb("act_g", [P, TOK]), p.sb("hid", [P, TOK])
        h_hi, h_lo = p.sb("h_hi", [P, 2, TOKP], F32R), p.sb("h_lo", [P, 2, TOKP], F32R)
        yo = p.sb("yo", [P, 3, D])
        gate = p.sb("gate", [P, 2, D])
        idx_g, idx_s = p.sb("idx_g", [P, 2, 3], U32), p.sb("idx_s", [P, 2, 3], U32)
        val_s = p.sb("val_s", [P, 2, 3])
        bank = [p.ps("g", [P, BLK]), p.ps("u", [P, BLK])]
        py = p.ps("py", [P, 3, D])
        gate_ld = p.sem("gate_ld")
        gu_ld, d_ld = p.sems("gu_ld", 2), p.sems("d_ld", 2)
        ghi_done, glo_done, dhi_done, dlo_done = (p.sem(n) for n in ("ghi_done", "glo_done", "dhi_done", "dlo_done"))
        pick_done, pick_s_done, xg_ld, y_st = p.sem("pick_done"), p.sem("pick_s_done"), p.sems("xg_ld", 3), p.sems("y_st", 3)
        tp_done, xhi_done, xlo_done = p.sem("tp_done"), p.sem("xhi_done"), p.sem("xlo_done")
        g_mm, u_mm, d_mm = p.sem("g_mm"), p.sem("u_mm"), p.sem("d_mm")
        silu_done, hid_done, hhi_done, hlo_done, y_done = (
            p.sem(n) for n in ("silu_done", "hid_done", "hhi_done", "hlo_done", "y_done"))
        zero_done, may_issue = p.sem("zero_done"), p.sem("may_issue")

        def pairs(eng, body):
            for u in range(2):
                body(u, u, u == 0, False)
            with eng.Fori(1, E // 2 - 1) as i:
                for u in range(2):
                    body(2 * i + u, u, False, False)
            for u in range(2):
                body(E - 2 + u, u, False, u == 1)

        with nc.Block() as block:
            @block.sync
            def _(sp):
                for s in range(2):
                    sp.dma_start(gate[:, s], t["mod"][s, 5 * D:6 * D].partition_broadcast(P)).then_inc(gate_ld, 16)

                def load(e, u, first, last):
                    for m in range(M):
                        q = M * e + m
                        if not (first and m < 2):
                            sp.wait_ge(glo_done, q - 1)
                        sp.dma_start(raw_gu[:, m % 2], t["w_gate_up"][bass.ds(q, 1)].rearrange("o p g k n -> (o p) g k n")
                                     ).then_inc(gu_ld[m % 2], 16)
                        if not (first and m < 2):
                            sp.wait_ge(dlo_done, q - 1)
                        sp.dma_start(raw_d[:, m % 2], t["w_down"][bass.ds(q * P, P), :]).then_inc(d_ld[m % 2], 16)
                pairs(sp, load)

            @block.gpsimd
            def _(pool):
                def gather(e, u):
                    pool.wait_ge(pick_done, e + 1)
                    pool.sem_inc(may_issue, 1)
                    for i, (_, n) in enumerate(SL):
                        pool.indirect_dma_start(xg[0:n, i], None, t["h2"], bass.IndirectOffsetOnAxis(ap=idx_g[0:n, u, i:i + 1], axis=0)
                                                ).then_inc(xg_ld[i], 16)

                def scatter(e, u):
                    pool.wait_ge(y_done, 3 * e + 3)
                    for i in range(3):
                        wait(pool, y_st[i], 16 * e)
                    pool.sem_inc(may_issue, 1)
                    for i, (_, n) in enumerate(SL):
                        pool.indirect_dma_start(t["x2"], bass.IndirectOffsetOnAxis(ap=idx_s[0:n, u, i:i + 1], axis=0),
                                                yo[0:n, i], None, compute_op=ALU.add).then_inc(y_st[i], 16)

                def split_gu(q, slot):
                    pool.wait_ge(ghi_done, q + 1)
                    pool.tensor_tensor(gu_lo[:, slot], raw_gu[:, slot], gu_hi[:, slot].bitcast(F32), ALU.subtract
                                       ).then_inc(glo_done, 1)

                gather(0, 0)
                for b in (h_hi, h_lo):
                    pool.memset(b[:, :, TOK:].bitcast(F32), 0.0).then_inc(zero_done, 1)
                split_gu(0, 0)

                def expert(e, u, first, last):
                    for m in range(M):
                        if m == 0 and not last:
                            pool.wait_ge(tp_done, 6 * e + 6)
                            gather(e + 1, 1 - u)
                        if not (last and m == M - 1):
                            split_gu(M * e + m + 1, (m + 1) % 2)
                        if m == 1 and not first:
                            scatter(e - 1, 1 - u)
                pairs(pool, expert)
                scatter(E - 1, 1)
                for i in range(3):
                    pool.wait_ge(y_st[i], 16 * E)

            @block.scalar
            def _(act):
                def split_gu(q, slot, half):
                    act.wait_ge(gu_ld[slot], 16 * half + 16)
                    wait(act, u_mm, q - 1)
                    act.activation(gu_hi[:, slot], raw_gu[:, slot], ACT.Copy).then_inc(ghi_done, 1)

                def x_hi_part(e, i, half, u):
                    n = SL[i][1]
                    act.wait_ge(tp_done, 6 * e + 2 * i + half + 1)
                    act.activation(x_hi[:, u, 4 * half:4 * half + 4, SL[i][0]:SL[i][0] + n],
                                   bank[half][:, 0:4 * n].rearrange("p (k n) -> p k n", k=4), ACT.Copy).then_inc(xhi_done, 1)

                for i in range(3):
                    for half in range(2):
                        x_hi_part(0, i, half, 0)
                split_gu(0, 0, 0)

                def expert(e, u, first, last):
                    for m in range(M):
                        q, slot = M * e + m, m % 2
                        if not (last and m == M - 1):
                            split_gu(q + 1, (m + 1) % 2, 2 * e + (m + 1) // 2)
                        act.wait_ge(d_ld[slot], 16 * (2 * e + m // 2) + 16)
                        if not (first and m < 2):
                            act.wait_ge(d_mm, q - 1)
                        act.activation(d_hi[:, slot], raw_d[:, slot], ACT.Copy).then_inc(dhi_done, 1)
                        act.wait_ge(g_mm, q + 1)
                        wait(act, hid_done, q)
                        act.activation(act_g[:], bank[0][:, 0:TOK], ACT.Silu).then_inc(silu_done, 1)
                        act.wait_ge(hid_done, q + 1)
                        act.activation(h_hi[:, slot, 0:TOK], hid[:], ACT.Copy).then_inc(hhi_done, 1)
                        if m > 0 and not last:
                            x_hi_part(e + 1, m - 1, 0, 1 - u)
                            x_hi_part(e + 1, m - 1, 1, 1 - u)
                pairs(act, expert)

            @block.vector
            def _(dve):
                def pick(e, u):
                    dve.wait_ge(gate_ld, 32)
                    for i in range(3):
                        wait(dve, xg_ld[i], 16 * (e - 1))
                    dve.tensor_copy(idx_g[:, u], idx[:, bass.ds(e, 1), :].rearrange("p o i -> p (o i)")
                                    ).then_inc(pick_done, 1)

                def pick_s(e, u):
                    dve.wait_ge(gate_ld, 32)
                    for i in range(3):
                        wait(dve, y_st[i], 16 * (e - 1))
                    for dst, src in ((idx_s, idx), (val_s, val)):
                        dve.tensor_copy(dst[:, u], src[:, bass.ds(e, 1), :].rearrange("p o i -> p (o i)")
                                        ).then_inc(pick_s_done, 1)

                def x_lo_part(e, i, half, u):
                    at0, n = SL[i]
                    dve.wait_ge(xhi_done, 6 * e + 2 * i + half + 1)
                    part = (slice(None), u, slice(4 * half, 4 * half + 4), slice(at0, at0 + n))
                    dve.tensor_tensor(x_lo[part], bank[half][:, 0:4 * n].rearrange("p (k n) -> p k n", k=4),
                                      x_hi[part].bitcast(F32), ALU.subtract).then_inc(xlo_done, 1)

                def scale_y(e, u):
                    dve.wait_ge(d_mm, M * e + M)
                    dve.wait_ge(pick_s_done, 2 * e + 2)
                    for i, (_, n) in enumerate(SL):
                        wait(dve, y_st[i], 16 * e)
                        dve.scalar_tensor_tensor(out=yo[0:n, i], in0=py[0:n, i], scalar=val_s[0:n, u, i:i + 1],
                                                 in1=gate[0:n, i // 2], op0=ALU.mult, op1=ALU.mult).then_inc(y_done, 1)

                pick(0, 0)
                for i in range(3):
                    for half in range(2):
                        x_lo_part(0, i, half, 0)
                dve.wait_ge(gate_ld, 32)

                def expert(e, u, first, last):
                    for m in range(M):
                        q, slot = M * e + m, m % 2
                        if m == 0 and not last:
                            pick(e + 1, 1 - u)
                        if m == 1:
                            pick_s(e, u)
                        dve.wait_ge(dhi_done, q + 1)
                        dve.tensor_tensor(d_lo[:, slot], raw_d[:, slot], d_hi[:, slot].bitcast(F32), ALU.subtract
                                          ).then_inc(dlo_done, 1)
                        dve.wait_ge(silu_done, q + 1)
                        dve.wait_ge(u_mm, q + 1)
                        wait(dve, hhi_done, q)
                        wait(dve, hlo_done, q)
                        dve.tensor_tensor(hid[:], bank[1][:, 0:TOK], act_g[:], ALU.mult).then_inc(hid_done, 1)
                        dve.wait_ge(hhi_done, q + 1)
                        dve.tensor_tensor(h_lo[:, slot, 0:TOK], hid[:], h_hi[:, slot, 0:TOK].bitcast(F32), ALU.subtract
                                          ).then_inc(hlo_done, 1)
                        if m == 0 and not first:
                            scale_y(e - 1, 1 - u)
                        if m > 0 and not last:
                            x_lo_part(e + 1, m - 1, 0, 1 - u)
                            x_lo_part(e + 1, m - 1, 1, 1 - u)
                pairs(dve, expert)
                scale_y(E - 1, 1)

            @block.tensor
            def _(pe):
                def turn(e, i, half, u):
                    n = SL[i][1]
                    for k in range(4):
                        at0 = (4 * half + k) * P
                        mm = pe.transpose(bank[half][:, k * n:(k + 1) * n], xg[0:n, i, at0:at0 + P], ident[0:n, 0:n])
                    mm.then_inc(tp_done, 1)

                def down(q, slot, first_piece, last_piece, part):
                    for i in part:
                        for h, w in ((h_hi, d_hi), (h_hi, d_lo), (h_lo, d_hi)):
                            for n in range(2):
                                mm = pe.matmul(py[:, i, n * BLK:(n + 1) * BLK], h[:, slot, i * P:(i + 1) * P],
                                               w[:, slot, n * BLK:(n + 1) * BLK],
                                               start=(first_piece and h is h_hi and w is d_hi),
                                               stop=(last_piece and h is h_lo))
                    if part[-1] == 2:
                        mm.then_inc(d_mm, 1)

                pe.wait_ge(zero_done, 2)
                for i in range(3):
                    pe.wait_ge(xg_ld[i], 16)
                    for half in range(2):
                        wait(pe, xlo_done, 2 * i + half - 1)
                        turn(0, i, half, 0)

                def expert(e, u, first, last):
                    for m in range(M):
                        q, slot = M * e + m, m % 2
                        pe.wait_ge(glo_done, q + 1)
                        for g in range(2):
                            if m == 0:
                                pe.wait_ge(xlo_done, 6 * e + 6)
                            elif m > 1 and not last:
                                pe.wait_ge(xlo_done, 6 * e + 6 + 2 * (m - 1) - 1 + g)
                            wait(pe, (silu_done, hid_done)[g], q)
                            for k in range(KD):
                                for w, x in ((gu_hi, x_hi), (gu_lo, x_hi), (gu_hi, x_lo)):
                                    mm = pe.matmul(bank[g][:, 0:TOK], w[:, slot, g, k], x[:, u, k],
                                                   start=(k == 0 and w is gu_hi and x is x_hi),
                                                   stop=(k == KD - 1 and x is x_lo))
                            mm.then_inc((g_mm, u_mm)[g], 1)
                        if m > 0 and not last:
                            pe.wait_ge(zero_done, 2)
                            pe.wait_ge(silu_done, q + 1)
                            pe.wait_ge(xg_ld[m - 1], 16 * e + 32)
                            turn(e + 1, m - 1, 0, 1 - u)
                        if not (first and m == 0):
                            pe.wait_ge(hlo_done, q)
                            pe.wait_ge(dlo_done, q)
                            if m == 1 and not first:
                                pe.wait_ge(y_done, 3 * e)
                            down(q - 1, 1 - slot, m == 1, m == 0, (0, 1))
                        if m > 0 and not last:
                            pe.wait_ge(zero_done, 2)
                            pe.wait_ge(hid_done, q + 1)
                            turn(e + 1, m - 1, 1, 1 - u)
                        if not (first and m == 0):
                            down(q - 1, 1 - slot, m == 1, m == 0, (2,))
                pairs(pe, expert)
                pe.wait_ge(hlo_done, M * E)
                pe.wait_ge(dlo_done, M * E)
                down(M * E - 1, 1, False, True, (0, 1, 2))


def final_phase(nc, t):
    U = 6
    with ExitStack() as ctx:
        p = Scope(nc, ctx, "fin")
        x, sq, y = p.sb("x", [P, U, D]), p.sb("sq", [P, 2, D]), p.sb("y", [P, U, D])
        norm = p.sb("norm", [P, D])
        sumsq, meansq, root, rstd = (p.sb(n, [P, U]) for n in ("sumsq", "meansq", "root", "rstd"))
        x_ld, y_st, norm_ld = p.sems("x_ld", U), p.sems("y_st", U), p.sem("norm_ld")
        sq_done, ms_done, root_done, rstd_done, y_done = (
            p.sem(n) for n in ("sq_done", "ms_done", "root_done", "rstd_done", "y_done"))
        N = T // P // U
        with nc.Block() as block:
            @block.sync
            def _(sp):
                sp.dma_start(norm[:], t["final_norm"].partition_broadcast(P)).then_inc(norm_ld, 16)

                def load(i):
                    for u in range(U):
                        wait(sp, y_done, U * i + u - U + 1)
                        sp.dma_start(x[:, u], t["x2"][bass.ds((U * i + u) * P, P), :]).then_inc(x_ld[u], 16)
                steps(sp, N, load)

            @block.scalar
            def _(act):
                def body(i):
                    for u in range(U):
                        j = U * i + u
                        act.wait_ge(x_ld[u], 16 * i + 16)
                        wait(act, sq_done, j - 1)
                        act.activation(sq[:, u % 2], x[:, u], ACT.Square, accum_out=sumsq[:, u:u + 1]).then_inc(sq_done, 1)
                        act.wait_ge(ms_done, j + 1)
                        act.activation(root[:, u:u + 1], meansq[:, u:u + 1], ACT.Sqrt).then_inc(root_done, 1)
                steps(act, N, body)

            @block.vector
            def _(dve):
                dve.wait_ge(norm_ld, 16)

                def body(i):
                    for u in range(U):
                        j = U * i + u
                        dve.wait_ge(sq_done, j + 1)
                        dve.tensor_scalar(meansq[:, u:u + 1], sumsq[:, u:u + 1], 1.0 / D, EPS, ALU.mult, ALU.add
                                          ).then_inc(ms_done, 1)
                        dve.wait_ge(root_done, j + 1)
                        dve.reciprocal(rstd[:, u:u + 1], root[:, u:u + 1]).then_inc(rstd_done, 1)
                        dve.wait_ge(rstd_done, j + 1)
                        wait(dve, y_st[u], 16 * i)
                        dve.scalar_tensor_tensor(out=y[:, u], in0=x[:, u], scalar=rstd[:, u:u + 1], in1=norm[:],
                                                 op0=ALU.mult, op1=ALU.mult).then_inc(y_done, 1)
                steps(dve, N, body)

            @block.gpsimd
            def _(pool):
                def store(i):
                    for u in range(U):
                        pool.wait_ge(y_done, U * i + u + 1)
                        pool.dma_start(t["y"][bass.ds((U * i + u) * P, P), :], y[:, u]).then_inc(y_st[u], 16)
                steps(pool, N, store)
                for u in range(U):
                    pool.wait_ge(y_st[u], 16 * N)


def program(nc, t, upto=99):
    with ExitStack() as ctx:
        ident = ctx.enter_context(nc.sbuf_tensor("identity", [P, P], F32))
        ada_phase(nc, t)
        with ExitStack() as hold:
            hT_hi = hold.enter_context(nc.sbuf_tensor("hT_hi", [P, KD, T], F32R))
            hT_lo = hold.enter_context(nc.sbuf_tensor("hT_lo", [P, KD, T], F32R))
            norm1_phase(nc, t, hT_hi, hT_lo, ident)
            if upto <= 1: return
            in_proj_phase(nc, t, hT_hi, hT_lo)
        if upto <= 2: return
        with ExitStack() as hold:
            V = hold.enter_context(nc.sbuf_tensor("V", [P, H, KEYS // P, DV], F32))
            latents_phase(nc, t, V)
            if upto <= 3: return
            attention_phase(nc, t, V, ident)
        if upto <= 4: return
        mix_phase(nc, t)
        affT = ctx.enter_context(nc.sbuf_tensor("affT", [E, T], F32))
        out_phase(nc, t, affT, ident)
        if upto <= 5: return
        idx = ctx.enter_context(nc.sbuf_tensor("idx", [P, E, 3], U32))
        val = ctx.enter_context(nc.sbuf_tensor("val", [P, E, 3], F32))
        topk_phase(nc, t, affT, idx, val, ident)
        if upto <= 6: return
        moe_phase(nc, t, idx, val, ident)
        if upto <= 7: return
        final_phase(nc, t)


SCRATCH = {
    "mod": [2, ADA], "gates": [2 * D, T], "misc": [4 * P, T], "conv": [CONV, T],
    "q": [H, HQ, T], "k": [H, NOPE, KEYS], "kpe": [ROPE, KEYS], "o": [H * DV, T],
    "sums": [H, T], "inverse": [H, T], "mixed": [D, T], "x2": [T, D], "h2": [T, D],
}


def rotary_constants():
    half = ROPE // 2
    freq = np.float32(10000.0) ** (-np.arange(0, half, 2, dtype=np.float32) / np.float32(half))
    n = np.arange(S)
    at = np.stack([n // 64, n % 64]).astype(np.float32)
    d = np.arange(ROPE)
    angle = at[d // half] * freq[d % (half // 2)][:, None]
    perm = np.zeros((ROPE, ROPE), np.float32)
    first = d % half < half // 2
    perm[d[first] + half // 2, d[first]] = -1.0
    perm[d[~first] - half // 2, d[~first]] = 1.0
    perm = np.concatenate([np.zeros((ROPE, NOPE), np.float32), perm], 1)
    return np.cos(angle), np.sin(angle), perm


def laid_out(i):
    w_in = i["w_in"][0].reshape(KD, P, -1)

    def cols(at):
        return w_in[:, :, at:at + P].transpose(1, 0, 2)
    QA = 2 * CONV
    GATE = QA + QL + KVL + ROPE
    tiles = []
    for c in range(CT):
        tiles += [cols(c * P), cols(CONV + c * P)]
        tiles += [cols(GATE + (4 * c + g) * P) for g in range(4)]
        tiles += [cols(QA + c * P)]
    w_qb = i["w_qb"][0].reshape(2, P, H, HQ).transpose(1, 2, 0, 3).reshape(P, H, 2 * HQ)
    w_kvb = i["w_kvb"][0].reshape(P, H, NOPE + DV)
    cos, sin, perm = rotary_constants()
    w_gate_up = np.stack([i["w_e_gate"][0], i["w_e_up"][0]]).reshape(2, E, KD, P, FF // P, P)
    w_gate_up = w_gate_up.transpose(1, 4, 3, 0, 2, 5).reshape(E * FF // P, P, 2, KD, P)
    a = {
        "cache_ckv": i["cache_ckv"][0, 0].T, "cache_kpe": i["cache_kpe"][0, 0].T,
        "latent_norms": np.concatenate([i["q_norm"][0], i["kv_norm"][0]]).reshape(3, P).T,
        "cos": cos, "sin": sin, "perm": perm,
        "w_head": np.concatenate([w_qb, w_kvb], -1),
        "conv_norm": np.stack([i["conv_ln_g"][0], i["conv_ln_b"][0]]).reshape(2, CT, P).transpose(2, 0, 1),
        "w_conv_out": i["w_conv_out"][0].reshape(CT, P, D).transpose(1, 0, 2),
        "w_o": i["w_o_mla"][0].reshape(CT, P, D).transpose(1, 0, 2),
        "w_out": i["w_out"][0], "norm2": i["norm2"][0],
        "w_router": i["w_router"][0].reshape(KD, P, E).transpose(1, 0, 2),
        "w_v": w_kvb[:, :, NOPE:].reshape(P, H * DV),
        "x": np.concatenate([i["x_sample"][0], i["x_prompt"][0]]),
        "cond": np.stack([i["c"][0], i["c_ctx"]], -1).reshape(KD, P, 2).transpose(1, 0, 2),
        "w_ada": i["w_ada"][0].reshape(KD, P, ADA // 512, 512).transpose(2, 1, 0, 3),
        "b_ada": i["b_ada"][0],
        "norm1": i["norm1"][0],
        "w_in": np.stack(tiles),
        "conv_dw": np.concatenate([i["conv_dw"][0], i["conv_dw_b"]]).reshape(TAPS + 1, CT, P).transpose(2, 1, 0),
        "w_gate_up": w_gate_up, "w_down": i["w_e_down"][0].reshape(E * FF, D), "final_norm": i["final_norm"],
        "ident": np.eye(P, dtype=np.float32),
    }
    return {k: np.ascontiguousarray(v) for k, v in a.items()}


OUTS = {"y": [T, D], "new_ckv": [KVL, PR], "new_kpe": [ROPE, PR]}


def declare(nc, arrays):
    t = {}
    for k, a in arrays.items():
        t[k] = nc.dram_tensor(k, list(a.shape), mybir.dt.from_np(a.dtype), kind="ExternalInput").ap()
    for k, shape in SCRATCH.items():
        t[k] = nc.dram_tensor(f"{k}_scratch", shape, F32, kind="Internal").ap()
    for k, shape in OUTS.items():
        t[k] = nc.dram_tensor(k, shape, F32, kind="ExternalOutput").ap()
    return t


def kernel(**inputs):
    from concourse import bacc
    from concourse.bass_utils import run_bass_kernel_spmd

    arrays = laid_out({k: np.asarray(v) for k, v in inputs.items()})
    nc = bacc.Bacc("TRN2", target_bir_lowering=False, num_devices=1)
    program(nc, declare(nc, arrays))
    got = run_bass_kernel_spmd(nc, [arrays], core_ids=[0]).results[0]
    y = np.asarray(got["y"])
    return (y[S:].reshape(1, PR, D), y[:S].reshape(1, S, D),
            np.ascontiguousarray(np.asarray(got["new_ckv"]).T).reshape(1, 1, PR, KVL),
            np.ascontiguousarray(np.asarray(got["new_kpe"]).T).reshape(1, 1, PR, ROPE))
```

```python
from contextlib import ExitStack

import numpy as np

import concourse.bass as bass
from concourse import mybir

F32 = mybir.dt.float32
F32R = mybir.dt.float32r
U32 = mybir.dt.uint32
ACT = mybir.ActivationFunctionType
ALU = mybir.AluOpType
AX = mybir.AxisListType

P = 128
D = 1024
KD = D // P
S = 2048
PR = 256
T = S + PR
PAST = 256
KEYS = PAST + T
BLK = 512
NB = S // BLK
BLOCKS = [(b * BLK, BLK) for b in range(NB)] + [(S, PR)]
CONV = 512
CT = CONV // P
TAPS = 31
PAD = TAPS // 2
H = 8
NOPE, ROPE, DV = 64, 32, 64
HQ = NOPE + ROPE
QL, KVL = 256, 128
E = 16
FF = 512
CAP = 2 * S // E
CAPP = 2 * PR // E
EPS = 1e-6
ADA = 6 * D
ADA_CH = 512
ADA_FIRST = 2 * D // ADA_CH
SM_SCALE = float(HQ) ** -0.5


def wait(eng, sem, value):
    if not isinstance(value, int) or value > 0:
        eng.wait_ge(sem, value)


def steps(eng, count, body):
    body(0)
    if count > 1:
        with eng.Fori(1, count) as i:
            body(i)


class Scope:

    def __init__(self, nc, ctx, tag):
        self.nc, self.ctx, self.tag, self.numbers = nc, ctx, tag, []
        ctx.callback(self.zero_sems)

    def sb(self, name, shape, dt=F32):
        return self.ctx.enter_context(self.nc.sbuf_tensor(f"{self.tag}_{name}", shape, dt))

    def ps(self, name, shape):
        return self.ctx.enter_context(self.nc.psum_tensor(f"{self.tag}_{name}", shape, F32))

    def sem(self, name):
        sem = self.ctx.enter_context(self.nc.semaphore(f"{self.tag}_{name}"))
        self.numbers.append(sem.num)
        return sem

    def sems(self, name, n):
        return [self.sem(f"{name}{k}") for k in range(n)]

    def zero_sems(self):
        runs = []
        for n in sorted(self.numbers):
            if runs and runs[-1][-1] == n - 1:
                runs[-1].append(n)
            else:
                runs.append([n])
        with self.nc.Block() as block:
            @block.gpsimd
            def _(pool):
                for run in runs:
                    pool.sem_clear(range(run[0], run[-1] + 1))


def ada_phase(nc, t, silu):
    U = ADA_FIRST
    N = U * ADA_CH
    with ExitStack() as ctx:
        p = Scope(nc, ctx, "ada")
        cond = p.sb("cond", [P, KD, 2])
        sig = p.sb("sig", [P, KD, 2])
        w = p.sb("w", [P, U, KD, ADA_CH])
        bias = p.sb("bias", [2, N])
        mod = p.sb("mod", [2, N])
        acc = p.ps("acc", [P, U, ADA_CH])
        cond_ld, bias_ld, mod_st = p.sem("cond_ld"), p.sem("bias_ld"), p.sem("mod_st")
        w_ld = p.sems("w_ld", U)
        sig_done, silu_done = p.sem("sig_done"), p.sem("silu_done")
        chunk_done, mod_done = p.sem("chunk_done"), p.sem("mod_done")
        with nc.Block() as block:
            @block.sync
            def _(sp):
                sp.dma_start(cond[:], t["cond"]).then_inc(cond_ld, 16)
                sp.dma_start(bias[:], t["b_ada"][0:N].partition_broadcast(2)).then_inc(bias_ld, 16)
                for u in range(U):
                    sp.dma_start(w[:, u], t["w_ada"][u]).then_inc(w_ld[u], 16)
                sp.wait_ge(mod_done, U)
                sp.dma_start(t["mod"][:, 0:N], mod[:]).then_inc(mod_st, 16)
                sp.wait_ge(mod_st, 16)

            @block.scalar
            def _(act):
                act.wait_ge(cond_ld, 16)
                act.activation(sig[:], cond[:], ACT.Sigmoid).then_inc(sig_done, 1)

            @block.tensor
            def _(pe):
                pe.wait_ge(silu_done, 1)
                for u in range(U):
                    pe.wait_ge(w_ld[u], 16)
                    for k in range(KD):
                        mm = pe.matmul(acc[0:2, u, :], silu[:, k, :], w[:, u, k, :], start=(k == 0), stop=(k == KD - 1))
                    mm.then_inc(chunk_done, 1)

            @block.vector
            def _(dve):
                dve.wait_ge(sig_done, 1)
                dve.tensor_tensor(silu[:], cond[:], sig[:], ALU.mult).then_inc(silu_done, 1)
                dve.wait_ge(bias_ld, 16)
                for u in range(U):
                    dve.wait_ge(chunk_done, u + 1)
                    col = slice(u * ADA_CH, (u + 1) * ADA_CH)
                    dve.tensor_tensor(mod[:, col], acc[0:2, u, :], bias[:, col], ALU.add).then_inc(mod_done, 1)


def norm1_phase(nc, t, hT_hi, hT_lo, ident, silu, kept):
    with ExitStack() as ctx:
        p = Scope(nc, ctx, "n1")
        gain = p.sb("gain", [P, 2, D])
        shift = p.sb("shift", [P, 2, D])
        norm = p.sb("norm", [P, D])
        x = p.sb("x", [P, 2, D])
        h = p.sb("h", [P, 2, D])
        sumsq, meansq, root, rstd = (p.sb(n, [P, 2]) for n in ("sumsq", "meansq", "root", "rstd"))
        tp = p.ps("tp", [P, 2, D])
        KH = KD // 2
        w_mod = p.sb("w_mod", [P, 2, KH, ADA_CH])
        bias, mod = p.sb("bias", [2, ADA_CH]), p.sb("mod", [2, ADA_CH])
        acc = p.ps("acc", [P, ADA_CH])
        wm_ld = [kept.enter_context(nc.semaphore(f"n1_wm_ld{v}")) for v in range(2)]
        bias_ld = kept.enter_context(nc.semaphore("n1_bias_ld"))
        mod_st = kept.enter_context(nc.semaphore("n1_mod_st"))
        half_mm, mod_done = p.sem("half_mm"), p.sem("mod_done")
        rows_ld, ident_ld = p.sem("rows_ld"), p.sem("ident_ld")
        x_ld = p.sems("x_ld", 2)
        gain_done, sq_done, ms_done, root_done = (p.sem(n) for n in ("gain_done", "sq_done", "ms_done", "root_done"))
        rstd_done, scaled_done, h_done, tp_done = (p.sem(n) for n in ("rstd_done", "scaled_done", "h_done", "tp_done"))
        hi_done, lo_done = p.sem("hi_done"), p.sem("lo_done")
        PAIRS = T // P // 2

        def skewed(eng, front, back, chunk=None):
            chunk = chunk or (lambda i: None)
            front(0, 0)
            if back is None:
                chunk(0)
                with eng.Fori(1, PAIRS - 1) as i:
                    front(i, 0)
                    chunk(i)
                front(PAIRS - 1, 1)
                return
            front(1, 0)
            back(0)
            chunk(0)
            with eng.Fori(2, PAIRS - 1) as i:
                front(i, 0)
                back(i - 1)
                chunk(i - 1)
            front(PAIRS - 1, 1)
            chunk(PAIRS - 2)
            back(PAIRS - 2)
            back(PAIRS - 1)

        with nc.Block() as block:
            @block.sync
            def _(sp):
                sp.dma_start(ident[:], t["ident"]).then_inc(ident_ld, 16)
                for s in range(2):
                    sp.dma_start(gain[:, s], t["mod"][s, D:2 * D].partition_broadcast(P)).then_inc(rows_ld, 16)
                    sp.dma_start(shift[:, s], t["mod"][s, 0:D].partition_broadcast(P)).then_inc(rows_ld, 16)
                sp.dma_start(norm[:], t["norm1"].partition_broadcast(P)).then_inc(rows_ld, 16)

                def load(i, s):
                    for u in range(2):
                        wait(sp, scaled_done, 2 * i + u - 1)
                        sp.dma_start(x[:, u], t["x"][bass.ds((2 * i + u) * P, P), :]).then_inc(x_ld[u], 16)

                skewed(sp, load, None)

            @block.scalar
            def _(act):
                def front(i, s):
                    for u in range(2):
                        act.wait_ge(x_ld[u], 16 * i + 16)
                        wait(act, tp_done, 2 * i + u - 1)
                        act.activation(h[:, u], x[:, u], ACT.Square, accum_out=sumsq[:, u:u + 1]
                                       ).then_inc(sq_done, 1)
                    for u in range(2):
                        act.wait_ge(ms_done, 2 * i + u + 1)
                        act.activation(root[:, u:u + 1], meansq[:, u:u + 1], ACT.Sqrt).then_inc(root_done, 1)

                def back(i):
                    for u in range(2):
                        act.wait_ge(tp_done, 2 * i + u + 1)
                        act.activation(hT_hi[:, :, bass.ds((2 * i + u) * P, P)],
                                       tp[:, u].rearrange("p (k n) -> p k n", k=KD), ACT.Copy).then_inc(hi_done, 1)
                skewed(act, front, back)

            @block.vector
            def _(dve):
                dve.wait_ge(rows_ld, 16 * 5)
                for s in range(2):
                    dve.scalar_tensor_tensor(out=gain[:, s], in0=gain[:, s], scalar=1.0, in1=norm[:],
                                             op0=ALU.add, op1=ALU.mult).then_inc(gain_done, 1)

                def front(i, s):
                    for u in range(2):
                        dve.wait_ge(sq_done, 2 * i + u + 1)
                        dve.tensor_scalar(meansq[:, u:u + 1], sumsq[:, u:u + 1], 1.0 / D, EPS, ALU.mult, ALU.add
                                          ).then_inc(ms_done, 1)
                    dve.wait_ge(gain_done, 2)
                    for u in range(2):
                        dve.wait_ge(root_done, 2 * i + u + 1)
                        dve.reciprocal(rstd[:, u:u + 1], root[:, u:u + 1]).then_inc(rstd_done, 1)
                        dve.wait_ge(rstd_done, 2 * i + u + 1)
                        dve.scalar_tensor_tensor(out=h[:, u], in0=x[:, u], scalar=rstd[:, u:u + 1],
                                                 in1=gain[:, s], op0=ALU.mult, op1=ALU.mult
                                                 ).then_inc(scaled_done, 1)

                def back(i):
                    for u in range(2):
                        dve.wait_ge(hi_done, 2 * i + u + 1)
                        cols = bass.ds((2 * i + u) * P, P)
                        dve.tensor_tensor(hT_lo[:, :, cols], tp[:, u].rearrange("p (k n) -> p k n", k=KD),
                                          hT_hi[:, :, cols].bitcast(F32), ALU.subtract).then_inc(lo_done, 1)

                def add(i):
                    dve.wait_ge(half_mm, 2 * i + 2)
                    dve.wait_ge(bias_ld, 16 * i + 16)
                    wait(dve, mod_st, 16 * i)
                    dve.tensor_tensor(mod[:], acc[0:2, :], bias[:], ALU.add).then_inc(mod_done, 1)
                skewed(dve, front, back, add)

            @block.gpsimd
            def _(pool):
                pool.wait_ge(rows_ld, 16 * 5)

                def front(i, s):
                    for u in range(2):
                        pool.wait_ge(scaled_done, 2 * i + u + 1)
                        pool.tensor_tensor(h[:, u], h[:, u], shift[:, s], ALU.add).then_inc(h_done, 1)

                def store(i):
                    pool.wait_ge(mod_done, i + 1)
                    pool.dma_start(t["mod"][:, bass.ds((ADA_FIRST + i) * ADA_CH, ADA_CH)], mod[:]).then_inc(mod_st, 16)

                def load_chunk(i):
                    for v in range(2):
                        wait(pool, half_mm, 2 * i + v - 1)
                        pool.dma_start(w_mod[:, v], t["w_ada"][bass.ds(ADA_FIRST + i, 1), :, v * KH:(v + 1) * KH]
                                     .rearrange("o p k n -> (o p) k n")).then_inc(wm_ld[v], 16)
                    if not isinstance(i, int):
                        store(i - 1)
                    pool.dma_start(bias[:], t["b_ada"][bass.ds((ADA_FIRST + i) * ADA_CH, ADA_CH)].partition_broadcast(2)
                                 ).then_inc(bias_ld, 16)
                skewed(pool, front, None, load_chunk)
                store(PAIRS - 2)
                pool.wait_ge(mod_st, 16 * (PAIRS - 1))

            @block.tensor
            def _(pe):
                pe.wait_ge(ident_ld, 16)

                def front(i, s):
                    for u in range(2):
                        pe.wait_ge(h_done, 2 * i + u + 1)
                        wait(pe, lo_done, 2 * i + u - 1)
                        for k in range(KD):
                            mm = pe.transpose(tp[:, u, k * P:(k + 1) * P], h[:, u, k * P:(k + 1) * P], ident[:])
                        mm.then_inc(tp_done, 1)

                def chunk(i):
                    for v in range(2):
                        pe.wait_ge(wm_ld[v], 16 * i + 16)
                        wait(pe, mod_done, i)
                        for k in range(KH):
                            mm = pe.matmul(acc[0:2, :], silu[:, v * KH + k, :], w_mod[:, v, k, :],
                                           start=(v == 0 and k == 0), stop=(v == 1 and k == KH - 1))
                        mm.then_inc(half_mm, 1)
                skewed(pe, front, None, chunk)


def in_proj_phase(nc, t, hT_hi, hT_lo):
    J = 7
    OTHER = J - 2
    VS = S + 2 * PAD
    with ExitStack() as ctx:
        p = Scope(nc, ctx, "ip")
        raw = p.sb("raw", [P, 2, KD, P])
        w_hi, w_lo = p.sb("w_hi", [P, 2, KD, P], F32R), p.sb("w_lo", [P, 2, KD, P], F32R)
        sig = p.sb("sig", [P, 2, BLK])
        stage = p.sb("stage", [P, len(BLOCKS), BLK])
        v = p.sb("v", [P, VS + PR + 2 * PAD])
        conv = p.sb("conv", [P, T])
        dw = p.sb("dw", [P, CT, TAPS + 1])
        pa = p.ps("pa", [P, 2, BLK])
        pb = p.ps("pb", [P, BLK])
        po = p.ps("po", [P, len(BLOCKS), BLK])
        raw_ld = p.sems("raw_ld", 2)
        dw_ld, conv_st = p.sem("dw_ld"), p.sem("conv_st")
        stage_st = p.sems("stage_st", len(BLOCKS))
        hi_done, lo_done = p.sem("hi_done"), p.sem("lo_done")
        a_done, b_done, o_done = p.sem("a_done"), p.sem("b_done"), p.sem("o_done")
        sig_done, v_done, out_done = p.sem("sig_done"), p.sem("v_done"), p.sem("out_done")
        pad_done, taps_s, taps_p = p.sem("pad_done"), p.sem("taps_s"), p.sem("taps_p")
        NBL = len(BLOCKS)

        def slot(j):
            return j % 2

        def slot_free(c, j):
            return J * c + j - {0: 0, 1: 2}.get(j, 1)

        def products_over(c, j):
            if j < 2:
                return o_done, NBL * (OTHER * c - j)
            if j < 4:
                return (a_done, b_done)[j - 2], NBL * (c + 1)
            return o_done, NBL * (OTHER * c + j - 3)

        def passes(pe, out, s, tok, n):
            ops = [(w_hi, hT_hi), (w_lo, hT_hi), (w_hi, hT_lo)]
            for k in range(KD):
                for q, (w, h) in enumerate(ops):
                    mm = pe.matmul(out, w[:, s, k, :], h[:, k, tok:tok + n],
                                   start=(k == 0 and q == 0), stop=(k == KD - 1 and q == 2))
            return mm

        with nc.Block() as block:
            @block.sync
            def _(sp):
                sp.dma_start(dw[:], t["conv_dw"]).then_inc(dw_ld, 16)

                def load(c):
                    for j in range(J):
                        n = J * c + j
                        wait(sp, lo_done, slot_free(c, j))
                        sp.dma_start(raw[:, slot(j)], t["w_in"][bass.ds(n, 1)].rearrange("o p k m -> (o p) k m")
                                     ).then_inc(raw_ld[slot(j)], 16)
                steps(sp, CT, load)

            def raw_count(c, j):
                return (4 * c + j // 2 + 1) if slot(j) == 0 else (3 * c + j // 2 + 1)

            @block.scalar
            def _(act):
                def split(c, j):
                    act.wait_ge(raw_ld[slot(j)], 16 * raw_count(c, j))
                    used, count = products_over(c, j)
                    wait(act, used, count)
                    act.activation(w_hi[:, slot(j)], raw[:, slot(j)], ACT.Copy).then_inc(hi_done, 1)

                def store(c, j, b):
                    tok, n = BLOCKS[b]
                    act.wait_ge(out_done, NBL * (OTHER * c + j - 2) + b + 1)
                    if j < J - 1:
                        dst = t["gates"][bass.ds((4 * c + j - 2) * P, P), tok:tok + n]
                    else:
                        dst = t["misc"][bass.ds(c * P, P), tok:tok + n]
                    act.dma_start(dst, stage[:, b, 0:n]).then_inc(stage_st[b], 16)

                def body(c):
                    split(c, 0)
                    split(c, 1)
                    for b, (tok, n) in enumerate(BLOCKS):
                        q = NBL * c + b
                        act.wait_ge(b_done, q + 1)
                        wait(act, v_done, q if b == 0 else q - 1)
                        act.activation(sig[:, b % 2, 0:n], pb[:, 0:n], ACT.Sigmoid).then_inc(sig_done, 1)
                    split(c, 2)
                    split(c, 3)
                    for j in range(2, J):
                        func = ACT.Sigmoid if j < J - 1 else ACT.Copy
                        for b, (tok, n) in enumerate(BLOCKS):
                            tile = OTHER * c + j - 2
                            act.wait_ge(o_done, NBL * tile + b + 1)
                            wait(act, stage_st[b], 16 * tile)
                            act.activation(stage[:, b, 0:n], po[:, b, 0:n], func).then_inc(out_done, 1)
                            if b:
                                store(c, j, b - 1)
                        store(c, j, NBL - 1)
                        if j + 2 < J:
                            split(c, j + 2)
                    act.wait_ge(taps_s, TAPS * c + TAPS)
                    act.wait_ge(taps_p, TAPS * c + TAPS)
                    act.dma_start(t["conv"][bass.ds(c * P, P), :], conv[:]).then_inc(conv_st, 16)

                steps(act, CT, body)
                for b in range(NBL):
                    act.wait_ge(stage_st[b], 16 * OTHER * CT)
                act.wait_ge(conv_st, 16 * CT)

            @block.gpsimd
            def _(pool):
                def split(c):
                    for j in range(J):
                        pool.wait_ge(hi_done, J * c + j + 1)
                        pool.tensor_tensor(w_lo[:, slot(j)], raw[:, slot(j)], w_hi[:, slot(j)].bitcast(F32),
                                           ALU.subtract).then_inc(lo_done, 1)
                steps(pool, CT, split)

            @block.tensor
            def _(pe):
                def body(c):
                    pe.wait_ge(lo_done, J * c + 2)
                    for b, (tok, n) in enumerate(BLOCKS):
                        q = NBL * c + b
                        wait(pe, v_done, q if b == 0 else q - 1)
                        mm = passes(pe, pa[:, b % 2, 0:n], 0, tok, n)
                        mm.then_inc(a_done, 1)
                        wait(pe, sig_done, q)
                        mm = passes(pe, pb[:, 0:n], 1, tok, n)
                        mm.then_inc(b_done, 1)
                    for j in range(2, J):
                        pe.wait_ge(lo_done, J * c + j + 1)
                        for b, (tok, n) in enumerate(BLOCKS):
                            tile = OTHER * c + j - 2
                            wait(pe, out_done, NBL * (tile - 1) + b + 1)
                            mm = passes(pe, po[:, b, 0:n], slot(j), tok, n)
                            mm.then_inc(o_done, 1)
                steps(pe, CT, body)

            @block.vector
            def _(dve):
                dve.memset(v[:], 0.0).then_inc(pad_done, 1)
                dve.wait_ge(pad_done, 1)
                dve.wait_ge(dw_ld, 16)
                segs = [(0, 0, S, taps_s), (VS, S, PR, taps_p)]

                def body(c):
                    for _, _, _, taps in segs:
                        wait(dve, taps, TAPS * c)
                    for b, (tok, n) in enumerate(BLOCKS):
                        q = NBL * c + b
                        at = PAD + tok if b < NB else VS + PAD
                        dve.wait_ge(a_done, q + 1)
                        dve.wait_ge(sig_done, q + 1)
                        dve.tensor_tensor(v[:, at:at + n], pa[:, b % 2, 0:n], sig[:, b % 2, 0:n], ALU.mult
                                          ).then_inc(v_done, 1)
                    dve.wait_ge(v_done, NBL * c + NBL)
                    wait(dve, conv_st, 16 * c)
                    def tap(w):
                        return dw[:, bass.ds(c, 1), w:w + 1].rearrange("p o w -> p (o w)")
                    for w in range(TAPS):
                        for at, tok, n, taps in segs:
                            out = conv[:, tok:tok + n]
                            if w == 0:
                                dve.tensor_scalar(out, v[:, at:at + n], tap(0), tap(TAPS), ALU.mult, ALU.add
                                                  ).then_inc(taps, 1)
                            else:
                                dve.wait_ge(taps, TAPS * c + w)
                                dve.scalar_tensor_tensor(out=out, in0=v[:, at + w:at + w + n], scalar=tap(w),
                                                         in1=out, op0=ALU.mult, op1=ALU.add).then_inc(taps, 1)
                steps(dve, CT, body)


def latents_phase(nc, t, V):
    KB = 5
    WH = 2 * HQ + P
    RO = slice(NOPE, HQ)
    NBL = len(BLOCKS)
    with ExitStack() as ctx:
        p = Scope(nc, ctx, "lt")
        qa = p.sb("qa", [P, 2, T])
        ckv = p.sb("ckv", [P, KEYS])
        kpe = p.sb("kpe", [HQ, KEYS])
        qn_hi, qn_lo = p.sb("qn_hi", [P, 2, T], F32R), p.sb("qn_lo", [P, 2, T], F32R)
        ckv_hi, ckv_lo = p.sb("ckv_hi", [P, KEYS], F32R), p.sb("ckv_lo", [P, KEYS], F32R)
        cos, sin = p.sb("cos", [HQ, S]), p.sb("sin", [HQ, S])
        wraw = p.sb("wraw", [P, H, WH])
        w_hi, w_lo = p.sb("w_hi", [P, 2, WH], F32R), p.sb("w_lo", [P, 2, WH], F32R)
        wv = p.sb("wv", [P, H * DV])
        wv_hi, wv_lo = p.sb("wv_hi", [P, H * DV], F32R), p.sb("wv_lo", [P, H * DV], F32R)
        stage_q = p.sb("stage_q", [P, NBL, BLK])
        stage_k = p.sb("stage_k", [P, KB, BLK])
        sq, root, rstd = stage_q[:, 0:3], stage_k[:, 0:2], stage_k[:, 2:4]
        turned = p.sb("turned", [HQ, 2, BLK])
        ones = p.sb("ones", [P, P])
        perm = p.sb("perm", [HQ, HQ])
        gain = p.sb("gain", [P, 3])
        eps = p.sb("eps", [P, 1])
        sums = p.ps("sums", [P, 2, BLK])
        pq = p.ps("pq", [P, 2, BLK])
        rot = p.ps("rot", [P, 2, BLK])
        pk = p.ps("pk", [P, 2, BLK])
        in_ld, w_ld, kpe_st = p.sem("in_ld"), p.sem("w_ld"), p.sem("kpe_st")
        const_done, sq_done, sums_done, root_done = (p.sem(n) for n in ("const_done", "sq_done", "sums_done", "root_done"))
        rstd_done, norm_done, hi_done, lo_done = (p.sem(n) for n in ("rstd_done", "norm_done", "hi_done", "lo_done"))
        v_mm, v_done, kr_mm, kr_rope = (p.sem(n) for n in ("v_mm", "v_done", "kr_mm", "kr_rope"))
        whi_done, wlo_done, q_mm, k_mm = (p.sem(n) for n in ("whi_done", "wlo_done", "q_mm", "k_mm"))
        q_done, k_done, rot_mm, rope_done = (p.sem(n) for n in ("q_done", "k_done", "rot_mm", "rope_done"))
        part_done = p.sem("part_done")
        q_st, k_st = p.sems("q_st", NBL), p.sems("k_st", KB)
        lat_ld = p.sem("lat_ld")
        IN = 7

        with nc.Block() as block:
            @block.sync
            def _(sp):
                sp.dma_start(qa[:], t["misc"][0:2 * P, :].rearrange("(k p) n -> p k n", p=P)).then_inc(lat_ld, 16)
                sp.dma_start(ckv[:, PAST:], t["misc"][2 * P:3 * P, :]).then_inc(lat_ld, 16)
                sp.dma_start(gain[:], t["latent_norms"]).then_inc(in_ld, 16)
                sp.dma_start(ckv[:, 0:PAST], t["cache_ckv"]).then_inc(in_ld, 16)
                sp.dma_start(kpe[RO, 0:PAST], t["cache_kpe"]).then_inc(in_ld, 16)
                sp.dma_start(kpe[RO, PAST:], t["misc"][3 * P:3 * P + ROPE, :]).then_inc(in_ld, 16)
                sp.dma_start(cos[RO, :], t["cos"]).then_inc(in_ld, 16)
                sp.dma_start(sin[RO, :], t["sin"]).then_inc(in_ld, 16)
                sp.dma_start(perm[RO, :], t["perm"]).then_inc(in_ld, 16)
                sp.dma_start(wv[:], t["w_v"]).then_inc(w_ld, 16)
                sp.dma_start(wraw[:], t["w_head"]).then_inc(w_ld, 16)
                sp.dma_start(t["new_kpe"], t["misc"][3 * P:3 * P + ROPE, S:]).then_inc(kpe_st, 16)
                sp.wait_ge(norm_done, 3 * NBL)
                sp.dma_start(t["new_ckv"], ckv[:, PAST + S:]).then_inc(kpe_st, 16)
                sp.wait_ge(kr_rope, NB)
                sp.dma_start(t["kpe"], kpe[RO, :]).then_inc(kpe_st, 16)

                def store(h):
                    for b, (tok, n) in enumerate(BLOCKS):
                        sp.wait_ge(k_done, KB * h + b + 1)
                        sp.dma_start(t["k"][bass.ds(h, 1), :, b * BLK:(b + 1) * BLK].rearrange("o p n -> (o p) n"),
                                     stage_k[0:NOPE, b]).then_inc(k_st[b], 16)
                        if b < NB:
                            sp.wait_ge(rope_done, NB * h + b + 1)
                        else:
                            sp.wait_ge(q_done, NBL * h + b + 1)
                        sp.dma_start(t["q"][bass.ds(h, 1), :, tok:tok + n].rearrange("o p n -> (o p) n"),
                                     stage_q[0:HQ, b, 0:n]).then_inc(q_st[b], 16)
                steps(sp, H, store)
                for st in q_st + k_st:
                    sp.wait_ge(st, 16 * H)
                sp.wait_ge(kpe_st, 48)

            @block.scalar
            def _(act):
                act.wait_ge(const_done, 2)
                def square(b):
                    tok, n = BLOCKS[b]
                    wait(act, sums_done, b)
                    act.activation(sq[:, 0:2, 0:n], qa[:, :, tok:tok + n], ACT.Square).then_inc(sq_done, 1)
                    act.activation(sq[:, 2, 0:n], ckv[:, PAST + tok:PAST + tok + n], ACT.Square).then_inc(sq_done, 1)

                act.wait_ge(lat_ld, 32)
                square(0)
                act.wait_ge(in_ld, 16 * IN)
                act.wait_ge(w_ld, 32)
                act.activation(wv_hi[:], wv[:], ACT.Copy).then_inc(hi_done, 1)
                for b, (tok, n) in enumerate(BLOCKS):
                    act.wait_ge(sums_done, b + 1)
                    wait(act, rstd_done, b)
                    act.activation(root[:, 0, 0:n], sums[:, 0, 0:n], ACT.Sqrt, scale=1.0 / QL, bias=eps[:]
                                   ).then_inc(root_done, 1)
                    act.activation(root[:, 1, 0:n], sums[:, 1, 0:n], ACT.Sqrt, scale=1.0 / KVL, bias=eps[:]
                                   ).then_inc(root_done, 1)
                    if b + 1 < NBL:
                        square(b + 1)
                    act.wait_ge(norm_done, 3 * b + 3)
                    act.activation(qn_hi[:, :, tok:tok + n], qa[:, :, tok:tok + n], ACT.Copy).then_inc(hi_done, 1)
                    at = 0 if b == 0 else PAST + tok
                    act.activation(ckv_hi[:, at:PAST + tok + n], ckv[:, at:PAST + tok + n], ACT.Copy
                                   ).then_inc(hi_done, 1)
                for k in range(KEYS // P):
                    act.wait_ge(v_mm, k + 1)
                    act.activation(V[:, :, k, :], pk[:, k % 2].rearrange("p (h d) -> p h d", h=H), ACT.Copy
                                   ).then_inc(v_done, 1)

                def heads(i):
                    for u in range(2):
                        h = 2 * i + u
                        wait(act, k_mm, KB * (h - 1))
                        act.activation(w_hi[:, u], wraw[:, bass.ds(h, 1)].rearrange("p o n -> p (o n)"), ACT.Copy
                                       ).then_inc(whi_done, 1)
                    for u in range(2):
                        h = 2 * i + u
                        for b, (tok, n) in enumerate(BLOCKS):
                            act.wait_ge(q_mm, NBL * h + b + 1)
                            wait(act, q_st[b], 16 * h)
                            act.activation(stage_q[0:HQ, b, 0:n], pq[0:HQ, b % 2, 0:n], ACT.Copy).then_inc(q_done, 1)
                            act.wait_ge(k_mm, KB * h + b + 1)
                            wait(act, k_st[b], 16 * h)
                            act.activation(stage_k[0:NOPE, b], pk[0:NOPE, b % 2], ACT.Copy).then_inc(k_done, 1)
                steps(act, H // 2, heads)

            @block.gpsimd
            def _(pool):
                pool.memset(ones[:], 1.0).then_inc(const_done, 1)
                pool.memset(eps[:], EPS).then_inc(const_done, 1)
                pool.wait_ge(hi_done, 1)
                pool.tensor_tensor(wv_lo[:], wv[:], wv_hi[:].bitcast(F32), ALU.subtract).then_inc(lo_done, 1)
                for b, (tok, n) in enumerate(BLOCKS):
                    pool.wait_ge(hi_done, 2 * b + 3)
                    pool.tensor_tensor(qn_lo[:, :, tok:tok + n], qa[:, :, tok:tok + n],
                                       qn_hi[:, :, tok:tok + n].bitcast(F32), ALU.subtract).then_inc(lo_done, 1)
                    at = 0 if b == 0 else PAST + tok
                    pool.tensor_tensor(ckv_lo[:, at:PAST + tok + n], ckv[:, at:PAST + tok + n],
                                       ckv_hi[:, at:PAST + tok + n].bitcast(F32), ALU.subtract).then_inc(lo_done, 1)

                def heads(i):
                    for u in range(2):
                        h = 2 * i + u
                        pool.wait_ge(whi_done, h + 1)
                        pool.tensor_tensor(w_lo[:, u], wraw[:, bass.ds(h, 1)].rearrange("p o n -> p (o n)"),
                                           w_hi[:, u].bitcast(F32), ALU.subtract).then_inc(wlo_done, 1)
                steps(pool, H // 2, heads)

            @block.tensor
            def _(pe):
                pe.wait_ge(const_done, 2)
                for b, (tok, n) in enumerate(BLOCKS):
                    pe.wait_ge(sq_done, 2 * b + 2)
                    wait(pe, root_done, 2 * b)
                    pe.matmul(sums[:, 0, 0:n], ones[:], sq[:, 0, 0:n], start=True, stop=False)
                    pe.matmul(sums[:, 0, 0:n], ones[:], sq[:, 1, 0:n], start=False, stop=True)
                    pe.matmul(sums[:, 1, 0:n], ones[:], sq[:, 2, 0:n], start=True, stop=True).then_inc(sums_done, 1)
                pe.wait_ge(in_ld, 16 * IN)
                for b in range(NB):
                    wait(pe, kr_rope, b - 1)
                    pe.matmul(rot[0:HQ, b % 2], perm[RO, :], kpe[RO, PAST + b * BLK:PAST + (b + 1) * BLK],
                              start=True, stop=True).then_inc(kr_mm, 1)
                pe.wait_ge(lo_done, 1 + 2 * NBL)
                for k in range(KEYS // P):
                    wait(pe, v_done, k - 1)
                    keys = slice(k * P, (k + 1) * P)
                    pe.matmul(pk[:, k % 2], ckv_hi[:, keys], wv_hi[:], start=True, stop=False)
                    pe.matmul(pk[:, k % 2], ckv_lo[:, keys], wv_hi[:], start=False, stop=False)
                    pe.matmul(pk[:, k % 2], ckv_hi[:, keys], wv_lo[:], start=False, stop=True).then_inc(v_mm, 1)
                pe.wait_ge(v_done, KEYS // P)
                pe.wait_ge(kr_rope, NB)

                def heads(i):
                    for u in range(2):
                        h = 2 * i + u
                        pe.wait_ge(wlo_done, h + 1)
                        for b, (tok, n) in enumerate(BLOCKS):
                            q = NBL * h + b
                            wait(pe, q_done, q if b == 0 else q - 1)
                            ops = [(w_hi, qn_hi), (w_lo, qn_hi), (w_hi, qn_lo)]
                            for k in range(2):
                                for o, (w, x) in enumerate(ops):
                                    mm = pe.matmul(pq[0:HQ, b % 2, 0:n], w[:, u, k * HQ:(k + 1) * HQ],
                                                   x[:, k, tok:tok + n], start=(k == 0 and o == 0),
                                                   stop=(k == 1 and o == 2))
                            mm.then_inc(q_mm, 1)
                            wait(pe, k_done, q if b == 0 else q - 1)
                            ops = [(w_hi, ckv_hi), (w_lo, ckv_hi), (w_hi, ckv_lo)]
                            for o, (w, x) in enumerate(ops):
                                mm = pe.matmul(pk[:, b % 2], w[:, u, 2 * HQ:], x[:, b * BLK:(b + 1) * BLK],
                                               start=(o == 0), stop=(o == 2))
                            mm.then_inc(k_mm, 1)
                            if b < NB:
                                pe.wait_ge(q_done, q + 1)
                                wait(pe, rope_done, NB * h + b - 1)
                                pe.matmul(rot[0:HQ, b % 2], perm[RO, :], stage_q[RO, b], start=True, stop=True
                                          ).then_inc(rot_mm, 1)
                steps(pe, H // 2, heads)

            @block.vector
            def _(dve):
                dve.wait_ge(in_ld, 16 * IN)
                for b, (tok, n) in enumerate(BLOCKS):
                    dve.wait_ge(root_done, 2 * b + 2)
                    wait(dve, norm_done, 3 * b)
                    dve.reciprocal(rstd[:, :, 0:n], root[:, :, 0:n]).then_inc(rstd_done, 1)
                    dve.wait_ge(rstd_done, b + 1)
                    for k in range(2):
                        x = qa[:, k, tok:tok + n]
                        dve.scalar_tensor_tensor(out=x, in0=x, scalar=gain[:, k:k + 1], in1=rstd[:, 0, 0:n],
                                                 op0=ALU.mult, op1=ALU.mult).then_inc(norm_done, 1)
                    x = ckv[:, PAST + tok:PAST + tok + n]
                    dve.scalar_tensor_tensor(out=x, in0=x, scalar=gain[:, 2:3], in1=rstd[:, 1, 0:n],
                                             op0=ALU.mult, op1=ALU.mult).then_inc(norm_done, 1)

                def rope(x, r, blk, parts, done):
                    wait(dve, part_done, parts)
                    dve.tensor_tensor(turned[RO, 0], x, cos[RO, blk], ALU.mult).then_inc(part_done, 1)
                    dve.tensor_tensor(turned[RO, 1], r, sin[RO, blk], ALU.mult).then_inc(part_done, 1)
                    dve.wait_ge(part_done, parts + 2)
                    dve.tensor_tensor(x, turned[RO, 0], turned[RO, 1], ALU.add).then_inc(done, 1)

                for b in range(NB):
                    dve.wait_ge(kr_mm, b + 1)
                    wait(dve, kr_rope, b)
                    rope(kpe[RO, PAST + b * BLK:PAST + (b + 1) * BLK], rot[RO, b % 2],
                         slice(b * BLK, (b + 1) * BLK), 2 * b, kr_rope)
                dve.wait_ge(kr_rope, NB)

                def heads(h):
                    for b in range(NB):
                        dve.wait_ge(rot_mm, NB * h + b + 1)
                        wait(dve, rope_done, NB * h + b)
                        rope(stage_q[RO, b], rot[RO, b % 2], slice(b * BLK, (b + 1) * BLK),
                             2 * (NB * h + b) + 2 * NB, rope_done)
                steps(dve, H, heads)


def attention_phase(nc, t, V, ident):
    NS = 9
    STEPS = [(b, c) for b in range(NB) for c in range(NS)] + [(NB, 0)]
    G = len(STEPS)
    BH = NB + 1
    PIECES = 5
    AT_STEP = {2: 0, 5: 1, 8: 2, 11: 3, 13: 4}
    FIRST_MAX = 2 * NS + 1
    KC, QC = KEYS // 2, T // 2
    PAIRS = H // 2
    LAG = 2
    with ExitStack() as ctx:
        p = Scope(nc, ctx, "at")
        q_hi = [p.sb(f"q_hi{u}", [HQ + 1, T], F32R) for u in range(2)]
        q_lo = [p.sb(f"q_lo{u}", [HQ, T], F32R) for u in range(2)]
        k_hi = [p.sb(f"k_hi{u}", [HQ + 1, KEYS], F32R) for u in range(2)]
        k_lo = [p.sb(f"k_lo{u}", [HQ, KEYS], F32R) for u in range(2)]
        v_hi = [p.sb(f"v_hi{u}", [P, KEYS // P, P], F32R) for u in range(2)]
        v_lo = [p.sb(f"v_lo{u}", [P, KEYS // P, P], F32R) for u in range(2)]
        raw = p.sb("raw", [HQ, KC])
        w = p.sb("w", [P, 2, 2, BLK])
        w_hi, w_lo = p.sb("w_hi", [P, LAG + 1, 2, BLK], F32R), p.sb("w_lo", [P, LAG + 1, 2, BLK], F32R)
        o = p.sb("o", [DV + 1, 2, BLK])
        mpart = p.sb("mpart", [P, 4, NS])
        mfin = p.sb("mfin", [P, 4])
        sc = p.ps("sc", [P, 4, BLK])
        mx = p.ps("mx", [P, 4, 256])
        acc = p.ps("acc", [P, 2, BLK])
        raw_ld, kpe_ld, o_st = p.sem("raw_ld"), p.sems("kpe_ld", 2), p.sem("o_st")
        warm_ld = p.sems("warm_ld", 4)
        hi_piece, lo_piece, kpe_hi, kpe_lo = (p.sem(n) for n in ("hi_piece", "lo_piece", "kpe_hi", "kpe_lo"))
        s_mm, exp_done, hi_done, lo_done, pv_mm = (p.sem(n) for n in ("s_mm", "exp_done", "hi_done", "lo_done", "pv_mm"))
        m_mm, red_done, mfin_done, tr_done, row_done = (p.sem(n) for n in ("m_mm", "red_done", "mfin_done", "tr_done", "row_done"))
        o_done, o_free, const_done = (p.sem(n) for n in ("o_done", "o_free", "const_done"))
        SLOTS = 2

        def max_of(u, b, last):
            if b < 2:
                return u, b + 2
            if last and u == 1:
                return None
            return 1 - u, (b - 2 if b < NB else NB)

        def blocks_in(last):
            out, before = [], (0, NB)
            for u in range(2):
                for b in range(BH):
                    out.append((u, b, before))
                    before = max_of(u, b, last)
            return out

        def needs_row(h, b):
            return {0: 5 * h + 1, 1: 5 * h + 2, 2: 5 * h + 4, 3: 5 * h + 5, 4: 5 * h + 3}[b]

        def warm_raw(r):
            return w[:].rearrange("p a b n -> p (a b n)")[0:HQ, 0:KC] if r % 2 else raw[:]

        def warm_load(sp, r):
            if r >= 2:
                sp.wait_ge(lo_piece, r - 1)
                sp.wait_ge(kpe_lo, r - 1)
            src = t["k"][0, :, r * KC:(r + 1) * KC] if r < 2 else t["q"][0, :, (r - 2) * QC:(r - 1) * QC]
            dst = warm_raw(r)[0:NOPE, :] if r < 2 else warm_raw(r)[:, 0:QC]
            sp.dma_start(dst, src).then_inc(warm_ld[r], 16)

        def piece_load(sp, h, r):
            wait(sp, lo_piece, PIECES * h + r if r else PIECES * h - 1)
            if r < 2:
                sp.dma_start(raw[0:NOPE, :], t["k"][bass.ds(h, 1), :, r * KC:(r + 1) * KC].rearrange("o p n -> (o p) n")
                             ).then_inc(raw_ld, 16)
            else:
                sp.dma_start(raw[0:HQ, 0:QC], t["q"][bass.ds(h, 1), :, (r - 2) * QC:(r - 1) * QC].rearrange("o p n -> (o p) n")
                             ).then_inc(raw_ld, 16)

        def piece_aps(u, r, rows, h):
            src = warm_raw(r) if isinstance(h, int) and h == 0 else raw[:]
            if r < 2:
                c = slice(r * KC, (r + 1) * KC)
                return src[rows, :], k_hi[u][rows, c], k_lo[u][rows, c]
            if r < 4:
                c = slice((r - 2) * QC, (r - 1) * QC)
                return src[0:HQ, 0:QC], q_hi[u][0:HQ, c], q_lo[u][0:HQ, c]
            return (V[:, bass.ds(h, 1)].rearrange("p o k d -> p (o k) d"),
                    v_hi[u][:, :, 0:DV], v_lo[u][:, :, 0:DV])

        def warm_bank(m):
            return sc[:, 0:2, :].rearrange("p s (q n) -> p (s q) n", q=2) if m % 2 else mx[:]

        def max_products(pe, buf, b, c, count, out=None):
            out = mx[:] if out is None else out
            pe.wait_ge(lo_piece, count)
            tok, n = BLOCKS[b]
            k0 = c * 256 if b < NB else PAST + S
            for q in range(n // P):
                mm = pe.matmul(out[:, q, :], q_hi[buf][0:HQ, tok + q * P:tok + (q + 1) * P],
                               k_hi[buf][0:HQ, k0:k0 + 256], start=True, stop=True)
            return mm

        def turn_max(pe, b):
            for q in range(BLOCKS[b][1] // P):
                mm = pe.transpose(mx[0:1, q, 0:P], mfin[:, q:q + 1], ident[:])
            return mm

        with nc.Block() as block:
            @block.sync
            def _(sp):
                sp.sem_inc(o_free, SLOTS)
                for r in range(4):
                    warm_load(sp, r)
                    if r < 2:
                        sp.dma_start(warm_raw(r)[NOPE:HQ, :], t["kpe"][:, r * KC:(r + 1) * KC]).then_inc(kpe_ld[r], 16)

                def pair(i, last):
                    for u in range(2):
                        h = 2 * i + u
                        if not (last and u == 1):
                            for r in range(4):
                                piece_load(sp, h + 1, r)
                        for b, (tok, n) in enumerate(BLOCKS):
                            j = BH * h + b
                            sp.wait_ge(o_done, SLOTS + j + 1)
                            slot = (BH * u + b) % 2
                            sp.dma_start(t["o"][bass.ds(h * DV, DV), tok:tok + n], o[0:DV, slot, 0:n]).then_inc(o_st, 16)
                            sp.dma_start(t["sums"][bass.ds(h, 1), tok:tok + n], o[DV:DV + 1, slot, 0:n]).then_inc(o_st, 16)
                            sp.wait_ge(o_st, 32 * j + 32)
                            sp.sem_inc(o_free, 1)
                with sp.Fori(0, PAIRS - 1) as i:
                    pair(i, False)
                pair(PAIRS - 1, True)

            @block.scalar
            def _(act):
                act.sem_inc(exp_done, SLOTS)

                def split(u, h, r, rows=slice(0, NOPE)):
                    if isinstance(h, int) and h == 0:
                        if r < 4:
                            act.wait_ge(warm_ld[r], 16)
                    elif r < 4:
                        act.wait_ge(raw_ld, 16 * (4 * (h - 1) + r + 1))
                    src, hi, _ = piece_aps(u, r, rows, h)
                    act.activation(hi, src, ACT.Copy).then_inc(hi_piece, 1)
                for r in range(PIECES):
                    if r < 2:
                        act.wait_ge(kpe_ld[r], 16)
                        c = slice(r * KC, (r + 1) * KC)
                        act.activation(k_hi[1][NOPE:HQ, c], warm_raw(r)[NOPE:HQ, :], ACT.Copy).then_inc(kpe_hi, 1)
                    split(0, 0, r, slice(0, HQ))

                def pair(i, last):
                    for u in range(2):
                        h = 2 * i + u
                        for l, (b, c) in enumerate(STEPS):
                            g, slot, n = G * h + l, (G * u + l) % 2, BLOCKS[b][1]
                            act.wait_ge(s_mm, g + 1)
                            act.wait_ge(lo_done, g + 1)
                            act.activation(w[:, slot, :, 0:n], sc[:, 2 * slot:2 * slot + 2, 0:n], ACT.Exp, scale=SM_SCALE
                                           ).then_inc(exp_done, 1)
                            act.wait_ge(exp_done, SLOTS + g + 1)
                            gu = G * u + l
                            act.wait_ge(pv_mm, SLOTS + (g - LAG if gu > LAG else 2 * G * i))
                            act.activation(w_hi[:, gu % (LAG + 1), :, 0:n], w[:, slot, :, 0:n], ACT.Copy).then_inc(hi_done, 1)
                            if l in AT_STEP and not (last and u == 1):
                                split(1 - u, h + 1, AT_STEP[l])
                with act.Fori(0, PAIRS - 1) as i:
                    pair(i, False)
                pair(PAIRS - 1, True)

            @block.gpsimd
            def _(pool):
                def split(u, h, r, rows=slice(0, NOPE)):
                    pool.wait_ge(hi_piece, PIECES * h + r + 1)
                    src, hi, lo = piece_aps(u, r, rows, h)
                    pool.tensor_tensor(lo, src, hi.bitcast(F32), ALU.subtract).then_inc(lo_piece, 1)
                for r in range(PIECES):
                    split(0, 0, r, slice(0, HQ))

                def pair(i, last):
                    for u in range(2):
                        if not (last and u == 1):
                            for r in range(PIECES):
                                split(1 - u, 2 * i + u + 1, r)
                with pool.Fori(0, PAIRS - 1) as i:
                    pair(i, False)
                pair(PAIRS - 1, True)

            @block.tensor
            def _(pe):
                pe.sem_inc(pv_mm, SLOTS)
                pe.wait_ge(const_done, 6)
                m = 0
                for x, b in enumerate((0, 1, NB)):
                    for c in range(NS if b < NB else 1):
                        wait(pe, red_done, m - 1)
                        if c == 0 and x:
                            pe.wait_ge(mfin_done, x)
                            turn_max(pe, (0, 1, NB)[x - 1]).then_inc(tr_done, 1)
                            pe.wait_ge(row_done, x)
                        max_products(pe, 0, b, c, 4, warm_bank(m)).then_inc(m_mm, 1)
                        m += 1

                def pair(i, last):
                    before = blocks_in(last)

                    def value_product(h, l, gu):
                        b, c = STEPS[l]
                        g, slot, n, u = G * h + l, gu % (LAG + 1), BLOCKS[b][1], gu // G
                        k0 = 2 * c if b < NB else (PAST + S) // P
                        if c == 0:
                            pe.wait_ge(o_done, BH * h + b + 1)
                        pe.wait_ge(lo_done, SLOTS + g + 1)
                        bank = acc[:, (BH * u + b) % 2, 0:n]
                        end = b == NB or c == NS - 1
                        for k in range(2):
                            pe.matmul(bank, v_hi[u][:, k0 + k, :], w_hi[:, slot, k, 0:n],
                                      start=(c == 0 and k == 0), stop=False)
                            pe.matmul(bank, v_lo[u][:, k0 + k, :], w_hi[:, slot, k, 0:n], start=False, stop=False)
                            mm = pe.matmul(bank, v_hi[u][:, k0 + k, :], w_lo[:, slot, k, 0:n],
                                           start=False, stop=(end and k == 1))
                        mm.then_inc(pv_mm, 1)

                    for u in range(2):
                        h = 2 * i + u
                        pe.wait_ge(lo_piece, PIECES * h + PIECES)
                        for l, (b, c) in enumerate(STEPS):
                            g, gu = G * h + l, G * u + l
                            slot = gu % 2
                            tok, n = BLOCKS[b]
                            k0 = 2 * c if b < NB else (PAST + S) // P
                            x = 3 + BH * h + b
                            tail = before[BH * u + b][2]
                            if c == 0 and tail is not None:
                                pe.wait_ge(mfin_done, x)
                                turn_max(pe, tail[1]).then_inc(tr_done, 1)
                            if c == 0:
                                pe.wait_ge(row_done, needs_row(h, b))
                            pe.wait_ge(exp_done, g + 1)
                            for k in range(2):
                                keys = slice((k0 + k) * P, (k0 + k + 1) * P)
                                bank = sc[:, 2 * slot + k, 0:n]
                                pe.matmul(bank, k_hi[u][:, keys], q_hi[u][:, tok:tok + n], start=True, stop=False)
                                pe.matmul(bank, k_lo[u][:, keys], q_hi[u][0:HQ, tok:tok + n], start=False, stop=False)
                                mm = pe.matmul(bank, k_hi[u][0:HQ, keys], q_lo[u][:, tok:tok + n], start=False, stop=True)
                            mm.then_inc(s_mm, 1)
                            ahead = max_of(u, b, last)
                            if ahead is not None:
                                if c == 0:
                                    pe.wait_ge(row_done, x)
                                pe.wait_ge(red_done, FIRST_MAX + g)
                                owner = h + 1 if ahead[0] != u else h
                                max_products(pe, ahead[0], ahead[1], c, PIECES * owner + 4).then_inc(m_mm, 1)
                            if gu >= LAG:
                                value_product(h if l >= LAG else h - 1, (gu - LAG) % G, gu - LAG)
                    for l in range(G - LAG, G):
                        value_product(h, l, G + l)
                with pe.Fori(0, PAIRS - 1) as i:
                    pair(i, False)
                pair(PAIRS - 1, True)

            @block.vector
            def _(dve):
                dve.sem_inc(lo_done, SLOTS)
                dve.sem_inc(o_done, SLOTS)
                for u in range(2):
                    if u:
                        for r in range(2):
                            dve.wait_ge(kpe_hi, r + 1)
                            c = slice(r * KC, (r + 1) * KC)
                            dve.tensor_tensor(k_lo[1][NOPE:HQ, c], warm_raw(r)[NOPE:HQ, :], k_hi[1][NOPE:HQ, c].bitcast(F32),
                                              ALU.subtract).then_inc(kpe_lo, 1)
                    dve.memset(k_hi[u][HQ:HQ + 1, :].bitcast(F32), 1.0).then_inc(const_done, 1)
                    dve.memset(v_hi[u][:, :, DV:].bitcast(F32), 1.0).then_inc(const_done, 1)
                    dve.memset(v_lo[u][:, :, DV:].bitcast(F32), 0.0).then_inc(const_done, 1)

                def reduce_max(b, c, m, src=None):
                    q = BLOCKS[b][1] // P
                    dve.wait_ge(m_mm, m + 1)
                    dve.tensor_reduce(mpart[:, 0:q, c], (mx[:] if src is None else src)[:, 0:q, :], AX.X, ALU.max).then_inc(red_done, 1)
                    if b == NB or c == NS - 1:
                        dve.wait_ge(red_done, m + 1)
                        dve.tensor_reduce(mfin[:, 0:q], mpart[:, 0:q, 0:c + 1], AX.X, ALU.max).then_inc(mfin_done, 1)

                def write_row(buf, b, x):
                    tok, n = BLOCKS[b]
                    dve.wait_ge(tr_done, x + 1)
                    dve.tensor_scalar(q_hi[buf][HQ:HQ + 1, tok:tok + n].rearrange("p (q n) -> p q n", n=P),
                                      mx[0:1, 0:n // P, 0:P], -1.0, None, ALU.mult).then_inc(row_done, 1)

                m = 0
                for x, b in enumerate((0, 1, NB)):
                    for c in range(NS if b < NB else 1):
                        if c == 0 and x:
                            write_row(0, (0, 1, NB)[x - 1], x - 1)
                        reduce_max(b, c, m, warm_bank(m))
                        m += 1

                def pair(i, last):
                    before = blocks_in(last)

                    def take_out(h, u, b):
                        j, slot, n = BH * h + b, (BH * u + b) % 2, BLOCKS[b][1]
                        dve.wait_ge(pv_mm, SLOTS + G * h + (NS * b + NS if b < NB else G))
                        dve.wait_ge(o_free, j + 1)
                        dve.tensor_copy(o[:, slot, 0:n], acc[0:DV + 1, slot, 0:n]).then_inc(o_done, 1)

                    for u in range(2):
                        h = 2 * i + u
                        for l, (b, c) in enumerate(STEPS):
                            g, slot, n = G * h + l, (G * u + l) % 2, BLOCKS[b][1]
                            tail = before[BH * u + b][2]
                            if c == 0 and tail is not None:
                                write_row(*tail, 2 + BH * h + b)
                            ahead = max_of(u, b, last)
                            if ahead is not None:
                                reduce_max(ahead[1], c, FIRST_MAX + g)
                            dve.wait_ge(hi_done, g + 1)
                            s3 = (G * u + l) % (LAG + 1)
                            dve.tensor_tensor(w_lo[:, s3, :, 0:n], w[:, slot, :, 0:n], w_hi[:, s3, :, 0:n].bitcast(F32),
                                              ALU.subtract).then_inc(lo_done, 1)
                            if c == LAG - 1 and b:
                                take_out(h, u, b - 1)
                            elif c == LAG - 1 and u:
                                take_out(h - 1, 0, NB - 1)
                                take_out(h - 1, 0, NB)
                    take_out(h, 1, NB - 1)
                    take_out(h, 1, NB)
                with dve.Fori(0, PAIRS - 1) as i:
                    pair(i, False)
                pair(PAIRS - 1, True)


def mix_phase(nc, t):
    M = D // P
    NBL = len(BLOCKS)
    with ExitStack() as ctx:
        p = Scope(nc, ctx, "mx")
        wraw = p.sb("wraw", [P, CT, D])
        wc_hi, wc_lo = p.sb("wc_hi", [P, CT, D], F32R), p.sb("wc_lo", [P, CT, D], F32R)
        wo_hi, wo_lo = p.sb("wo_hi", [P, CT, D], F32R), p.sb("wo_lo", [P, CT, D], F32R)
        c = p.sb("c", [P, CT, BLK])
        sq = p.sb("sq", [P, CT, BLK])
        o = p.sb("o", [P, CT, BLK])
        c_hi, c_lo = p.sb("c_hi", [P, 2, CT, BLK], F32R), p.sb("c_lo", [P, 2, CT, BLK], F32R)
        o_hi, o_lo = p.sb("o_hi", [P, 2, CT, BLK], F32R), p.sb("o_lo", [P, 2, CT, BLK], F32R)
        gates = p.sb("gates", [P, 2, 2, BLK])
        mixed = p.sb("mixed", [P, 2, BLK])
        root, rstd = p.sb("root", [P, BLK]), p.sb("rstd", [P, BLK])
        mean_w = p.sb("mean_w", [P, P])
        inv = p.sb("inv", [P, CT, BLK])
        sums = p.sb("sums", [P, 2, H * T // P])
        sums_ld, inv_done, inv_st, inv_ld, o_scaled = (p.sem(n) for n in ("sums_ld", "inv_done", "inv_st", "inv_ld", "o_scaled"))
        norm = p.sb("norm", [P, 2, CT])
        eps = p.sb("eps", [P, 1])
        mean, var = p.ps("mean", [P, BLK]), p.ps("var", [P, BLK])
        pc, po = p.ps("pc", [P, 2, BLK]), p.ps("po", [P, 2, BLK])
        w_ld, in_ld, norm_ld = p.sems("w_ld", CT), p.sem("in_ld"), p.sem("norm_ld")
        g_ld, mix_st = p.sems("g_ld", 2), p.sems("mix_st", 2)
        const_done, w_hi_done, w_lo_done = p.sem("const_done"), p.sem("w_hi_done"), p.sems("w_lo_done", 2)
        mean_mm, cent_done, sq_done, var_mm = (p.sem(n) for n in ("mean_mm", "cent_done", "sq_done", "var_mm"))
        root_done, rstd_done, y_done, silu_done = (p.sem(n) for n in ("root_done", "rstd_done", "y_done", "silu_done"))
        hi_done, lo_done, mm_done, gated, mix_done = (p.sem(n) for n in ("hi_done", "lo_done", "mm_done", "gated", "mix_done"))

        def split_w_lo(eng, j):
            hi, lo = (wc_hi, wc_lo) if j >= CT else (wo_hi, wo_lo)
            eng.wait_ge(w_hi_done, j + 1)
            eng.tensor_tensor(lo[:, j % CT], wraw[:, j % CT], hi[:, j % CT].bitcast(F32), ALU.subtract
                              ).then_inc(w_lo_done[j % 2], 1)

        with nc.Block() as block:
            @block.sync
            def _(sp):
                def load(b):
                    tok, n = BLOCKS[b]
                    wait(sp, hi_done, 2 * b)
                    wait(sp, lo_done, 2 * b)
                    sp.dma_start(c[:, :, 0:n], t["conv"][:, tok:tok + n].rearrange("(k p) n -> p k n", p=P)
                                 ).then_inc(in_ld, 16)
                    sp.dma_start(o[:, :, 0:n], t["o"][:, tok:tok + n].rearrange("(k p) n -> p k n", p=P)
                                 ).then_inc(in_ld, 16)
                    if b == 0:
                        sp.wait_ge(inv_done, 1)
                        sp.dma_start(flat(t["inverse"]), sums[:, 1]).then_inc(inv_st, 16)
                        sp.wait_ge(inv_st, 16)
                    for h in range(H):
                        sp.dma_start(inv[h % 2 * DV:h % 2 * DV + DV, h // 2, 0:n],
                                     t["inverse"][h, tok:tok + n].partition_broadcast(DV)).then_inc(inv_ld, 16)
                def flat(rows):
                    return rows.rearrange("h (g n) -> (h g) n", n=H * T // P)
                sp.dma_start(norm[:], t["conv_norm"]).then_inc(norm_ld, 16)
                sp.dma_start(sums[:, 0], flat(t["sums"])).then_inc(sums_ld, 16)

                def load_w(j):
                    if j >= CT:
                        sp.wait_ge(w_lo_done[j % 2], (j - CT) // 2 + 1)
                    sp.dma_start(wraw[:, j % CT], t["w_conv_out" if j >= CT else "w_o"][:, j % CT]).then_inc(w_ld[j % CT], 16)
                for j in range(CT):
                    load_w(j)
                load(0)
                for j in range(CT, 2 * CT):
                    load_w(j)
                for b, (tok, n) in enumerate(BLOCKS):
                    if b + 1 < NBL:
                        load(b + 1)
                    for m in range(M):
                        j = M * b + m
                        wait(sp, mix_done, j - 1)
                        for g in range(2):
                            sp.dma_start(gates[:, m % 2, g, 0:n], t["gates"][g * D + m * P:g * D + (m + 1) * P, tok:tok + n]
                                         ).then_inc(g_ld[m % 2], 16)

            @block.gpsimd
            def _(pool):
                pool.memset(mean_w[:], 1.0 / CONV).then_inc(const_done, 1)
                pool.memset(eps[:], EPS).then_inc(const_done, 1)
                for j in (0, 2):
                    split_w_lo(pool, j)
                for b, (tok, n) in enumerate(BLOCKS):
                    pool.wait_ge(in_ld, 32 * b + 32)
                    pool.wait_ge(inv_ld, 16 * H * (b + 1))
                    pool.tensor_tensor(o[:, :, 0:n], o[:, :, 0:n], inv[:, :, 0:n], ALU.mult).then_inc(o_scaled, 1)
                    for q, (src, hi, lo) in enumerate(((o, o_hi, o_lo), (c, c_hi, c_lo))):
                        if b == 0 and q == 1:
                            for j in (CT, CT + 2):
                                split_w_lo(pool, j)
                        pool.wait_ge(hi_done, 2 * b + q + 1)
                        pool.tensor_tensor(lo[:, b % 2, :, 0:n], src[:, :, 0:n], hi[:, b % 2, :, 0:n].bitcast(F32),
                                           ALU.subtract).then_inc(lo_done, 1)

            @block.scalar
            def _(act):
                act.wait_ge(const_done, 2)
                act.wait_ge(norm_ld, 16)

                def store(j):
                    b, m = divmod(j, M)
                    tok, n = BLOCKS[b]
                    act.wait_ge(mix_done, j + 1)
                    act.dma_start(t["mixed"][m * P:(m + 1) * P, tok:tok + n], mixed[:, m % 2, 0:n]
                                  ).then_inc(mix_st[m % 2], 16)

                def prepare(b):
                    tok, n = BLOCKS[b]
                    act.wait_ge(in_ld, 32 * b + 32)
                    wait(act, mm_done, M * (b - 1))
                    act.wait_ge(cent_done, CT * b + CT)
                    act.activation(sq[:, :, 0:n], c[:, :, 0:n], ACT.Square).then_inc(sq_done, 1)
                    act.wait_ge(o_scaled, b + 1)
                    act.activation(o_hi[:, b % 2, :, 0:n], o[:, :, 0:n], ACT.Copy).then_inc(hi_done, 1)
                    yield
                    act.wait_ge(var_mm, b + 1)
                    wait(act, rstd_done, b)
                    act.activation(root[:, 0:n], var[:, 0:n], ACT.Sqrt, bias=eps[:]).then_inc(root_done, 1)
                    act.wait_ge(y_done, CT * b + CT)
                    for k in range(CT):
                        act.activation(c[:, k, 0:n], c[:, k, 0:n], ACT.Silu, bias=norm[:, 1, k:k + 1]
                                       ).then_inc(silu_done, 1)
                    act.wait_ge(silu_done, CT * b + CT)
                    act.activation(c_hi[:, b % 2, :, 0:n], c[:, :, 0:n], ACT.Copy).then_inc(hi_done, 1)

                def split_w_hi(j):
                    act.wait_ge(w_ld[j % CT], 16 * (j // CT) + 16)
                    act.activation((wc_hi if j >= CT else wo_hi)[:, j % CT], wraw[:, j % CT], ACT.Copy).then_inc(w_hi_done, 1)
                for j in range(CT):
                    split_w_hi(j)
                for _ in prepare(0):
                    for j in range(CT, 2 * CT):
                        split_w_hi(j)
                for b in range(NBL):
                    ahead = prepare(b + 1) if b + 1 < NBL else iter(())
                    for m in range(M):
                        store(M * b + m)
                        if m in (2, 4):
                            next(ahead, None)
                for u in range(2):
                    act.wait_ge(mix_st[u], 16 * NBL * M // 2)

            @block.vector
            def _(dve):
                dve.wait_ge(sums_ld, 16)
                dve.reciprocal(sums[:, 1], sums[:, 0]).then_inc(inv_done, 1)
                dve.wait_ge(norm_ld, 16)

                def prepare(b):
                    tok, n = BLOCKS[b]
                    dve.wait_ge(mean_mm, b + 1)
                    for k in range(CT):
                        dve.tensor_tensor(c[:, k, 0:n], c[:, k, 0:n], mean[:, 0:n], ALU.subtract).then_inc(cent_done, 1)
                    yield
                    dve.wait_ge(root_done, b + 1)
                    wait(dve, y_done, CT * b)
                    dve.reciprocal(rstd[:, 0:n], root[:, 0:n]).then_inc(rstd_done, 1)
                    dve.wait_ge(rstd_done, b + 1)
                    for k in range(CT):
                        dve.scalar_tensor_tensor(out=c[:, k, 0:n], in0=c[:, k, 0:n], scalar=norm[:, 0, k:k + 1],
                                                 in1=rstd[:, 0:n], op0=ALU.mult, op1=ALU.mult).then_inc(y_done, 1)

                for j in (1, 3):
                    split_w_lo(dve, j)
                for _ in prepare(0):
                    for j in (CT + 1, CT + 3):
                        split_w_lo(dve, j)
                for b, (tok, n) in enumerate(BLOCKS):
                    ahead = prepare(b + 1) if b + 1 < NBL else iter(())
                    for m in range(M):
                        j = M * b + m
                        u = m % 2
                        dve.wait_ge(g_ld[u], 32 * (j // 2 + 1))
                        dve.wait_ge(mm_done, j + 1)
                        for g, bank in enumerate((pc, po)):
                            dve.tensor_tensor(gates[:, u, g, 0:n], bank[:, u, 0:n], gates[:, u, g, 0:n], ALU.mult
                                              ).then_inc(gated, 1)
                        wait(dve, mix_st[u], 16 * (j // 2))
                        dve.wait_ge(gated, 2 * j + 2)
                        dve.tensor_tensor(mixed[:, u, 0:n], gates[:, u, 0, 0:n], gates[:, u, 1, 0:n], ALU.add
                                          ).then_inc(mix_done, 1)
                        if m in (2, 4):
                            next(ahead, None)

            @block.tensor
            def _(pe):
                pe.wait_ge(const_done, 2)

                def average(b, out, src, done):
                    n = BLOCKS[b][1]
                    for k in range(CT):
                        mm = pe.matmul(out[:, 0:n], mean_w[:], src[:, k, 0:n], start=(k == 0), stop=(k == CT - 1))
                    mm.then_inc(done, 1)

                pe.wait_ge(in_ld, 32)
                average(0, mean, c, mean_mm)
                pe.wait_ge(sq_done, 1)
                average(0, var, sq, var_mm)
                pe.wait_ge(w_lo_done[0], CT)
                pe.wait_ge(w_lo_done[1], CT)
                for b, (tok, n) in enumerate(BLOCKS):
                    pe.wait_ge(lo_done, 2 * b + 2)
                    for m in range(M):
                        j, u = M * b + m, m % 2
                        wait(pe, mix_done, j - 1)
                        cols = slice(m * P, (m + 1) * P)
                        for bank, w, x in ((pc, (wc_hi, wc_lo), (c_hi, c_lo)), (po, (wo_hi, wo_lo), (o_hi, o_lo))):
                            for k in range(CT):
                                for q, (a, e) in enumerate(((0, 0), (1, 0), (0, 1))):
                                    mm = pe.matmul(bank[:, u, 0:n], w[a][:, k, cols], x[e][:, b % 2, k, 0:n],
                                                   start=(k == 0 and q == 0), stop=(k == CT - 1 and q == 2))
                        mm.then_inc(mm_done, 1)
                        if b + 1 < NBL and m == 1:
                            pe.wait_ge(in_ld, 32 * b + 64)
                            pe.wait_ge(cent_done, CT * b + CT)
                            average(b + 1, mean, c, mean_mm)
                        if b + 1 < NBL and m == 4:
                            pe.wait_ge(sq_done, b + 2)
                            pe.wait_ge(root_done, b + 1)
                            average(b + 1, var, sq, var_mm)


def out_phase(nc, t, affT, ident):
    PAIRS = T // P // 2
    with ExitStack() as ctx:
        p = Scope(nc, ctx, "op")
        wraw = p.sb("wraw", [P, 2, D])
        w_hi, w_lo = p.sb("w_hi", [P, KD, D], F32R), p.sb("w_lo", [P, KD, D], F32R)
        gate, gain, shift = p.sb("gate", [P, 2, D]), p.sb("gain", [P, 2, D]), p.sb("shift", [P, 2, D])
        norm = p.sb("norm", [P, D])
        m_raw = p.sb("m_raw", [P, 2, KD, 2 * P])
        m_hi, m_lo = p.sb("m_hi", [P, 2, KD, 2 * P], F32R), p.sb("m_lo", [P, 2, KD, 2 * P], F32R)
        x, h = p.sb("x", [P, 2, D]), p.sb("h", [P, 2, D])
        y = p.sb("y", [P, 2, D])
        hT = p.sb("hT", [P, 2, KD, P])
        w_r = p.sb("w_r", [P, KD, E])
        sumsq, meansq, root, rstd = (p.sb(n, [P, 2]) for n in ("sumsq", "meansq", "root", "rstd"))
        top, esum, einv = (p.sb(n, [P, 2]) for n in ("top", "esum", "einv"))
        ex, aff = p.sb("ex", [P, 2, E]), p.sb("aff", [P, 2, E])
        po = p.ps("po", [P, 2, D])
        tp = p.ps("tp", [P, D])
        lg = p.ps("lg", [P, 2, E])
        at = p.ps("at", [E, 2, P])
        raw_at = [wraw[:, 0], wraw[:, 1], y[:, 0], y[:, 1]] + [hT[:, v].rearrange("p k n -> p (k n)") for v in range(2)]
        RAW = len(raw_at)
        w_ld, wr_ld = p.sems("w_ld", RAW), p.sem("wr_ld")
        rows_ld, m_ld = p.sem("rows_ld"), p.sems("m_ld", 2)
        x_ld, x2_st, h_st = p.sems("x_ld", 2), p.sems("x2_st", 2), p.sems("h_st", 2)
        w_hi_done, w_lo_done = p.sem("w_hi_done"), p.sems("w_lo_done", 2)
        m_hi_done, m_lo_done = p.sem("m_hi_done"), p.sem("m_lo_done")
        gain_done, mm_done, gated, x2_done = (p.sem(n) for n in ("gain_done", "mm_done", "gated", "x2_done"))
        sq_done, ms_done, root_done, rstd_done = (p.sem(n) for n in ("sq_done", "ms_done", "root_done", "rstd_done"))
        scaled, h_done, tp_done, hT_done = (p.sem(n) for n in ("scaled", "h_done", "tp_done", "hT_done"))
        lg_done, top_done, ex_done, einv_done = (p.sem(n) for n in ("lg_done", "top_done", "ex_done", "einv_done"))
        aff_done, at_done, affT_done = (p.sem(n) for n in ("aff_done", "at_done", "affT_done"))

        def pipeline(eng, step):
            step(0, 0, 0, True, False, False)
            step(0, 1, 0, True, True, False)
            with eng.Fori(1, (PAIRS - 1) // 2) as c:
                step(c, 0, 0, True, True, True)
                step(c, 1, 0, True, True, True)
            step(PAIRS // 2, 0, 1, True, True, True)
            step(PAIRS // 2, 1, 1, False, True, True)
            step(PAIRS // 2 + 1, 0, 1, False, False, True)

        with nc.Block() as block:
            @block.sync
            def _(sp):
                def load_m(i, slot):
                    wait(sp, m_lo_done, i - 1)
                    sp.dma_start(m_raw[:, slot], t["mixed"][:, bass.ds(i * 2 * P, 2 * P)].rearrange("(k p) n -> p k n", p=P)
                                 ).then_inc(m_ld[slot], 16)

                def load_x(i, u):
                    sp.dma_start(x[:, u], t["x"][bass.ds((2 * i + u) * P, P), :]).then_inc(x_ld[u], 16)

                for k in range(KD):
                    if k >= RAW:
                        sp.wait_ge(w_lo_done[k % 2], (k - RAW) // 2 + 1)
                    sp.dma_start(raw_at[k % RAW], t["w_out"][k * P:(k + 1) * P, :]).then_inc(w_ld[k % RAW], 16)
                    if k == 1:
                        load_m(0, 0)
                    if k == RAW - 1:
                        sp.dma_start(gate[:, 0], t["mod"][0, 2 * D:3 * D].partition_broadcast(P)).then_inc(rows_ld, 16)
                        sp.dma_start(gate[:, 1], t["mod"][1, 2 * D:3 * D].partition_broadcast(P)).then_inc(rows_ld, 16)
                load_x(0, 0)
                load_x(0, 1)
                for s in range(2):
                    for dst, at_col in ((shift, 3), (gain, 4)):
                        sp.dma_start(dst[:, s], t["mod"][s, at_col * D:(at_col + 1) * D].partition_broadcast(P)
                                     ).then_inc(rows_ld, 16)
                sp.dma_start(norm[:], t["norm2"].partition_broadcast(P)).then_inc(rows_ld, 16)
                sp.dma_start(w_r[:], t["w_router"]).then_inc(wr_ld, 16)

                def step(c, slot, s, cur, prev, old):
                    i = 2 * c + slot
                    if not cur:
                        return
                    if s == 0:
                        load_m(i + 1, 1 - slot)
                    for u in range(2):
                        j = 2 * i + u
                        sp.wait_ge(x2_done, j + 1)
                        sp.dma_start(t["x2"][bass.ds(j * P, P), :], y[:, u]).then_inc(x2_st[u], 16)
                        if s == 0:
                            load_x(i + 1, u)
                    for u in range(2):
                        j = 2 * i + u
                        sp.wait_ge(h_done, j + 1)
                        sp.dma_start(t["h2"][bass.ds(j * P, P), :], h[:, u]).then_inc(h_st[u], 16)
                pipeline(sp, step)
                for u in range(2):
                    sp.wait_ge(x2_st[u], 16 * PAIRS)
                    sp.wait_ge(h_st[u], 16 * PAIRS)

            @block.scalar
            def _(act):
                def split_m(i, slot, half):
                    act.wait_ge(m_ld[slot], 16 * half + 16)
                    wait(act, mm_done, 2 * i - 2)
                    act.activation(m_hi[:, slot], m_raw[:, slot], ACT.Copy).then_inc(m_hi_done, 1)

                for k in range(KD):
                    act.wait_ge(w_ld[k % RAW], 16 * (k // RAW + 1))
                    act.activation(w_hi[:, k], raw_at[k % RAW], ACT.Copy).then_inc(w_hi_done, 1)
                    if k == 1:
                        split_m(0, 0, 0)

                def step(c, slot, s, cur, prev, old):
                    i = 2 * c + slot
                    if cur and s == 0:
                        split_m(i + 1, 1 - slot, c + slot)
                    for u in range(2):
                        if prev:
                            j = 2 * (i - 1) + u
                            act.wait_ge(tp_done, j + 1)
                            wait(act, lg_done, i - 1)
                            act.activation(hT[:, u], tp[:].rearrange("p (k n) -> p k n", k=KD), ACT.Copy).then_inc(hT_done, 1)
                        if cur:
                            j = 2 * i + u
                            act.wait_ge(x2_done, j + 1)
                            wait(act, tp_done, j - 1)
                            wait(act, h_st[u], 16 * i)
                            act.activation(h[:, u], y[:, u], ACT.Square, accum_out=sumsq[:, u:u + 1]).then_inc(sq_done, 1)
                            act.wait_ge(ms_done, j + 1)
                            act.activation(root[:, u:u + 1], meansq[:, u:u + 1], ACT.Sqrt).then_inc(root_done, 1)
                        if old and u == 0:
                            act.wait_ge(top_done, i - 1)
                            for v in range(2):
                                act.activation(ex[:, v], lg[:, v], ACT.Exp, bias=top[:, v:v + 1], accum_out=esum[:, v:v + 1]
                                               ).then_inc(ex_done, 1)
                    if old:
                        act.wait_ge(at_done, i - 1)
                        act.activation(affT[:, bass.ds((i - 2) * 2 * P, 2 * P)], at[:].rearrange("e u n -> e (u n)"), ACT.Copy
                                       ).then_inc(affT_done, 1)
                pipeline(act, step)

            @block.gpsimd
            def _(pool):
                def split_m(i, slot):
                    pool.wait_ge(m_hi_done, i + 1)
                    pool.tensor_tensor(m_lo[:, slot], m_raw[:, slot], m_hi[:, slot].bitcast(F32), ALU.subtract
                                       ).then_inc(m_lo_done, 1)

                for k in range(0, KD, 2):
                    pool.wait_ge(w_hi_done, k + 1)
                    pool.tensor_tensor(w_lo[:, k], raw_at[k % RAW], w_hi[:, k].bitcast(F32), ALU.subtract
                                       ).then_inc(w_lo_done[0], 1)
                    if k == 0:
                        split_m(0, 0)
                pool.wait_ge(rows_ld, 16 * 7)

                def step(c, slot, s, cur, prev, old):
                    i = 2 * c + slot
                    if cur:
                        if s == 0:
                            split_m(i + 1, 1 - slot)
                        for u in range(2):
                            pool.wait_ge(scaled, 2 * i + u + 1)
                            pool.tensor_tensor(h[:, u], h[:, u], shift[:, s], ALU.add).then_inc(h_done, 1)
                pipeline(pool, step)

            @block.vector
            def _(dve):
                for k in range(1, KD, 2):
                    dve.wait_ge(w_hi_done, k + 1)
                    dve.tensor_tensor(w_lo[:, k], raw_at[k % RAW], w_hi[:, k].bitcast(F32), ALU.subtract
                                      ).then_inc(w_lo_done[1], 1)
                dve.wait_ge(rows_ld, 16 * 7)
                for s in range(2):
                    dve.scalar_tensor_tensor(out=gain[:, s], in0=gain[:, s], scalar=1.0, in1=norm[:],
                                             op0=ALU.add, op1=ALU.mult).then_inc(gain_done, 1)
                dve.wait_ge(gain_done, 2)

                def step(c, slot, s, cur, prev, old):
                    i = 2 * c + slot
                    for u in range(2):
                        j = 2 * i + u
                        if cur:
                            dve.wait_ge(mm_done, j + 1)
                            wait(dve, x2_st[u], 16 * i)
                            dve.tensor_tensor(y[:, u], po[:, u], gate[:, s], ALU.mult).then_inc(gated, 1)
                            dve.wait_ge(gated, j + 1)
                            dve.wait_ge(x_ld[u], 16 * i + 16)
                            dve.tensor_tensor(y[:, u], y[:, u], x[:, u], ALU.add).then_inc(x2_done, 1)
                        if old and u == 0:
                            dve.wait_ge(lg_done, i - 1)
                            dve.tensor_reduce(top[:], lg[:], AX.X, ALU.max, negate=True).then_inc(top_done, 1)
                        if cur:
                            dve.wait_ge(sq_done, j + 1)
                            dve.tensor_scalar(meansq[:, u:u + 1], sumsq[:, u:u + 1], 1.0 / D, EPS, ALU.mult, ALU.add
                                              ).then_inc(ms_done, 1)
                            dve.wait_ge(root_done, j + 1)
                            dve.reciprocal(rstd[:, u:u + 1], root[:, u:u + 1]).then_inc(rstd_done, 1)
                            dve.wait_ge(rstd_done, j + 1)
                            dve.scalar_tensor_tensor(out=h[:, u], in0=y[:, u], scalar=rstd[:, u:u + 1], in1=gain[:, s],
                                                     op0=ALU.mult, op1=ALU.mult).then_inc(scaled, 1)
                        if old and u == 0:
                            dve.wait_ge(ex_done, 2 * i - 2)
                            wait(dve, aff_done, 2 * i - 4)
                            dve.reciprocal(einv[:], esum[:]).then_inc(einv_done, 1)
                            dve.wait_ge(einv_done, i - 1)
                            wait(dve, at_done, i - 2)
                            for v in range(2):
                                dve.tensor_scalar(aff[:, v], ex[:, v], einv[:, v:v + 1], None, ALU.mult).then_inc(aff_done, 1)
                pipeline(dve, step)

            @block.tensor
            def _(pe):
                def step(c, slot, s, cur, prev, old):
                    i = 2 * c + slot
                    for u in range(2):
                        j = 2 * i + u
                        if cur:
                            wait(pe, gated, j - 1)
                            pe.wait_ge(m_lo_done, i + 1)
                            for k in range(KD):
                                if isinstance(i, int) and i == 0 and u == 0:
                                    pe.wait_ge(w_lo_done[k % 2], k // 2 + 1)
                                for m, w in ((m_hi, w_hi), (m_hi, w_lo), (m_lo, w_hi)):
                                    for n in range(2):
                                        mm = pe.matmul(po[:, u, n * BLK:(n + 1) * BLK], m[:, slot, k, u * P:(u + 1) * P],
                                                       w[:, k, n * BLK:(n + 1) * BLK],
                                                       start=(k == 0 and m is m_hi and w is w_hi),
                                                       stop=(k == KD - 1 and m is m_lo))
                            mm.then_inc(mm_done, 1)
                        if old and u == 0:
                            if not isinstance(i, int) or i > 2:
                                pe.wait_ge(ex_done, 2 * i - 4)
                            pe.wait_ge(hT_done, 2 * i - 2)
                            pe.wait_ge(wr_ld, 16)
                            for v in range(2):
                                for k in range(KD):
                                    mm = pe.matmul(lg[:, v], hT[:, v, k], w_r[:, k], start=(k == 0), stop=(k == KD - 1),
                                                   skip_group_check=True)
                            mm.then_inc(lg_done, 1)
                        if prev:
                            jp = 2 * (i - 1) + u
                            pe.wait_ge(h_done, jp + 1)
                            wait(pe, hT_done, jp)
                            for k in range(KD):
                                mm = pe.transpose(tp[:, k * P:(k + 1) * P], h[:, u, k * P:(k + 1) * P], ident[:])
                            mm.then_inc(tp_done, 1)
                    if old:
                        pe.wait_ge(aff_done, 2 * i - 2)
                        wait(pe, affT_done, i - 2)
                        for v in range(2):
                            mm = pe.transpose(at[:, v], aff[:, v], ident[:])
                        mm.then_inc(at_done, 1)
                pipeline(pe, step)


def topk_phase(nc, t, affT, tab, pos, ident):
    GR = S // CAP
    BITS = 30
    ROUNDS = CAP // 8
    with ExitStack() as ctx:
        p = Scope(nc, ctx, "tk")
        aff, left = p.sb("aff", [P, CAP]), p.sb("left", [P, CAP])
        val, at = p.sb("val", [P, CAP]), p.sb("at", [P, CAP], U32)
        pair = p.sb("pair", [P, CAP, 2])
        over = p.sb("over", [P, CAP])
        topp, atp, atpf = p.sb("topp", [E, CAPP]), p.sb("atp", [E, CAPP], U32), p.sb("atpf", [E, CAPP])
        cand, low, kept = (p.sb(n, [P, 1], U32) for n in ("cand", "low", "kept"))
        bits = p.sb("bits", [P, BITS], U32)
        same, before, group0 = p.sb("same", [P, P]), p.sb("before", [P, P]), p.sb("group0", [P, 1])
        slot, base = p.sb("slot", [P, 2]), p.sb("base", [P, 2, E])
        ones = p.sb("ones", [P, P])
        count, n_gt, n_ge, n_eq, room, take, off = (p.sb(n, [P, 1]) for n in (
            "count", "n_gt", "n_ge", "n_eq", "room", "take", "off"))
        diag = p.sb("diag", [P, P])
        reached, start = p.sb("reached", [P, 2, E, GR]), p.sb("start", [P, 2, E, GR])
        groups, begun = p.sb("groups", [P, 2, E]), p.sb("begun", [P, 2, E])
        total = p.ps("total", [P, 4])
        offs = p.ps("offs", [P, P])
        tp = p.ps("tp", [CAPP, 2, E])
        ld, max_done, at_done, cut_done = p.sem("ld"), p.sem("max_done"), p.sem("at_done"), p.sem("cut_done")
        count_done, total_done, kept_done, low_done, cand_done = (
            p.sem(n) for n in ("count_done", "total_done", "kept_done", "low_done", "cand_done"))
        atp_done, tp_done, out_done, tail, sums_done, pair_done, list_st, tab_ld = (
            p.sem(n) for n in ("atp_done", "tp_done", "out_done", "tail", "sums_done", "pair_done", "list_st", "tab_ld"))
        LOADS = 8 + 7

        with nc.Block() as block:
            @block.sync
            def _(sp):
                for g in range(GR):
                    sp.dma_start(aff[g * E:(g + 1) * E, :], affT[:, g * CAP:(g + 1) * CAP]).then_inc(ld, 16)
                for dst, src in ((bits, "rank_bits"), (same, "rank_same"), (before, "rank_before"), (group0, "rank_group0"),
                                 (slot, "rank_slot"), (base, "rank_base"), (ones, "rank_ones")):
                    sp.dma_start(dst[:], t[src]).then_inc(ld, 16)
                sp.wait_ge(pair_done, 2)
                sp.dma_start(t["ranked"].rearrange("(p n) c -> p n c", p=P), pair[:]).then_inc(list_st, 16)
                sp.wait_ge(list_st, 16)

            @block.vector
            def _(dve):
                done = [0]

                def rank_round(r, src, dst, top, where, n):
                    cols = slice(8 * r, 8 * r + 8)
                    done[0] += 1
                    wait(dve, cut_done, done[0] - 1)
                    dve.max(top[:, cols], src).then_inc(max_done, 1)
                    dve.wait_ge(max_done, done[0])
                    dve.max_index(where[:, cols], top[:, cols], src).then_inc(at_done, 1)
                    dve.wait_ge(at_done, done[0])
                    dve.match_replace(dst, top[:, cols], src, -1.0).then_inc(cut_done, 1)

                steps_done = [0]

                def tail_step(*args, op=None, **kw):
                    if steps_done[0]:
                        dve.wait_ge(tail, steps_done[0])
                    op(*args, **kw).then_inc(tail, 1)
                    steps_done[0] += 1

                dve.memset(tab[:], 0.0).then_inc(out_done, 1)
                prompt = affT[:, S:T]
                for r in range(CAPP // 8):
                    rank_round(r, prompt, prompt, topp, atp, PR)
                dve.wait_ge(at_done, CAPP // 8)
                dve.tensor_scalar(atpf[:], atp[:], 1.0, float(S), ALU.mult, ALU.add).then_inc(atp_done, 1)
                dve.wait_ge(ld, 16 * LOADS)
                dve.tensor_copy(cand[:], bits[:, 0:1]).then_inc(cand_done, 1)
                dve.memset(low[:].bitcast(F32), 0.0).then_inc(low_done, 1)
                for r in range(ROUNDS):
                    if r < BITS:
                        dve.wait_ge(cand_done, r + 1)
                        wait(dve, total_done, r)
                        dve.tensor_scalar(over[:], aff[:], cand[:].bitcast(F32), None, ALU.is_ge, ALU.add, accum_out=count[:]
                                          ).then_inc(count_done, 1)
                    rank_round(r, aff[:] if r == 0 else left[:], left[:], val, at, CAP)
                    if r < BITS:
                        dve.wait_ge(total_done, r + 1)
                        wait(dve, low_done, r + 1)
                        dve.tensor_scalar(kept[:], total[:, 0:1], float(CAP), float(2 ** (BITS - 1 - r)), ALU.is_ge, ALU.mult
                                          ).then_inc(kept_done, 1)
                        dve.wait_ge(kept_done, r + 1)
                        dve.tensor_tensor(low[:], low[:], kept[:], ALU.bitwise_or).then_inc(low_done, 1)
                        dve.wait_ge(low_done, r + 2)
                        if r + 1 < BITS:
                            dve.tensor_tensor(cand[:], low[:], bits[:, r + 1:r + 2], ALU.bitwise_or).then_inc(cand_done, 1)
                dve.wait_ge(cut_done, done[0])
                dve.tensor_scalar(pair[:, :, 0].bitcast(U32), at[:], group0[:], None, ALU.add).then_inc(pair_done, 1)
                dve.wait_ge(count_done, BITS)
                tail_step(over[:], aff[:], low[:].bitcast(F32), None, ALU.is_gt, ALU.add, accum_out=n_gt[:], op=dve.tensor_scalar)
                tail_step(over[:], aff[:], low[:].bitcast(F32), None, ALU.is_ge, ALU.add, accum_out=n_ge[:], op=dve.tensor_scalar)
                tail_step(n_eq[:], n_ge[:], n_gt[:], ALU.subtract, op=dve.tensor_tensor)
                dve.wait_ge(sums_done, 1)
                tail_step(room[:], total[:, 1:2], -1.0, float(CAP), ALU.mult, ALU.add, op=dve.tensor_scalar)
                tail_step(take[:], room[:], total[:, 2:3], 0.0, ALU.subtract, ALU.max, op=dve.tensor_scalar)
                tail_step(take[:], take[:], n_eq[:], n_gt[:], ALU.min, ALU.add, op=dve.tensor_scalar)
                dve.wait_ge(sums_done, 2)
                tail_step(off[:], total[:, 3:4], op=dve.tensor_copy)
                tail_step(diag[:], ident[:], off[:], None, ALU.mult, op=dve.tensor_scalar)
                dve.wait_ge(sums_done, 3)
                by_group = offs[:].rearrange("p (g e) -> p e g", e=E)
                for i in range(2):
                    tail_step(start[:, i], by_group, 1.0, None, ALU.mult, op=dve.tensor_scalar)
                for i in range(2):
                    tail_step(reached[:, i], start[:, i], slot[:, i:i + 1], None, ALU.is_le, op=dve.tensor_scalar)
                    tail_step(start[:, i], start[:, i], reached[:, i], ALU.mult, op=dve.tensor_tensor)
                tail_step(groups[:], reached[:], AX.X, ALU.add, op=dve.tensor_reduce)
                tail_step(begun[:], start[:], AX.X, ALU.max, op=dve.tensor_reduce)
                tail_step(out=groups[:], in0=groups[:], scalar=float(E * CAP), in1=base[:], op0=ALU.mult, op1=ALU.add,
                          op=dve.scalar_tensor_tensor)
                tail_step(pos[:], groups[:], begun[:], ALU.subtract, op=dve.tensor_tensor)
                dve.wait_ge(tp_done, 1)
                dve.wait_ge(out_done, 1)
                dve.tensor_copy(tab[0:CAPP, :, 2, 0].bitcast(U32), tp[:, 0]).then_inc(out_done, 1)
                dve.tensor_copy(tab[0:CAPP, :, 2, 1], tp[:, 1]).then_inc(out_done, 1)

            @block.scalar
            def _(act):
                act.wait_ge(max_done, CAPP // 8 + ROUNDS)
                act.activation(pair[:, :, 1], val[:], ACT.Copy).then_inc(pair_done, 1)

            @block.tensor
            def _(pe):
                pe.wait_ge(atp_done, 1)
                pe.wait_ge(max_done, CAPP // 8)
                pe.transpose(tp[:, 0], atpf[:], ident[0:E, 0:E])
                pe.transpose(tp[:, 1], topp[:], ident[0:E, 0:E]).then_inc(tp_done, 1)
                pe.wait_ge(ld, 16 * LOADS)
                for r in range(BITS):
                    pe.wait_ge(count_done, r + 1)
                    wait(pe, kept_done, r)
                    pe.matmul(total[:, 0:1], same[:], count[:], start=True, stop=True).then_inc(total_done, 1)
                pe.wait_ge(kept_done, BITS)
                pe.wait_ge(tail, 3)
                pe.matmul(total[:, 1:2], same[:], n_gt[:], start=True, stop=True)
                pe.matmul(total[:, 2:3], before[:], n_eq[:], start=True, stop=True).then_inc(sums_done, 1)
                pe.wait_ge(tail, 6)
                pe.matmul(total[:, 3:4], before[:], take[:], start=True, stop=True).then_inc(sums_done, 1)
                pe.wait_ge(tail, 8)
                pe.matmul(offs[:], ones[:], diag[:], start=True, stop=True).then_inc(sums_done, 1)


def moe_phase(nc, t, tab, pos, ident):
    TOK = CAP + CAPP
    TOKP = 3 * P
    M = FF // P
    SL = ((0, P), (P, P), (CAP, CAPP))
    with ExitStack() as ctx:
        p = Scope(nc, ctx, "moe")
        raw_gu, raw_d = p.sb("raw_gu", [P, 2, 2, KD, P]), p.sb("raw_d", [P, 2, D])
        gu_hi, gu_lo = p.sb("gu_hi", [P, 2, 2, KD, P], F32R), p.sb("gu_lo", [P, 2, 2, KD, P], F32R)
        d_hi, d_lo = p.sb("d_hi", [P, 2, D], F32R), p.sb("d_lo", [P, 2, D], F32R)
        xg = p.sb("xg", [P, 3, D])
        x_hi, x_lo = p.sb("x_hi", [P, 2, KD, TOK], F32R), p.sb("x_lo", [P, 2, KD, TOK], F32R)
        act_g, hid = p.sb("act_g", [P, TOK]), p.sb("hid", [P, TOK])
        h_hi, h_lo = p.sb("h_hi", [P, 2, TOKP], F32R), p.sb("h_lo", [P, 2, TOKP], F32R)
        yo = p.sb("yo", [P, 3, D])
        gate = p.sb("gate", [P, 2, D])
        idx_g, idx_s = p.sb("idx_g", [P, 2, 3], U32), p.sb("idx_s", [P, 2, 3], U32)
        val_s = p.sb("val_s", [P, 2, 3])
        bank = [p.ps("g", [P, BLK]), p.ps("u", [P, BLK])]
        py = p.ps("py", [P, 3, D])
        gate_ld = p.sem("gate_ld")
        gu_ld, d_ld = p.sems("gu_ld", 2), p.sems("d_ld", 2)
        ghi_done, glo_done, dhi_done, dlo_done = (p.sem(n) for n in ("ghi_done", "glo_done", "dhi_done", "dlo_done"))
        pick_done, pick_s_done, xg_ld, y_st = p.sem("pick_done"), p.sem("pick_s_done"), p.sems("xg_ld", 3), p.sems("y_st", 3)
        tp_done, xhi_done, xlo_done = p.sem("tp_done"), p.sem("xhi_done"), p.sem("xlo_done")
        g_mm, u_mm, d_mm = p.sem("g_mm"), p.sem("u_mm"), p.sem("d_mm")
        silu_done, hid_done, hhi_done, hlo_done, y_done = (
            p.sem(n) for n in ("silu_done", "hid_done", "hhi_done", "hlo_done", "y_done"))
        zero_done, may_issue = p.sem("zero_done"), p.sem("may_issue")

        tab_ld = p.sems("tab_ld", 5)

        def wait_tab(eng, e):
            if isinstance(e, int) and e < 4:
                eng.wait_ge(tab_ld[e], 32)
            else:
                eng.wait_ge(tab_ld[2], 32)
                eng.wait_ge(tab_ld[3], 32)
                eng.wait_ge(tab_ld[4], 32 * (E - 4))

        def pairs(eng, body):
            for u in range(2):
                body(u, u, u == 0, False)
            with eng.Fori(1, E // 2 - 1) as i:
                for u in range(2):
                    body(2 * i + u, u, False, False)
            for u in range(2):
                body(E - 2 + u, u, False, u == 1)

        with nc.Block() as block:
            @block.sync
            def _(sp):
                for s in range(2):
                    sp.dma_start(gate[:, s], t["mod"][s, 5 * D:6 * D].partition_broadcast(P)).then_inc(gate_ld, 16)

                def load(e, u, first, last):
                    for m in range(M):
                        q = M * e + m
                        if not (first and m < 2):
                            sp.wait_ge(glo_done, q - 1)
                        sp.dma_start(raw_gu[:, m % 2], t["w_gate_up"][bass.ds(q, 1)].rearrange("o p g k n -> (o p) g k n")
                                     ).then_inc(gu_ld[m % 2], 16)
                        if not (first and m < 2):
                            sp.wait_ge(dlo_done, q - 1)
                        sp.dma_start(raw_d[:, m % 2], t["w_down"][bass.ds(q * P, P), :]).then_inc(d_ld[m % 2], 16)
                pairs(sp, load)

            @block.gpsimd
            def _(pool):
                def gather(e, u):
                    pool.wait_ge(pick_done, e + 1)
                    pool.sem_inc(may_issue, 1)
                    for i, (_, n) in enumerate(SL):
                        pool.indirect_dma_start(xg[0:n, i], None, t["h2"], bass.IndirectOffsetOnAxis(ap=idx_g[0:n, u, i:i + 1], axis=0)
                                                ).then_inc(xg_ld[i], 16)

                def scatter(e, u):
                    pool.wait_ge(y_done, 3 * e + 3)
                    for i in range(3):
                        wait(pool, y_st[i], 16 * e)
                    pool.sem_inc(may_issue, 1)
                    for i, (_, n) in enumerate(SL):
                        pool.indirect_dma_start(t["x2"], bass.IndirectOffsetOnAxis(ap=idx_s[0:n, u, i:i + 1], axis=0),
                                                yo[0:n, i], None, compute_op=ALU.add).then_inc(y_st[i], 16)

                def split_gu(q, slot):
                    pool.wait_ge(ghi_done, q + 1)
                    pool.tensor_tensor(gu_lo[:, slot], raw_gu[:, slot], gu_hi[:, slot].bitcast(F32), ALU.subtract
                                       ).then_inc(glo_done, 1)

                def look_up(e):
                    for i in range(2):
                        pool.indirect_dma_start(tab[:, e, i], None, t["ranked"],
                                                bass.IndirectOffsetOnAxis(ap=pos[:, i, e:e + 1], axis=0)
                                                ).then_inc(tab_ld[min(e, 4)], 16)

                for e in range(4):
                    look_up(e)
                gather(0, 0)
                for b in (h_hi, h_lo):
                    pool.memset(b[:, :, TOK:].bitcast(F32), 0.0).then_inc(zero_done, 1)
                split_gu(0, 0)

                def expert(e, u, first, last):
                    for m in range(M):
                        if m == 0 and not last:
                            pool.wait_ge(tp_done, 6 * e + 6)
                            gather(e + 1, 1 - u)
                        if not (last and m == M - 1):
                            split_gu(M * e + m + 1, (m + 1) % 2)
                        if m == 1 and not first:
                            scatter(e - 1, 1 - u)
                        if isinstance(e, int) and M * e + m < 6:
                            for ahead in range(2):
                                look_up(4 + 2 * (M * e + m) + ahead)
                pairs(pool, expert)
                scatter(E - 1, 1)
                for i in range(3):
                    pool.wait_ge(y_st[i], 16 * E)

            @block.scalar
            def _(act):
                def split_gu(q, slot, half):
                    act.wait_ge(gu_ld[slot], 16 * half + 16)
                    wait(act, u_mm, q - 1)
                    act.activation(gu_hi[:, slot], raw_gu[:, slot], ACT.Copy).then_inc(ghi_done, 1)

                def x_hi_part(e, i, half, u):
                    n = SL[i][1]
                    act.wait_ge(tp_done, 6 * e + 2 * i + half + 1)
                    act.activation(x_hi[:, u, 4 * half:4 * half + 4, SL[i][0]:SL[i][0] + n],
                                   bank[half][:, 0:4 * n].rearrange("p (k n) -> p k n", k=4), ACT.Copy).then_inc(xhi_done, 1)

                for i in range(3):
                    for half in range(2):
                        x_hi_part(0, i, half, 0)
                split_gu(0, 0, 0)

                def expert(e, u, first, last):
                    for m in range(M):
                        q, slot = M * e + m, m % 2
                        if not (last and m == M - 1):
                            split_gu(q + 1, (m + 1) % 2, 2 * e + (m + 1) // 2)
                        act.wait_ge(d_ld[slot], 16 * (2 * e + m // 2) + 16)
                        if not (first and m < 2):
                            act.wait_ge(d_mm, q - 1)
                        act.activation(d_hi[:, slot], raw_d[:, slot], ACT.Copy).then_inc(dhi_done, 1)
                        act.wait_ge(g_mm, q + 1)
                        wait(act, hid_done, q)
                        act.activation(act_g[:], bank[0][:, 0:TOK], ACT.Silu).then_inc(silu_done, 1)
                        act.wait_ge(hid_done, q + 1)
                        act.activation(h_hi[:, slot, 0:TOK], hid[:], ACT.Copy).then_inc(hhi_done, 1)
                        if m > 0 and not last:
                            x_hi_part(e + 1, m - 1, 0, 1 - u)
                            x_hi_part(e + 1, m - 1, 1, 1 - u)
                pairs(act, expert)

            @block.vector
            def _(dve):
                def pick(e, u):
                    wait_tab(dve, e)
                    for i in range(3):
                        wait(dve, xg_ld[i], 16 * (e - 1))
                    dve.tensor_copy(idx_g[:, u], tab[:, bass.ds(e, 1), :, 0].bitcast(U32).rearrange("p o i -> p (o i)")
                                    ).then_inc(pick_done, 1)

                def pick_s(e, u):
                    dve.wait_ge(gate_ld, 32)
                    for i in range(3):
                        wait(dve, y_st[i], 16 * (e - 1))
                    for dst, c, dt in ((idx_s, 0, U32), (val_s, 1, F32)):
                        dve.tensor_copy(dst[:, u], tab[:, bass.ds(e, 1), :, c].bitcast(dt).rearrange("p o i -> p (o i)")
                                        ).then_inc(pick_s_done, 1)

                def x_lo_part(e, i, half, u):
                    at0, n = SL[i]
                    dve.wait_ge(xhi_done, 6 * e + 2 * i + half + 1)
                    part = (slice(None), u, slice(4 * half, 4 * half + 4), slice(at0, at0 + n))
                    dve.tensor_tensor(x_lo[part], bank[half][:, 0:4 * n].rearrange("p (k n) -> p k n", k=4),
                                      x_hi[part].bitcast(F32), ALU.subtract).then_inc(xlo_done, 1)

                def scale_y(e, u):
                    dve.wait_ge(d_mm, M * e + M)
                    dve.wait_ge(pick_s_done, 2 * e + 2)
                    for i, (_, n) in enumerate(SL):
                        wait(dve, y_st[i], 16 * e)
                        dve.scalar_tensor_tensor(out=yo[0:n, i], in0=py[0:n, i], scalar=val_s[0:n, u, i:i + 1],
                                                 in1=gate[0:n, i // 2], op0=ALU.mult, op1=ALU.mult).then_inc(y_done, 1)

                pick(0, 0)
                for i in range(3):
                    for half in range(2):
                        x_lo_part(0, i, half, 0)
                dve.wait_ge(gate_ld, 32)

                def expert(e, u, first, last):
                    for m in range(M):
                        q, slot = M * e + m, m % 2
                        if m == 0 and not last:
                            pick(e + 1, 1 - u)
                        if m == 1:
                            pick_s(e, u)
                        dve.wait_ge(dhi_done, q + 1)
                        dve.tensor_tensor(d_lo[:, slot], raw_d[:, slot], d_hi[:, slot].bitcast(F32), ALU.subtract
                                          ).then_inc(dlo_done, 1)
                        dve.wait_ge(silu_done, q + 1)
                        dve.wait_ge(u_mm, q + 1)
                        wait(dve, hhi_done, q)
                        wait(dve, hlo_done, q)
                        dve.tensor_tensor(hid[:], bank[1][:, 0:TOK], act_g[:], ALU.mult).then_inc(hid_done, 1)
                        dve.wait_ge(hhi_done, q + 1)
                        dve.tensor_tensor(h_lo[:, slot, 0:TOK], hid[:], h_hi[:, slot, 0:TOK].bitcast(F32), ALU.subtract
                                          ).then_inc(hlo_done, 1)
                        if m == 0 and not first:
                            scale_y(e - 1, 1 - u)
                        if m > 0 and not last:
                            x_lo_part(e + 1, m - 1, 0, 1 - u)
                            x_lo_part(e + 1, m - 1, 1, 1 - u)
                pairs(dve, expert)
                scale_y(E - 1, 1)

            @block.tensor
            def _(pe):
                def turn(e, i, half, u):
                    n = SL[i][1]
                    for k in range(4):
                        at0 = (4 * half + k) * P
                        mm = pe.transpose(bank[half][:, k * n:(k + 1) * n], xg[0:n, i, at0:at0 + P], ident[0:n, 0:n])
                    mm.then_inc(tp_done, 1)

                def down(q, slot, first_piece, last_piece, part):
                    for i in part:
                        for h, w in ((h_hi, d_hi), (h_hi, d_lo), (h_lo, d_hi)):
                            for n in range(2):
                                mm = pe.matmul(py[:, i, n * BLK:(n + 1) * BLK], h[:, slot, i * P:(i + 1) * P],
                                               w[:, slot, n * BLK:(n + 1) * BLK],
                                               start=(first_piece and h is h_hi and w is d_hi),
                                               stop=(last_piece and h is h_lo))
                    if part[-1] == 2:
                        mm.then_inc(d_mm, 1)

                pe.wait_ge(zero_done, 2)
                for i in range(3):
                    pe.wait_ge(xg_ld[i], 16)
                    for half in range(2):
                        wait(pe, xlo_done, 2 * i + half - 1)
                        turn(0, i, half, 0)

                def expert(e, u, first, last):
                    for m in range(M):
                        q, slot = M * e + m, m % 2
                        pe.wait_ge(glo_done, q + 1)
                        for g in range(2):
                            if m == 0:
                                pe.wait_ge(xlo_done, 6 * e + 6)
                            elif m > 1 and not last:
                                pe.wait_ge(xlo_done, 6 * e + 6 + 2 * (m - 1) - 1 + g)
                            wait(pe, (silu_done, hid_done)[g], q)
                            for k in range(KD):
                                for w, x in ((gu_hi, x_hi), (gu_lo, x_hi), (gu_hi, x_lo)):
                                    mm = pe.matmul(bank[g][:, 0:TOK], w[:, slot, g, k], x[:, u, k],
                                                   start=(k == 0 and w is gu_hi and x is x_hi),
                                                   stop=(k == KD - 1 and x is x_lo))
                            mm.then_inc((g_mm, u_mm)[g], 1)
                        if m > 0 and not last:
                            pe.wait_ge(zero_done, 2)
                            pe.wait_ge(silu_done, q + 1)
                            pe.wait_ge(xg_ld[m - 1], 16 * e + 32)
                            turn(e + 1, m - 1, 0, 1 - u)
                        if not (first and m == 0):
                            pe.wait_ge(hlo_done, q)
                            pe.wait_ge(dlo_done, q)
                            if m == 1 and not first:
                                pe.wait_ge(y_done, 3 * e)
                            down(q - 1, 1 - slot, m == 1, m == 0, (0, 1))
                        if m > 0 and not last:
                            pe.wait_ge(zero_done, 2)
                            pe.wait_ge(hid_done, q + 1)
                            turn(e + 1, m - 1, 1, 1 - u)
                        if not (first and m == 0):
                            down(q - 1, 1 - slot, m == 1, m == 0, (2,))
                pairs(pe, expert)
                pe.wait_ge(hlo_done, M * E)
                pe.wait_ge(dlo_done, M * E)
                down(M * E - 1, 1, False, True, (0, 1, 2))


def final_phase(nc, t):
    U = 6
    with ExitStack() as ctx:
        p = Scope(nc, ctx, "fin")
        x, sq, y = p.sb("x", [P, U, D]), p.sb("sq", [P, 2, D]), p.sb("y", [P, U, D])
        norm = p.sb("norm", [P, D])
        sumsq, meansq, root, rstd = (p.sb(n, [P, U]) for n in ("sumsq", "meansq", "root", "rstd"))
        x_ld, y_st, norm_ld = p.sems("x_ld", U), p.sems("y_st", U), p.sem("norm_ld")
        sq_done, ms_done, root_done, rstd_done, y_done = (
            p.sem(n) for n in ("sq_done", "ms_done", "root_done", "rstd_done", "y_done"))
        N = T // P // U
        with nc.Block() as block:
            @block.sync
            def _(sp):
                sp.dma_start(norm[:], t["final_norm"].partition_broadcast(P)).then_inc(norm_ld, 16)

                def load(i):
                    for u in range(U):
                        wait(sp, y_done, U * i + u - U + 1)
                        sp.dma_start(x[:, u], t["x2"][bass.ds((U * i + u) * P, P), :]).then_inc(x_ld[u], 16)
                steps(sp, N, load)

            @block.scalar
            def _(act):
                def body(i):
                    for u in range(U):
                        j = U * i + u
                        act.wait_ge(x_ld[u], 16 * i + 16)
                        wait(act, sq_done, j - 1)
                        act.activation(sq[:, u % 2], x[:, u], ACT.Square, accum_out=sumsq[:, u:u + 1]).then_inc(sq_done, 1)
                        act.wait_ge(ms_done, j + 1)
                        act.activation(root[:, u:u + 1], meansq[:, u:u + 1], ACT.Sqrt).then_inc(root_done, 1)
                steps(act, N, body)

            @block.vector
            def _(dve):
                dve.wait_ge(norm_ld, 16)

                def body(i):
                    for u in range(U):
                        j = U * i + u
                        dve.wait_ge(sq_done, j + 1)
                        dve.tensor_scalar(meansq[:, u:u + 1], sumsq[:, u:u + 1], 1.0 / D, EPS, ALU.mult, ALU.add
                                          ).then_inc(ms_done, 1)
                        dve.wait_ge(root_done, j + 1)
                        dve.reciprocal(rstd[:, u:u + 1], root[:, u:u + 1]).then_inc(rstd_done, 1)
                        dve.wait_ge(rstd_done, j + 1)
                        wait(dve, y_st[u], 16 * i)
                        dve.scalar_tensor_tensor(out=y[:, u], in0=x[:, u], scalar=rstd[:, u:u + 1], in1=norm[:],
                                                 op0=ALU.mult, op1=ALU.mult).then_inc(y_done, 1)
                steps(dve, N, body)

            @block.gpsimd
            def _(pool):
                def store(i):
                    for u in range(U):
                        pool.wait_ge(y_done, U * i + u + 1)
                        pool.dma_start(t["y"][bass.ds((U * i + u) * P, P), :], y[:, u]).then_inc(y_st[u], 16)
                steps(pool, N, store)
                for u in range(U):
                    pool.wait_ge(y_st[u], 16 * N)


def program(nc, t, upto=99):
    with ExitStack() as ctx:
        ident = ctx.enter_context(nc.sbuf_tensor("identity", [P, P], F32))
        silu = ctx.enter_context(nc.sbuf_tensor("silu", [P, KD, 2], F32))
        ada_phase(nc, t, silu)
        with ExitStack() as hold:
            hT_hi = hold.enter_context(nc.sbuf_tensor("hT_hi", [P, KD, T], F32R))
            hT_lo = hold.enter_context(nc.sbuf_tensor("hT_lo", [P, KD, T], F32R))
            norm1_phase(nc, t, hT_hi, hT_lo, ident, silu, ctx)
            if upto <= 1: return
            in_proj_phase(nc, t, hT_hi, hT_lo)
        if upto <= 2: return
        with ExitStack() as hold:
            V = hold.enter_context(nc.sbuf_tensor("V", [P, H, KEYS // P, DV], F32))
            latents_phase(nc, t, V)
            if upto <= 3: return
            attention_phase(nc, t, V, ident)
        if upto <= 4: return
        mix_phase(nc, t)
        affT = ctx.enter_context(nc.sbuf_tensor("affT", [E, T], F32))
        out_phase(nc, t, affT, ident)
        if upto <= 5: return
        tab = ctx.enter_context(nc.sbuf_tensor("tab", [P, E, 3, 2], F32))
        pos = ctx.enter_context(nc.sbuf_tensor("pos", [P, 2, E], U32))
        topk_phase(nc, t, affT, tab, pos, ident)
        if upto <= 6: return
        moe_phase(nc, t, tab, pos, ident)
        if upto <= 7: return
        final_phase(nc, t)


SCRATCH = {
    "mod": [2, ADA], "gates": [2 * D, T], "misc": [4 * P, T], "conv": [CONV, T],
    "q": [H, HQ, T], "k": [H, NOPE, KEYS], "kpe": [ROPE, KEYS], "o": [H * DV, T],
    "sums": [H, T], "inverse": [H, T], "ranked": [S * E, 2], "mixed": [D, T], "x2": [T, D], "h2": [T, D],
}


def rotary_constants():
    half = ROPE // 2
    freq = np.float32(10000.0) ** (-np.arange(0, half, 2, dtype=np.float32) / np.float32(half))
    n = np.arange(S)
    at = np.stack([n // 64, n % 64]).astype(np.float32)
    d = np.arange(ROPE)
    angle = at[d // half] * freq[d % (half // 2)][:, None]
    perm = np.zeros((ROPE, ROPE), np.float32)
    first = d % half < half // 2
    perm[d[first] + half // 2, d[first]] = -1.0
    perm[d[~first] - half // 2, d[~first]] = 1.0
    perm = np.concatenate([np.zeros((ROPE, NOPE), np.float32), perm], 1)
    return np.cos(angle), np.sin(angle), perm


def ranking_constants():
    group, expert = np.divmod(np.arange(P), E)
    same = expert[:, None] == expert[None, :]
    slot = np.arange(P)[:, None] + np.array([0, P])[None, :]
    base = slot[:, :, None] + CAP * np.arange(E)[None, None, :] - E * CAP
    f = np.float32
    return {"rank_bits": np.tile((1 << np.arange(29, -1, -1)).astype(np.uint32), (P, 1)),
            "rank_same": same.astype(f), "rank_before": (same & (group[:, None] < group[None, :])).astype(f),
            "rank_group0": (group * CAP).astype(f)[:, None], "rank_slot": slot.astype(f),
            "rank_base": base.astype(f), "rank_ones": np.ones((P, P), f)}


def laid_out(i):
    w_in = i["w_in"][0].reshape(KD, P, -1)

    def cols(at):
        return w_in[:, :, at:at + P].transpose(1, 0, 2)
    QA = 2 * CONV
    GATE = QA + QL + KVL + ROPE
    tiles = []
    for c in range(CT):
        tiles += [cols(c * P), cols(CONV + c * P)]
        tiles += [cols(GATE + (4 * c + g) * P) for g in range(4)]
        tiles += [cols(QA + c * P)]
    w_qb = i["w_qb"][0].reshape(2, P, H, HQ).transpose(1, 2, 0, 3).reshape(P, H, 2 * HQ)
    w_kvb = i["w_kvb"][0].reshape(P, H, NOPE + DV)
    cos, sin, perm = rotary_constants()
    w_gate_up = np.stack([i["w_e_gate"][0], i["w_e_up"][0]]).reshape(2, E, KD, P, FF // P, P)
    w_gate_up = w_gate_up.transpose(1, 4, 3, 0, 2, 5).reshape(E * FF // P, P, 2, KD, P)
    a = {
        "cache_ckv": i["cache_ckv"][0, 0].T, "cache_kpe": i["cache_kpe"][0, 0].T,
        "latent_norms": np.concatenate([i["q_norm"][0], i["kv_norm"][0]]).reshape(3, P).T,
        "cos": cos, "sin": sin, "perm": perm,
        "w_head": np.concatenate([w_qb, w_kvb], -1),
        "conv_norm": np.stack([i["conv_ln_g"][0], i["conv_ln_b"][0]]).reshape(2, CT, P).transpose(2, 0, 1),
        "w_conv_out": i["w_conv_out"][0].reshape(CT, P, D).transpose(1, 0, 2),
        "w_o": i["w_o_mla"][0].reshape(CT, P, D).transpose(1, 0, 2),
        "w_out": i["w_out"][0], "norm2": i["norm2"][0],
        "w_router": i["w_router"][0].reshape(KD, P, E).transpose(1, 0, 2),
        "w_v": w_kvb[:, :, NOPE:].reshape(P, H * DV),
        "x": np.concatenate([i["x_sample"][0], i["x_prompt"][0]]),
        "cond": np.stack([i["c"][0], i["c_ctx"]], -1).reshape(KD, P, 2).transpose(1, 0, 2),
        "w_ada": i["w_ada"][0].reshape(KD, P, ADA // 512, 512).transpose(2, 1, 0, 3),
        "b_ada": i["b_ada"][0],
        "norm1": i["norm1"][0],
        "w_in": np.stack(tiles),
        "conv_dw": np.concatenate([i["conv_dw"][0], i["conv_dw_b"]]).reshape(TAPS + 1, CT, P).transpose(2, 1, 0),
        "w_gate_up": w_gate_up, "w_down": i["w_e_down"][0].reshape(E * FF, D), "final_norm": i["final_norm"],
        "ident": np.eye(P, dtype=np.float32),
    }
    a.update(ranking_constants())
    return {k: np.ascontiguousarray(v) for k, v in a.items()}


OUTS = {"y": [T, D], "new_ckv": [KVL, PR], "new_kpe": [ROPE, PR]}


def declare(nc, arrays):
    t = {}
    for k, a in arrays.items():
        t[k] = nc.dram_tensor(k, list(a.shape), mybir.dt.from_np(a.dtype), kind="ExternalInput").ap()
    for k, shape in SCRATCH.items():
        t[k] = nc.dram_tensor(f"{k}_scratch", shape, F32, kind="Internal").ap()
    for k, shape in OUTS.items():
        t[k] = nc.dram_tensor(k, shape, F32, kind="ExternalOutput").ap()
    return t


def kernel(**inputs):
    from concourse import bacc
    from concourse.bass_utils import run_bass_kernel_spmd

    arrays = laid_out({k: np.asarray(v) for k, v in inputs.items()})
    nc = bacc.Bacc("TRN2", target_bir_lowering=False, num_devices=1)
    program(nc, declare(nc, arrays))
    got = run_bass_kernel_spmd(nc, [arrays], core_ids=[0]).results[0]
    y = np.asarray(got["y"])
    return (y[S:].reshape(1, PR, D), y[:S].reshape(1, S, D),
            np.ascontiguousarray(np.asarray(got["new_ckv"]).T).reshape(1, 1, PR, KVL),
            np.ascontiguousarray(np.asarray(got["new_kpe"]).T).reshape(1, 1, PR, ROPE))
```
